# Optimizing a Trainium2 kernel written in Bass

```python
import jax
import jax.numpy as jnp
from jax import lax
import numpy as np

D_MODEL = 1024
BATCH = 1
SEQ = 256
DEPTH = 1
DEC_BATCH = 8
DEC_SEQ = 4
PAST_LEN = 256
PAGE_SIZE = 128

HEAD_DIM = 64
N_MIXERS = 4
MIX_W = D_MODEL
GROUP_W = MIX_W // N_MIXERS
H_A = GROUP_W // HEAD_DIM
H_B = GROUP_W // HEAD_DIM
H_C = GROUP_W // HEAD_DIM
H_D = GROUP_W // HEAD_DIM
LORA_W = 64
LORA_A = 64
LORA_G = 128
A_PROJ = 3 * GROUP_W + LORA_W + LORA_A + LORA_G
B_PROJ = 3 * GROUP_W + H_B
C_PROJ = 2 * GROUP_W
D_PROJ = 3 * GROUP_W
IN_W = A_PROJ + B_PROJ + C_PROJ + D_PROJ
IN_SPLITS = (A_PROJ, A_PROJ + B_PROJ, A_PROJ + B_PROJ + C_PROJ)
CHUNK = 128
Q_BLOCK = 128
DIL_PATTERNS = ((128, 1), (512, 4), (2048, 16))
DIL_MAX_WINDOW = 2048
N_MEM = 256
CA_HEADS = 4
CA_HEAD_DIM = D_MODEL // CA_HEADS
CA_W = CA_HEADS * CA_HEAD_DIM
PEER_HEADS = 8
PEER_DK = 256
N_KEYS = 128
N_EXPERTS = N_KEYS * N_KEYS
PEER_TOPK = 16
PEER_BLOCK = 128
FORGET_BIAS = 3.0
NORM_EPS = 1e-6
GN_EPS = 64e-5
NEG_INF = -1e30

kernel_name = "hybrid_rwkv7_fox_sgu_dilated_peer_step"

def rmsnorm(x, g):
    xf = x.astype(jnp.float32)
    return xf * lax.rsqrt(jnp.mean(xf * xf, axis=-1, keepdims=True) + NORM_EPS) * g.astype(jnp.float32)

def layernorm(x, g, b, eps):
    xf = x.astype(jnp.float32)
    mu = jnp.mean(xf, axis=-1, keepdims=True)
    var = jnp.mean(jnp.square(xf - mu), axis=-1, keepdims=True)
    return (xf - mu) * lax.rsqrt(var + eps) * g + b

def heads(t, h):
    return t.reshape(t.shape[:-1] + (h, HEAD_DIM))

def alibi_slopes(n):
    return 2.0 ** (-8.0 * jnp.arange(1, n + 1, dtype=jnp.float32) / n)

def wkv7_scan(s0, r, w, k, v, kk, a):
    def step(s, inp):
        r_t, w_t, k_t, v_t, kk_t, a_t = inp
        s_kk = jnp.einsum('bhij,bhj->bhi', s, kk_t)
        s = (s * w_t[:, :, None, :] - s_kk[..., None] * (kk_t * a_t)[:, :, None, :]
             + v_t[..., None] * k_t[:, :, None, :])
        return s, jnp.einsum('bhij,bhj->bhi', s, r_t)
    xs = tuple(jnp.moveaxis(t.astype(jnp.float32), 1, 0) for t in (r, w, k, v, kk, a))
    s_last, ys = lax.scan(step, s0.astype(jnp.float32), xs)
    return s_last, jnp.moveaxis(ys, 0, 1)

def rwkv7_mixer(pa, shift_prev, s0, mu, w0, w2, a0, a2, g2, kk_scale, ka, rk, lnw, lnb):
    pa = pa.astype(jnp.float32)
    prev = jnp.concatenate([shift_prev[:, None, :].astype(jnp.float32), pa[:, :-1]], axis=1)
    xs = pa + mu * (prev - pa)
    r, k, v, xw, xa, xg = jnp.split(
        xs, [GROUP_W, 2 * GROUP_W, 3 * GROUP_W, 3 * GROUP_W + LORA_W,
             3 * GROUP_W + LORA_W + LORA_A], axis=-1)
    w_log = -jax.nn.softplus(-(w0 + jnp.tanh(xw) @ w2)) - 0.5
    decay = jnp.exp(-jnp.exp(w_log))
    a = jax.nn.sigmoid(a0 + xa @ a2)
    g = jax.nn.sigmoid(xg) @ g2
    kk = heads(k * kk_scale, H_A)
    kk = kk / jnp.maximum(jnp.sqrt(jnp.sum(kk * kk, axis=-1, keepdims=True)), 1e-12)
    k = k * (1.0 + (a - 1.0) * ka)
    rh, kh, vh, wh, ah = (heads(t, H_A) for t in (r, k, v, decay, a))
    s_last, y = wkv7_scan(s0, rh, wh, kh, vh, kk, ah)
    yn = layernorm(y, heads(lnw, H_A), heads(lnb, H_A), GN_EPS)
    bonus = jnp.sum(rh * kh * rk, axis=-1, keepdims=True) * vh
    out = (yn + bonus).reshape(y.shape[:2] + (GROUP_W,)) * g
    return out, s_last, pa[:, -1]

def fox_split(pb, b_f):
    q, k, v, fl = jnp.split(pb, [GROUP_W, 2 * GROUP_W, 3 * GROUP_W], axis=-1)
    logf = jax.nn.log_sigmoid((fl + b_f).astype(jnp.float32))
    return heads(q, H_B), heads(k, H_B), heads(v, H_B), logf

def fox_attend(q, cq, qpos, k, v, ck, kpos):
    s = jnp.einsum('bqhd,bkhd->bhqk', q, k).astype(jnp.float32) * (HEAD_DIM ** -0.5)
    s = s + jnp.swapaxes(cq, 1, 2)[..., :, None] - jnp.swapaxes(ck, 1, 2)[..., None, :]
    s = jnp.where(kpos[None, :] <= qpos[:, None], s, NEG_INF)
    p = jax.nn.softmax(s, axis=-1)
    return jnp.einsum('bhqk,bkhd->bqhd', p, v.astype(jnp.float32))

def fox_prompt(pb, b_f):
    q, k, v, logf = fox_split(pb, b_f)
    B, T = q.shape[:2]
    c = jnp.cumsum(logf, axis=1)
    kpos = jnp.arange(T)

    def block(i):
        q0 = i * Q_BLOCK
        qb = lax.dynamic_slice_in_dim(q, q0, Q_BLOCK, axis=1)
        cb = lax.dynamic_slice_in_dim(c, q0, Q_BLOCK, axis=1)
        return fox_attend(qb, cb, q0 + jnp.arange(Q_BLOCK), k, v, c, kpos)

    o = lax.map(block, jnp.arange(T // Q_BLOCK))
    o = jnp.moveaxis(o, 0, 1).reshape(B, T, GROUP_W)
    return o, k, v, logf

def fox_sample(pb, b_f, k_pool, v_pool, lf_pool, page_table):
    q, k, v, logf = fox_split(pb, b_f)
    B, T = q.shape[:2]
    n_past = page_table.shape[1] * PAGE_SIZE
    kp = k_pool[page_table].reshape(B, n_past, H_B, HEAD_DIM).astype(k.dtype)
    vp = v_pool[page_table].reshape(B, n_past, H_B, HEAD_DIM).astype(v.dtype)
    lfp = lf_pool[page_table].reshape(B, n_past, H_B).astype(jnp.float32)
    k_all = jnp.concatenate([kp, k], axis=1)
    v_all = jnp.concatenate([vp, v], axis=1)
    c = jnp.cumsum(jnp.concatenate([lfp, logf], axis=1), axis=1)
    o = fox_attend(q, c[:, n_past:], n_past + jnp.arange(T), k_all, v_all, c, jnp.arange(n_past + T))
    return o.reshape(B, T, GROUP_W), k, v, logf

def sgu(pc, lng, lnb, ws, bs):
    B, T, _ = pc.shape
    L = min(T, CHUNK)
    u, v = jnp.split(jax.nn.gelu(pc.astype(jnp.float32), approximate=False), 2, axis=-1)
    v = layernorm(v, lng, lnb, NORM_EPS)
    vh = v.reshape(B, T // L, L, H_C, HEAD_DIM)
    wm = jnp.tril(ws[:, :L, :L])
    mix = jnp.einsum('hij,bnjhc->bnihc', wm, vh) + bs[:, :L].T[None, None, :, :, None]
    return u * mix.reshape(B, T, GROUP_W), v

def dilated_attend(q, k_all, v_all, qpos, base, slopes):
    L = k_all.shape[1]
    qf = q.astype(jnp.float32) * (HEAD_DIM ** -0.5)
    nums, dens, maxs = [], [], []
    for window, dil in DIL_PATTERNS:
        offs = dil * jnp.arange(window // dil + 1)
        kabs = qpos[:, None] - offs[None, :]
        valid = kabs >= 0
        idx = jnp.clip(kabs - base, 0, L - 1)
        kg = k_all[:, idx].astype(jnp.float32)
        vg = v_all[:, idx].astype(jnp.float32)
        s = jnp.einsum('bqhd,bqkhd->bhqk', qf, kg) - slopes[:, None, None] * offs.astype(jnp.float32)
        s = jnp.where(valid, s, NEG_INF)
        m = jnp.max(s, axis=-1)
        p = jnp.exp(s - m[..., None])
        dens.append(jnp.sum(p, axis=-1))
        nums.append(jnp.einsum('bhqk,bqkhd->bhqd', p, vg))
        maxs.append(m)
    m_all = jnp.stack(maxs)
    wts = jnp.exp(m_all - jnp.max(m_all, axis=0))
    num = jnp.sum(wts[..., None] * jnp.stack(nums), axis=0)
    den = jnp.sum(wts * jnp.stack(dens), axis=0)
    return jnp.swapaxes(num / den[..., None], 1, 2)

def dilated_prompt(pd, slopes):
    q, k, v = (heads(t, H_D) for t in jnp.split(pd, 3, axis=-1))
    B, T = q.shape[:2]

    def block(i):
        q0 = i * Q_BLOCK
        qb = lax.dynamic_slice_in_dim(q, q0, Q_BLOCK, axis=1)
        return dilated_attend(qb, k, v, q0 + jnp.arange(Q_BLOCK), 0, slopes)

    o = lax.map(block, jnp.arange(T // Q_BLOCK))
    o = jnp.moveaxis(o, 0, 1).reshape(B, T, GROUP_W)
    keep = min(DIL_MAX_WINDOW, T)
    return o, k[:, T - keep:], v[:, T - keep:]

def dilated_sample(pd, k_buf, v_buf, n_past, slopes):
    q, k, v = (heads(t, H_D) for t in jnp.split(pd, 3, axis=-1))
    B, T = q.shape[:2]
    n_buf = k_buf.shape[1]
    k_all = jnp.concatenate([k_buf.astype(k.dtype), k], axis=1)
    v_all = jnp.concatenate([v_buf.astype(v.dtype), v], axis=1)
    o = dilated_attend(q, k_all, v_all, n_past + jnp.arange(T), n_past - n_buf, slopes)
    return o.reshape(B, T, GROUP_W), k, v

def merge_groups(ya, yb, yc, yd, out_g, w_out):
    y = jnp.stack([ya, yb, yc, yd], axis=-2).astype(jnp.float32)
    y = y * lax.rsqrt(jnp.mean(y * y, axis=-1, keepdims=True) + NORM_EPS)
    return (y.reshape(y.shape[:-2] + (MIX_W,)) * out_g) @ w_out

def memory_kv(mem, g, wk, wv):
    mn = rmsnorm(mem, g)
    shp = mem.shape[:2] + (CA_HEADS, CA_HEAD_DIM)
    return (mn @ wk).reshape(shp), (mn @ wv).reshape(shp)

def cross_attend(xn, wq, wo, mk, mv):
    q = (xn @ wq).reshape(xn.shape[:-1] + (CA_HEADS, CA_HEAD_DIM))
    s = jnp.einsum('bqhd,bkhd->bhqk', q, mk.astype(jnp.float32)).astype(jnp.float32) * (CA_HEAD_DIM ** -0.5)
    p = jax.nn.softmax(s, axis=-1)
    o = jnp.einsum('bhqk,bkhd->bqhd', p, mv.astype(jnp.float32))
    return o.reshape(xn.shape[:-1] + (CA_W,)) @ wo

def peer_ffn(xn, wq, keys, u_tab, v_tab):
    B, T, D = xn.shape
    n = B * T
    xf = jnp.pad(xn.reshape(n, D), ((0, (-n) % PEER_BLOCK), (0, 0)))

    def block(xt):
        q = (xt @ wq).reshape(PEER_BLOCK, PEER_HEADS, 2, PEER_DK // 2)
        s = jnp.einsum('phcd,hcnd->phcn', q, keys).astype(jnp.float32)
        top_s, top_i = lax.top_k(s, PEER_TOPK)
        cand_s = (top_s[:, :, 0, :, None] + top_s[:, :, 1, None, :]).reshape(
            PEER_BLOCK, PEER_HEADS, PEER_TOPK * PEER_TOPK)
        cand_i = (top_i[:, :, 0, :, None] * N_KEYS + top_i[:, :, 1, None, :]).reshape(
            PEER_BLOCK, PEER_HEADS, PEER_TOPK * PEER_TOPK)
        best_s, best_j = lax.top_k(cand_s, PEER_TOPK)
        e_idx = jnp.take_along_axis(cand_i, best_j, axis=-1)
        gate = jax.nn.softmax(best_s, axis=-1)
        act = jax.nn.gelu(jnp.einsum('pd,phkd->phk', xt, u_tab[e_idx]).astype(jnp.float32),
                          approximate=False)
        return jnp.einsum('phk,phkd->pd', gate * act, v_tab[e_idx].astype(jnp.float32))

    out = lax.map(block, xf.reshape(-1, PEER_BLOCK, D))
    return out.reshape(-1, D)[:n].reshape(B, T, D)

def setup_inputs(seed: int = 0) -> dict:
    key = jax.random.key(seed)
    ks = list(jax.random.split(key, 64))

    def nrm(shape, scale=1.0):
        return jax.random.normal(ks.pop(), shape, jnp.float32) * scale

    def gain(shape):
        return 1.0 + nrm(shape, 0.05)

    L = DEPTH
    n_pages = PAST_LEN // PAGE_SIZE
    n_phys = (5 * DEC_BATCH * n_pages + 3) // 4
    d_buf = min(DIL_MAX_WINDOW, PAST_LEN)
    page_table = jax.random.permutation(ks.pop(), n_phys)[:DEC_BATCH * n_pages]
    page_table = page_table.reshape(DEC_BATCH, n_pages).astype(jnp.int32)
    return {
        "x_prompt": nrm((BATCH, SEQ, D_MODEL)),
        "x_sample": nrm((DEC_BATCH, DEC_SEQ, D_MODEL)),
        "mem_prompt": nrm((BATCH, N_MEM, D_MODEL)),
        "state_a_wkv": nrm((L, DEC_BATCH, H_A, HEAD_DIM, HEAD_DIM), 0.5),
        "state_a_shift": nrm((L, DEC_BATCH, A_PROJ)),
        "cache_b_k": nrm((L, n_phys, PAGE_SIZE, H_B, HEAD_DIM)),
        "cache_b_v": nrm((L, n_phys, PAGE_SIZE, H_B, HEAD_DIM)),
        "cache_b_logf": jax.nn.log_sigmoid(nrm((L, n_phys, PAGE_SIZE, H_B)) + FORGET_BIAS),
        "cache_d_k": nrm((L, DEC_BATCH, d_buf, H_D, HEAD_DIM)),
        "cache_d_v": nrm((L, DEC_BATCH, d_buf, H_D, HEAD_DIM)),
        "cache_mem_k": nrm((L, DEC_BATCH, N_MEM, CA_HEADS, CA_HEAD_DIM)),
        "cache_mem_v": nrm((L, DEC_BATCH, N_MEM, CA_HEADS, CA_HEAD_DIM)),
        "page_table": page_table,
        "norm_g": gain((L, 3, D_MODEL)),
        "w_in": nrm((L, D_MODEL, IN_W), D_MODEL ** -0.5),
        "b_f": FORGET_BIAS + nrm((L, H_B), 0.5),
        "a_mu": jax.random.uniform(ks.pop(), (L, A_PROJ), jnp.float32),
        "a_w0": jax.random.uniform(ks.pop(), (L, GROUP_W), jnp.float32, -6.0, 0.0),
        "a_w2": nrm((L, LORA_W, GROUP_W), 0.1),
        "a_a0": nrm((L, GROUP_W), 0.1),
        "a_a2": nrm((L, LORA_A, GROUP_W), 0.1),
        "a_g2": nrm((L, LORA_G, GROUP_W), LORA_G ** -0.5),
        "a_kk": 0.85 + nrm((L, GROUP_W), 0.05),
        "a_ka": gain((L, GROUP_W)),
        "a_rk": nrm((L, H_A, HEAD_DIM), 0.1),
        "a_lnw": gain((L, GROUP_W)),
        "a_lnb": nrm((L, GROUP_W), 0.02),
        "c_lng": gain((L, GROUP_W)),
        "c_lnb": nrm((L, GROUP_W), 0.02),
        "c_ws": jnp.tril(nrm((L, H_C, CHUNK, CHUNK), CHUNK ** -0.5)),
        "c_bs": gain((L, H_C, CHUNK)),
        "out_g": gain((L, MIX_W)),
        "w_out": nrm((L, MIX_W, D_MODEL), MIX_W ** -0.5),
        "ca_mem_g": gain((L, D_MODEL)),
        "ca_wq": nrm((L, D_MODEL, CA_W), D_MODEL ** -0.5),
        "ca_wk": nrm((L, D_MODEL, CA_W), D_MODEL ** -0.5),
        "ca_wv": nrm((L, D_MODEL, CA_W), D_MODEL ** -0.5),
        "ca_wo": nrm((L, CA_W, D_MODEL), CA_W ** -0.5),
        "peer_wq": nrm((L, D_MODEL, PEER_HEADS * PEER_DK), D_MODEL ** -0.5),
        "peer_keys": nrm((L, PEER_HEADS, 2, N_KEYS, PEER_DK // 2), (PEER_DK // 2) ** -0.5),
        "peer_u": nrm((L, N_EXPERTS, D_MODEL), D_MODEL ** -0.5),
        "peer_v": nrm((L, N_EXPERTS, D_MODEL), PEER_HEADS ** -0.5),
        "final_g": gain((D_MODEL,)),
    }

def reference(x_prompt, x_sample, mem_prompt, state_a_wkv, state_a_shift, cache_b_k, cache_b_v,
              cache_b_logf, cache_d_k, cache_d_v, cache_mem_k, cache_mem_v, page_table,
              norm_g, w_in, b_f, a_mu, a_w0, a_w2, a_a0, a_a2, a_g2, a_kk, a_ka, a_rk, a_lnw, a_lnb,
              c_lng, c_lnb, c_ws, c_bs, out_g, w_out, ca_mem_g, ca_wq, ca_wk, ca_wv, ca_wo,
              peer_wq, peer_keys, peer_u, peer_v, final_g):
    slopes = alibi_slopes(H_D)
    n_past = page_table.shape[1] * PAGE_SIZE
    xp, xs = x_prompt, x_sample
    bp = x_prompt.shape[0]
    (pa_wkv, pa_sh, pb_k, pb_v, pb_lf, pd_k, pd_v, pm_k, pm_v,
     sa_wkv, sa_sh, sb_k, sb_v, sb_lf, sc_v, sd_k, sd_v) = ([] for _ in range(17))
    for l in range(DEPTH):
        rw = (a_mu[l], a_w0[l], a_w2[l], a_a0[l], a_a2[l], a_g2[l], a_kk[l], a_ka[l], a_rk[l],
              a_lnw[l], a_lnb[l])
        cp = (c_lng[l], c_lnb[l], c_ws[l], c_bs[l])

        pa, pb, pc, pd = jnp.split(rmsnorm(xp, norm_g[l, 0]) @ w_in[l], IN_SPLITS, axis=-1)
        ya, s_fin, sh = rwkv7_mixer(pa, jnp.zeros((bp, A_PROJ), jnp.float32),
                                    jnp.zeros((bp, H_A, HEAD_DIM, HEAD_DIM), jnp.float32), *rw)
        yb, kb, vb, lfb = fox_prompt(pb, b_f[l])
        yc, _ = sgu(pc, *cp)
        yd, kd, vd = dilated_prompt(pd, slopes)
        xp = xp + merge_groups(ya, yb, yc, yd, out_g[l], w_out[l])
        mk, mv = memory_kv(mem_prompt, ca_mem_g[l], ca_wk[l], ca_wv[l])
        xp = xp + cross_attend(rmsnorm(xp, norm_g[l, 1]), ca_wq[l], ca_wo[l], mk, mv)
        xp = xp + peer_ffn(rmsnorm(xp, norm_g[l, 2]), peer_wq[l], peer_keys[l], peer_u[l], peer_v[l])
        pa_wkv.append(s_fin); pa_sh.append(sh)
        pb_k.append(kb); pb_v.append(vb); pb_lf.append(lfb)
        pd_k.append(kd); pd_v.append(vd)
        pm_k.append(mk); pm_v.append(mv)

        qa, qb, qc, qd = jnp.split(rmsnorm(xs, norm_g[l, 0]) @ w_in[l], IN_SPLITS, axis=-1)
        ya, s_new, sh_new = rwkv7_mixer(qa, state_a_shift[l], state_a_wkv[l], *rw)
        yb, kb, vb, lfb = fox_sample(qb, b_f[l], cache_b_k[l], cache_b_v[l], cache_b_logf[l], page_table)
        yc, vc = sgu(qc, *cp)
        yd, kd, vd = dilated_sample(qd, cache_d_k[l], cache_d_v[l], n_past, slopes)
        xs = xs + merge_groups(ya, yb, yc, yd, out_g[l], w_out[l])
        xs = xs + cross_attend(rmsnorm(xs, norm_g[l, 1]), ca_wq[l], ca_wo[l], cache_mem_k[l], cache_mem_v[l])
        xs = xs + peer_ffn(rmsnorm(xs, norm_g[l, 2]), peer_wq[l], peer_keys[l], peer_u[l], peer_v[l])
        sa_wkv.append(s_new); sa_sh.append(sh_new)
        sb_k.append(kb); sb_v.append(vb); sb_lf.append(lfb)
        sc_v.append(vc)
        sd_k.append(kd); sd_v.append(vd)

    y_prompt = rmsnorm(xp, final_g)
    y_sample = rmsnorm(xs, final_g)
    return (y_prompt, y_sample,
            jnp.stack(pa_wkv), jnp.stack(pa_sh), jnp.stack(pb_k), jnp.stack(pb_v), jnp.stack(pb_lf),
            jnp.stack(pd_k), jnp.stack(pd_v), jnp.stack(pm_k), jnp.stack(pm_v),
            jnp.stack(sa_wkv), jnp.stack(sa_sh), jnp.stack(sb_k), jnp.stack(sb_v), jnp.stack(sb_lf),
            jnp.stack(sc_v), jnp.stack(sd_k), jnp.stack(sd_v))


_drawn_inputs = setup_inputs


def setup_inputs(seed=0):
    import zlib

    import numpy as np

    out = dict(_drawn_inputs(seed))
    spreads = {}
    factors = {'a_lnb': 4.055, 'c_lnb': 2.912, 'c_bs': 7.701}
    for name, (base, spread) in spreads.items():
        noise = np.random.default_rng([zlib.crc32(name.encode()), seed]).standard_normal(out[name].shape)
        drawn = base * np.exp(spread * noise) if base else spread * noise
        out[name] = jnp.asarray(drawn.astype(out[name].dtype))
    for name, factor in factors.items():
        out[name] = (out[name] * factor).astype(out[name].dtype)
    return out
```

```python
from contextlib import ExitStack

import concourse.bass as bass
import numpy as np
from concourse import mybir

ALU = mybir.AluOpType
ACT = mybir.ActivationFunctionType
F32 = mybir.dt.float32
I32 = mybir.dt.int32
U32 = mybir.dt.uint32
X = mybir.AxisListType.X

P = 128
D = 1024
KC = D // P
T = 256
B, Q = 8, 4
TS = B * Q
N = T + TS
TILES = [(0, P), (P, P), (T, TS)]
HD = 64
PAST = 256
PAGE = 128
MEM = 256
GW = 256
CH = 32
HEADS, TOPK, NK = 8, 16, 128
NEG = -1e30
EPS, GN_EPS = 1e-6, 64e-5
DIL = ((128, 1), (512, 4), (2048, 16))

BLOCKS = (
    [("w_in", 256 * i, 256, "F") for i in range(6)]
    + [("w_in", 1536, 260, "T"), ("w_in", 1796, 256, "F"), ("w_in", 2052, 256, "T"),
       ("w_in", 2308, 256, "F"), ("w_in", 2564, 256, "F"), ("w_in", 2820, 256, "T")]
    + [("ca_wk", 256 * i, 256, "F") for i in range(4)]
    + [("ca_wv", 256 * i, 256, "T") for i in range(4)]
    + [("w_out", 256 * i, 256, "T") for i in range(4)]
    + [("ca_wq", 256 * i, 256, "F") for i in range(4)]
    + [("ca_wo", 256 * i, 256, "T") for i in range(4)]
    + [("peer_wq", 256 * i, 256, "F") for i in range(8)]
)
RING = 3
NR = 8
AHEAD = 4
NIT = 18
LINKS = 15
WCOLS = 260
BQ, BK, CU, DQ, DK = 8, 10, 12, 14, 16
TBV, TLF, TCV, TDV, TW = 0, 256, 260, 516, 772


def linear_units():
    units, last = [], []
    for b, (name, c0, n, form) in enumerate(BLOCKS):
        if form == "F":
            units += [(b, 128 * j, 128, None) for j in range(2)]
        else:
            units += [(b, 0, n, t) for t in range(2 if name == "ca_wv" else 3)]
        last.append(len(units))
    return units, last


UNITS, LAST = linear_units()
ADDS = ("w_out", "ca_wo")
EVAC = []
for _u in UNITS:
    _v = BLOCKS[_u[0]][0] in ADDS
    EVAC.append((_v, 1 + sum(e[0] == _v for e in EVAC)))


def constants():
    i = np.arange(P)
    r, c = i[:, None], i[None, :]
    cols = {}
    cols["ident"] = (r == c) * 1.0
    cols["headsum"] = (r // HD == c // HD) * 1.0
    cols["upinc"] = (r <= c) * 1.0
    cols["ones_lstr"] = np.hstack([np.ones((P, P)), r > c])
    cols["caus"] = np.hstack([np.zeros((P, P)), np.where(c <= r, 0.0, NEG)])
    m16t = (r < c) & (r // 16 == c // 16)
    mi32t = (r <= c) & (r // CH == c // CH)
    ms32t = (r < c) & (r // CH == c // CH)
    cols["m_ab"] = np.hstack([m16t, mi32t])
    cols["m_ak"] = np.hstack([ms32t, mi32t])
    m16 = (r > c) & (r // 16 == c // 16)
    mo = (r > c) & (r // CH == c // CH) & (r // 16 != c // 16)
    cols["m_a"] = np.hstack([m16, mo])
    q4 = (r // Q == c // Q)[:, :TS]
    ms4t, mi4t = ((r < c)[:, :TS] & q4), ((r <= c)[:, :TS] & q4)
    cols["s_ab"] = np.hstack([ms4t, mi4t])
    cols["s_a"] = (r > c)[:, :TS] & q4
    cols["batch"] = (r // Q == np.arange(B)[None]) * 1.0
    reset = np.ones((P, N))
    reset[:, 0:T:CH] = 0
    reset[:, T::Q] = 0
    cols["reset"] = reset
    m = np.arange(P)
    mb, mt = m // 16, m % Q
    nb, nt = np.arange(TS) // Q, np.arange(TS) % Q
    cols["lf_new_l"] = np.tile((nb[:, None] == mb[None]) & (nt[:, None] <= mt[None]), (4, 1)) * 1.0
    rhs = np.ones((TS, PAST + TS))
    rhs[:, PAST:] = nt[:, None] > nt[None]
    cols["lf_new_r"] = np.tile(rhs, (4, 1))
    newmask = np.where((nb[None] == mb[:, None]) & (nt[None] <= mt[:, None]), 0.0, NEG)
    cols["sb_bias"] = np.hstack([np.zeros((P, PAST)), newmask])
    slopes = 2.0 ** (-8.0 * np.arange(1, 5) / 4)

    def dil(off, slope):
        mult = sum(((off >= 0) & (off <= w) & (off % d == 0)) * 1.0 for w, d in DIL)
        return np.where(mult > 0, -slope * off + np.log(np.maximum(mult, 1)), NEG)

    mh = m // Q % 4
    cols["sd_bias"] = np.hstack([
        dil((PAST + mt)[:, None] - np.arange(PAST)[None], slopes[mh][:, None]),
        np.where(newmask == 0, dil(mt[:, None] - nt[None], slopes[mh][:, None]), NEG)])
    for h in range(4):
        cols[f"d_bias{h}0"] = dil(r - c, slopes[h])
        cols[f"d_bias{h}1"] = dil(P + r - np.arange(T)[None], slopes[h])
    cols["iota16"] = np.tile(np.arange(16.0), (P, 1))
    cols["prow"] = i[:, None] * 1.0
    cols["groupsum"] = (r % TS == np.arange(TS)[None]) * 1.0
    cols["eps"] = np.tile([EPS, GN_EPS], (P, 1))
    where, at = {}, 0
    for k, v in cols.items():
        where[k] = (at, v.shape[1])
        at += v.shape[1]
    return np.hstack([np.asarray(v, np.float32) for v in cols.values()]), where


CONST, CONST_AT = constants()

COLS = {}
_n = 0
for _k, _c in (("g0", 8), ("g1", 8), ("g2", 8), ("gm", 8), ("gout", 8), ("mu", 8), ("w0", 2), ("a0", 2),
               ("kks", 2), ("ka", 2), ("rk", 2), ("lnw", 2), ("lnb", 2)):
    COLS[_k] = (_n, _c)
    _n += _c
NCOLS = _n


class Steps:

    def __init__(self, new_semaphore, known=None):
        self.new, self.known = new_semaphore, known or {}
        self.sems, self.order = {}, {}

    def sem(self, name):
        if name not in self.sems:
            self.sems[name] = self.new(name)
            self.order.setdefault(name, [])
        return self.sems[name]

    def inc(self, name, step=None):
        s = self.sem(name)
        self.order[name].append(step)
        return s, 1

    def at(self, name, step):
        s = self.sem(name)
        order = self.known.get(name)
        return s, 1 if order is None else order.index(step) + 1

    def now(self, name):
        return self.sem(name), len(self.order[name])


def sbuf_map(nc):
    m = {}
    at = [(nc.sbuf_base + 63) // 64 * 64]
    places = {}

    def put(name, *shape, dt=F32, rows=P):
        size = int(np.prod(shape)) * 4
        places[name] = at[0]
        m[name] = nc.alloc_sbuf_tensor_at(name, [rows, *shape], dt, offset=at[0])
        at[0] += (size + 63) // 64 * 64
        return m[name]

    put("const", CONST.shape[1])
    put("cols", NCOLS)
    put("xT", KC, N)
    put("W", RING, KC, WCOLS)
    put("YT", KC, N)
    put("stat", 32)
    put("stage", 2, 256)
    put("rows", 776)
    base = at[0]
    put("x", 3, D)
    put("xn", 2, D)
    put("xm", 2, D)
    norms_end = at[0]
    at[0] = base
    put("hT", 18, N)
    put("hTok", 3, TW)
    at[0] = max(at[0], norms_end)
    put("xmT", KC, MEM)
    mix = at[0]
    put("dlt", KC, N)
    for name in ("lw", "aa", "gg", "kk", "kp", "bh", "kh", "t1"):
        put(name, 2, N)
    put("KR", 2, 2, N)
    put("lora", 2 * GW)
    put("shiftc", KC, 1 + B)
    put("shift", KC, B)
    for name in ("AB", "AK", "A1"):
        put(name, 4, 2 * P)
    for name in ("R", "PA", "PTA", "PB", "PTB"):
        put(name, 4, P)
    put("TOK", 4, GW)
    put("WA", 2, GW)
    put("U0", GW)
    put("U0n", GW)
    put("YLT", 2, N)
    put("Y0", 2, N)
    put("MT", 8, 2, P)
    put("NP", 8, 2, HD)
    put("ST", 9, 2, HD)
    put("S0T", B, 2, HD)
    put("sAB", 4, 2 * TS, rows=TS)
    put("sAK", 4, 2 * TS, rows=TS)
    put("sA1", 4, TS, rows=TS)
    put("SC", 2, 256)
    put("PT", 2, 2, P)
    put("LFU", 2, 2, P)
    put("lf", 3, 4)
    put("soft", 64)
    assert at[0] <= nc.sbuf_usable_end, at[0]
    end, at[0] = at[0], mix
    put("KTB", B, 2, 2, P)
    put("VB", B, 2, GW)
    put("KTD", B, 2, PAST)
    put("VD", B, 2, GW)
    put("VL", 3, GW)
    put("wm", 4, P)
    put("wm4", 4, TS, rows=TS)
    put("bsr", 2, P)
    put("sg", 2, P)
    put("QB", 2, B, 2, 32)
    put("SS", 2, PAST + TS)
    put("PTs", 2, 3, P)
    put("LFP", 2, P)
    put("LFN", P, rows=TS)
    put("lfg", B * 2, 4)
    put("pt", B * 2, dt=I32)
    put("idx", B * 2, dt=U32)
    mix2, at[0] = at[0], mix
    put("SQ", KC, N)
    put("RS", 4, N)
    at[0] = mix2
    assert at[0] <= nc.sbuf_usable_end, at[0]
    at[0] = max(at[0], end)
    at[0] = base
    put("X1", 3, D)
    put("XN", 3, D)
    put("gr", 3, D)
    put("softx", 64)
    peer = at[0]
    put("hX", KC, N)
    put("QX", B, KC, 32)
    put("MK", KC, MEM)
    put("MV", 2, D)
    put("MR", 4, KC * MEM)
    put("SCx", 2, 256)
    put("PTx", 2, 2, P)
    put("SSx", 256)
    put("PTy", 2, P)
    assert at[0] <= nc.sbuf_usable_end, at[0]
    at[0] = peer
    put("UR", NR, D)
    put("VR", NR, D)
    put("keys", 16, NK)
    put("SA", NIT, 2, NK)
    put("dg", 4, P)
    put("cur", 2, NK)
    put("cur2", 2, NK)
    put("cand", TOPK, TOPK)
    put("cand2", TOPK, TOPK)
    put("eq", 2, TOPK, TOPK)
    put("ts", 2, TOPK)
    put("ti", 2, TOPK, dt=U32)
    put("tif", 2, TOPK)
    put("bj", 2, TOPK, dt=U32)
    put("bji", 2, TOPK, dt=U32)
    put("bjf", 2, TOPK)
    put("ef", 2, TOPK)
    put("idxu", 2, TOPK, dt=U32)
    put("idxv", 2, TOPK, dt=U32)
    for name in ("bs", "ge", "act", "gl", "wv"):
        put(name, 2, TOPK)
    put("gs", 16)
    assert at[0] <= nc.sbuf_usable_end, at[0]
    at[0] = places["YT"]
    put("qPa", KC, N)
    at[0] = places["const"] + 4 * CONST_AT["m_ab"][0]
    put("qPb", KC, N)
    assert at[0] <= places["const"] + 4 * CONST_AT["iota16"][0]
    return m


def build(nc, io, steps_known=None):
    ctx = ExitStack()
    with ctx:
        S = Steps(lambda n: ctx.enter_context(nc.semaphore(n)), steps_known)
        M = sbuf_map(nc)
        PS = ctx.enter_context(nc.psum_tensor("ps", [P, 8, 512], F32))
        block = ctx.enter_context(nc.Block())
        program(nc, io, S, M, PS, block)
    return S.order


def program(nc, io, S, M, PS, block):
    inc, at, now = S.inc, S.at, S.now

    def cst(name, rows=P, cols=None):
        a, n = CONST_AT[name]
        return M["const"][0:rows, a:a + (cols or n)]

    def col(name, chunk, p0=0, p1=P):
        a = COLS[name][0] + chunk
        return M["cols"][p0:p1, a:a + 1]

    def colb(name, c0, c1, n):
        a = COLS[name][0]
        return M["cols"][:, a + c0:a + c1].unsqueeze(2).to_broadcast([P, c1 - c0, n])

    xT, W, YT, stat, stage = M["xT"], M["W"], M["YT"], M["stat"], M["stage"]
    hT, hTok = M["hT"], M["hTok"]
    ident = cst("ident")

    lw, aa, gg, kk, kp, bh, kh, t1, KR = (M[k] for k in ("lw", "aa", "gg", "kk", "kp", "bh", "kh", "t1", "KR"))
    dlt, lora = M["dlt"], M["lora"]
    Gc, Pp, Pi, t2 = (dlt[:, 2 * j:2 * j + 2, :] for j in range(4))
    TOK, WA, U0, U0n, YLT, Y0 = (M[k] for k in ("TOK", "WA", "U0", "U0n", "YLT", "Y0"))
    MT, NPr, ST, S0T = M["MT"], M["NP"], M["ST"], M["S0T"]
    rT, kT, vT = hT[:, 0:2, :], hT[:, 2:4, :], hT[:, 4:6, :]

    ORDER = (
        [("lin", b) for b in range(12)] + [("rw_pre", 0), ("lin", 12), ("rw_kk", 0), ("lin", 13), ("lin", 14),
         ("rw_vec", 0), ("rw_tile", 0), ("rw_tile", 1), ("rw_scan", 0), ("rw_tile", 2), ("rw_sample", 0), ("rw_out", 0)]
        + [("lf", 0), ("lin", 15), ("lin", 16), ("lin", 17), ("attn", 0), ("sgu", 0), ("lin", 18), ("lin", 19),
           ("sattn", 0), ("gnorm", 0)]
        + [("lin", b) for b in range(20, 24)] + [("norm", 0)] + [("lin", b) for b in range(24, 28)]
        + [("cross", 0), ("scross", 0)] + [("lin", b) for b in range(28, 32)] + [("norm", 1)]
        + [("lin", 32), ("score", 0), ("lin", 33)]
        + [s for h in range(1, 7) for s in (("lin", 33 + h), ("score", h))] + [("score", 7), ("peer", 0)])
    X1, XN, gr, hX, QX, MK, MV, MR, SCx, PTx, SSx, PTy, softx = (
        M[k] for k in ("X1", "XN", "gr", "hX", "QX", "MK", "MV", "MR", "SCx", "PTx", "SSx", "PTy", "softx"))
    UR, VR, keys, SA, dg = (M[k] for k in ("UR", "VR", "keys", "SA", "dg"))

    def qP(chunk):
        return M["qPa" if chunk < KC else "qPb"][:, chunk % KC, :]

    CUNITS = [(h, qb) for h in range(4) for qb in range(2)]

    def x_of_block(b):
        return "xT" if b < 12 or 24 <= b < 28 or b >= 32 else "xmT" if b < 20 else "YT"

    def peer_tiles():
        return ((0, 0, 8), (1, 8, 8), (2, 16, 2))

    AUNITS = [(BQ, BK, TBV, 2, h, qb) for h in range(4) for qb in range(2)] \
        + [(DQ, DK, TDV, 6, h, qb) for h in range(4) for qb in range(2)]
    NA = len(AUNITS)
    SC, PT, LFU, lf, soft = (M[k] for k in ("SC", "PT", "LFU", "lf", "soft"))
    KTB, VB, KTD, VD, VL, QB, SS, PTs = (M[k] for k in ("KTB", "VB", "KTD", "VD", "VL", "QB", "SS", "PTs"))
    upinc, ones_lstr = cst("upinc"), cst("ones_lstr")
    ones, lstr = ones_lstr[:, 0:P], ones_lstr[:, P:]

    def heads():
        for par in range(2):
            for c in range(2):
                yield 2 * par + c, par, c, 2 * c + par, slice(HD * par, HD * par + HD)

    def tile_mats(t):
        m = TILES[t][1]
        if t < 2:
            ab, ak, a1 = M["AB"], M["AK"], M["A1"]
            return (lambda i: ab[:, i, 0:m], lambda i: ab[:, i, m:2 * m], lambda i: ak[:, i, 0:m],
                    lambda i: ak[:, i, m:2 * m], lambda i: a1[:, i, 0:m], lambda i: a1[:, i, m:2 * m])
        ab, ak, a1 = M["sAB"], M["sAK"], M["sA1"]
        return (lambda i: ab[:, i, 0:m], lambda i: ab[:, i, m:2 * m], lambda i: ak[:, i, 0:m],
                lambda i: ak[:, i, m:2 * m], lambda i: a1[:, i, :], None)

    def quad(name, m):
        return M[name][0:m].rearrange("p a b -> p (a b)")[:, 0:4 * m].rearrange("p (a b) -> p a b", a=4)

    XB, XV, XU = (M[k][0:TS].rearrange("p a b -> p (a b)").rearrange("p (b f) -> p b f", b=B)
                  for k in ("AB", "AK", "A1"))

    def xpose_bank(j):
        return PS[:, 2 + j % 6, :]

    NORMS0 = [("x", t) for t in range(3)] + [("xm", t) for t in range(2)]

    def rows_of(kind, t):
        return TILES[t][1] if kind == "x" else P

    @block.sync
    def _(sp):
        sp.dma_start(M["x"][:, 0, :], io["x_all"][0:P, :]).then_inc(S.sem("x0_in"), 16)
        sp.dma_start(M["cols"][:], io["cols"]).then_inc(S.sem("cols_in"), 16)
        sp.dma_start(M["const"][:], io["const"]).then_inc(S.sem("const_in"), 16)
        sp.dma_start(M["x"][:, 1, :], io["x_all"][P:T, :]).then_inc(S.sem("x1_in"), 16)
        sp.dma_start(M["x"][0:TS, 2, :], io["x_all"][T:N, :]).then_inc(S.sem("x2_in"), 16)
        for t in range(2):
            sp.dma_start(M["xm"][:, t, :], io["mem_prompt"][t * P:(t + 1) * P, :]).then_inc(S.sem(f"xm{t}_in"), 16)

        def load_block(b):
            name, c0, n, _ = BLOCKS[b]
            if b >= RING:
                sp.wait_ge(S.sem("pe_lin"), LAST[b - RING])
            sp.dma_start(W[:, b % RING, :, 0:n], io[name].rearrange("(k p) n -> p k n", p=P)[:, :, c0:c0 + n])\
                .then_inc(S.sem(f"w{b % RING}_in"), 16)

        for b in range(3):
            load_block(b)
        sp.dma_start(lora[0:64, 0:GW], io["a_w2"]).then_inc(S.sem("rwp_in"), 16)
        sp.dma_start(lora[64:128, 0:GW], io["a_a2"]).then_inc(S.sem("rwp_in"), 16)
        sp.dma_start(lora[:, GW:], io["a_g2"]).then_inc(S.sem("rwp_in"), 16)
        sp.dma_start(M["shift"][:], io["shift"]).then_inc(S.sem("rwp_in"), 16)
        sp.dma_start(S0T[:], io["s0T"]).then_inc(S.sem("rwp_in"), 16)
        for a, n, name in ((0, GW, "c_lng"), (GW, GW, "c_lnb"), (2 * GW, 4, "b_f")):
            sp.dma_start(M["rows"][:, a:a + n], io[name].to_broadcast([P, n])).then_inc(S.sem("rows_in"), 16)
        for b in range(3, 20):
            load_block(b)

        sp.wait_ge(*at("act_lin", ("unit", LAST[11])))
        n_out = 0
        for name, src in (("o_bk", hT[:, BK:BK + 2, :]), ("o_dk", hT[:, DK:DK + 2, :]),
                          ("o_tok0", hTok[:, 0, :]), ("o_tok1", hTok[:, 1, :]), ("o_tok2", hTok[0:TS, 2, :])):
            sp.dma_start(io[name], src).then_inc(S.sem("out_sp"), 16)
            n_out += 1
        sp.wait_ge(*at("dve_rw", "shiftc"))
        sp.dma_start(io["o_shift"], M["shiftc"][:]).then_inc(S.sem("out_sp"), 16)
        sp.wait_ge(*at("dve_st", 7))
        sp.dma_start(io["o_pwkv"], ST[:, 8, :, :]).then_inc(S.sem("out_sp"), 16)
        sp.wait_ge(*at("dve_rw", "swkv"))
        sp.dma_start(io["o_swkv"], NPr[:]).then_inc(S.sem("out_sp"), 16)
        sp.wait_ge(*at("dve_y", "a"))
        sp.dma_start(M["wm"][:], io["wsT"]).then_inc(S.sem("sgu_in"), 16)
        sp.dma_start(M["wm4"][:], io["ws4"]).then_inc(S.sem("sgu_in"), 16)
        sp.dma_start(M["bsr"][:], io["bsr"]).then_inc(S.sem("sgu_in"), 16)
        sp.dma_start(M["pt"][:], io["page_table"].to_broadcast([P, B * 2])).then_inc(S.sem("pt_in"), 16)
        sp.dma_start(KTD[:], io["dkT"]).then_inc(S.sem("dk_in"), 16)
        sp.dma_start(VD[:], io["dv"]).then_inc(S.sem("dv_in"), 16)
        sp.wait_ge(*at("dve_lf", "lf"))
        sp.dma_start(io["o_lf"], lf[:]).then_inc(S.sem("out_sp"), 16)
        sp.wait_ge(*at("dve_sg", ("v", 2)))
        sp.dma_start(io["o_cv"], VL[0:TS, 2, :]).then_inc(S.sem("out_sp"), 16)
        for b in range(20, 23):
            load_block(b)
        sp.wait_ge(*at("dve_gn", 3))
        for j in range(2):
            sp.wait_ge(S.sem(f"out_stage{j}"), 16 * 8)
        for t, (t0, m) in enumerate(TILES):
            sp.dma_start(X1[0:m, t, :], io["x_all"][t0:t0 + m, :]).then_inc(S.sem("X1_in"), 16)
        for r in range(3):
            sp.dma_start(gr[:, r, :], io["gains"][r:r + 1, :].to_broadcast([P, D])).then_inc(S.sem("gr_in"), 16)
        sp.dma_start(MK[:], io["o_memk"].rearrange("(c p) m -> p c m", p=P)).then_inc(S.sem("mk_in"), 16)
        sp.dma_start(MV[:], io["o_memv"].rearrange("(k p) n -> p k n", p=P)).then_inc(S.sem("mv_in"), 16)
        for b in range(23, 28):
            load_block(b)
        for i in range(2 * B):
            if i >= 4:
                j = i - 4
                sp.wait_ge(*at("pe_mr", ("k", j) if j < B else ("v", j - B)))
            sp.dma_start(MR[:, i % 4, :], io["mk_s" if i < B else "mv_s"][i % B]).then_inc(S.sem(f"mr{i % 4}_in"), 16)
        for b in range(28, 31):
            load_block(b)
        sp.wait_ge(*at("act_cx", "ys"))
        sp.dma_start(keys[:], io["keysT"]).then_inc(S.sem("keys_in"), 16)
        for b in range(31, 40):
            load_block(b)
        sp.wait_ge(*at("dve_nx", (1, 2)))
        for g in range(4):
            sp.dma_start(gr[32 * g:32 * g + 32, 0, :], XN[0:TS, 2, :]).then_inc(S.sem("xs_in"), 16)
        for t, (t0, m) in enumerate(TILES):
            sp.wait_ge(*at("dve_fin", ("y", t)))
            sp.dma_start(io["o_y"][t0:t0 + m, :], X1[0:m, t, :]).then_inc(S.sem("out_sp"), 16)
        sp.wait_ge(S.sem("out_sp"), 16 * (n_out + 8))

    @block.tensor
    def _(pe):
        mm, tr = nc.tensor.matmul, nc.tensor.transpose
        npose = [0]

        def transposes(kind, t, src, m, done):
            for half in range(2):
                if npose[0] >= 6:
                    pe.wait_ge(*at("dve_xT", npose[0] - 6))
                for j in range(4):
                    k = 4 * half + j
                    ins = tr(xpose_bank(npose[0])[:, j * P:j * P + m], src[0:m, k * P:(k + 1) * P], ident[0:m, 0:m])
                ins.then_inc(*inc(done, npose[0]))
                npose[0] += 1

        pe.wait_ge(S.sem("const_in"), 16)
        for i, (kind, t) in enumerate(NORMS0):
            pe.wait_ge(*at("dve_xn", (kind, t)))
            transposes(kind, t, M["xn"][:, i % 2, :], rows_of(kind, t), "pe_xT")

        def linear(b, src="xT"):
            name, c0, n, form = BLOCKS[b]
            pe.wait_ge(S.sem(f"w{b % RING}_in"), 16 * (b // RING + 1))
            w = W[:, b % RING, :, :]
            for u in range(LAST[b - 1] if b else 0, LAST[b]):
                _, cc, nn, t = UNITS[u]
                if u >= 2:
                    dve, count = EVAC[u - 2]
                    pe.wait_ge(S.sem("dve_lin" if dve else "act_lin"), count)
                a = M[src]
                for k in range(KC):
                    if t is None:
                        ins = mm(PS[:, u % 2, 0:a.shape[2]], w[:, k, cc:cc + nn], a[:, k, :],
                                 start=k == 0, stop=k == KC - 1)
                    else:
                        t0, m = TILES[t]
                        ins = mm(PS[0:m, u % 2, 0:nn], a[:, k, t0:t0 + m], w[:, k, 0:nn],
                                 start=k == 0, stop=k == KC - 1)
                ins.then_inc(*inc("pe_lin", ("unit", u + 1)))

        def rw_pre():
            pe.wait_ge(S.sem("rwp_in"), 16 * 5)
            pe.wait_ge(*at("dve_xT", 9))
            pe.wait_ge(*at("act_rw", "tanh"))
            for c in range(2):
                ins = mm(PS[:, 2 + c, 0:N], lora[0:64, c * P:(c + 1) * P], t1[0:64, 0, :], start=True, stop=True)
            ins.then_inc(*inc("pe_rw", "lora_w"))
            for c in range(2):
                ins = mm(PS[:, 4 + c, 0:N], lora[64:128, c * P:(c + 1) * P], hT[64:128, 6, :], start=True, stop=True)
            ins.then_inc(*inc("pe_rw", "lora_a"))
            pe.wait_ge(*at("act_rw", "sigg"))
            for c in range(2):
                ins = mm(PS[:, 6 + c, 0:N], lora[:, GW + c * P:GW + (c + 1) * P], t1[:, 1, :], start=True, stop=True)
            ins.then_inc(*inc("pe_rw", "lora_g"))

        def headsum(src, bank, step):
            for c in range(2):
                ins = mm(PS[:, bank + c, 0:N], cst("headsum"), src[:, c, :], start=True, stop=True)
            ins.then_inc(*inc("pe_rw", step))

        def rw_kk():
            pe.wait_ge(*at("dve_rw", "kksq"))
            pe.wait_ge(*at("act_rw", "sigw"))
            headsum(t2, 2, "kkn")

        def rw_vec():
            pe.wait_ge(*at("dve_rw", "bon"))
            pe.wait_ge(*at("act_rw", "siga"))
            headsum(t2, 4, "bonus")

        def rw_tile(t):
            t0, m = TILES[t]
            a1t, a3t, a2t, a4t, a16, off = tile_mats(t)
            if t == 0:
                pe.wait_ge(*at("act_rw", "g"))
                pe.wait_ge(*at("dve_rw", "kh"))
            else:
                pe.wait_ge(*at("dve_rw", ("mn", t - 1)))
                pe.wait_ge(*at("act_rw", ("y0", t - 1)))
            for j, src in enumerate((KR[:, :, 0, :], bh, kh, vT)):
                for c in range(2):
                    ins = tr(PS[0:m, 6 + j // 2, (j % 2) * 256 + c * P:(j % 2) * 256 + (c + 1) * P],
                             src[:, c, t0:t0 + m], ident)
            ins.then_inc(*inc("pe_rw", ("tok", t)))
            if t == 0:
                pe.wait_ge(*at("dve_rw", "kkm"))
                pe.wait_ge(*at("dve_rw", "bonus"))
            if t == 2:
                pe.wait_ge(*at("dve_st", 7))
            for i, par, c, h, ph in heads():
                ins = mm(PS[0:m, 2 + par, c * 2 * m:(c + 1) * 2 * m], bh[ph, c, t0:t0 + m],
                         KR[ph, c, 0:2, t0:t0 + m], start=True, stop=True)
            ins.then_inc(*inc("pe_rw", ("x1", t)))
            for i, par, c, h, ph in heads():
                ins = mm(PS[0:m, 4 + par, c * 2 * m:(c + 1) * 2 * m], kh[ph, c, t0:t0 + m],
                         KR[ph, c, 0:2, t0:t0 + m], start=True, stop=True)
            ins.then_inc(*inc("pe_rw", ("x2", t)))
            pe.wait_ge(*at("act_rw", ("tok", t)))
            for i, par, c, h, ph in heads():
                ins = mm(PS[0:m, 6 + par, c * m:(c + 1) * m], KR[ph, c, 0, t0:t0 + m],
                         bh[ph, c, t0:t0 + m], start=True, stop=True)
            ins.then_inc(*inc("pe_rw", ("x3", t)))

            def four(bank, lhs, rhs, step):
                for i in range(4):
                    ins = mm(PS[0:m, bank, i * m:(i + 1) * m], lhs(i), rhs(i), start=True, stop=True)
                ins.then_inc(*inc("pe_rw", (step, t)))

            R, PA, PTA, PB, PTB = ((lambda i, q=quad(k, m): q[:, i, :]) for k in ("R", "PA", "PTA", "PB", "PTB"))
            pe.wait_ge(*at("dve_rw", ("R0", t)))
            four(2, a1t, a16, "P2")
            if t == 2:
                pe.wait_ge(*at("act_rw", ("P2", t)))
                four(4, PA, R, "R1")
            else:
                four(3, a16, a1t, "P2T")
                pe.wait_ge(*at("act_rw", ("P2", t)))
                four(4, PA, R, "R1")
                pe.wait_ge(*at("act_rw", ("P2T", t)))
                four(5, PTA, PA, "P4")
                four(2, PA, PTA, "P4T")
                pe.wait_ge(*at("act_rw", ("P4", t)))
                pe.wait_ge(*at("dve_rw", ("R1", t)))
                four(3, PB, R, "R2")
                pe.wait_ge(*at("act_rw", ("P4T", t)))
                four(4, PTB, PB, "P8")
                pe.wait_ge(*at("act_rw", ("P8", t)))
                pe.wait_ge(*at("dve_rw", ("R2", t)))
                four(2, PA, R, "R3")
                pe.wait_ge(*at("dve_rw", ("R3", t)))
                for i in range(4):
                    ins = tr(PS[:, 5, i * P:(i + 1) * P], R(i), ident)
                ins.then_inc(*inc("pe_rw", ("T16", t)))
                four(4, off, R, "Q")
                pe.wait_ge(*at("act_rw", ("T16", t)))
                pe.wait_ge(*at("act_rw", ("Q", t)))
                four(3, PTA, PB, "Z")
            pe.wait_ge(*at("dve_rw", ("T", t)))
            hs = lambda h: slice(h * HD, (h + 1) * HD)
            for i, par, c, h, ph in heads():
                mm(PS[0:m, 6, hs(h)], R(i), TOK[0:m, 0, hs(h)], start=True, stop=True)
                ins = mm(PS[0:m, 6, 256 + h * HD:256 + (h + 1) * HD], a2t(i), TOK[0:m, 3, hs(h)],
                         start=True, stop=True)
            ins.then_inc(*inc("pe_rw", ("wa", t)))
            pe.wait_ge(*at("act_rw", ("wa", t)))
            for i, par, c, h, ph in heads():
                ins = mm(PS[0:m, 7, hs(h)], R(i), WA[0:m, 1, hs(h)], start=True, stop=True)
            ins.then_inc(*inc("pe_rw", ("u0", t)))
            for i, par, c, h, ph in heads():
                ins = mm(PS[ph, 5, c * m:(c + 1) * m], WA[0:m, 0, hs(h)], a3t(i), start=True, stop=True)
            ins.then_inc(*inc("pe_rw", ("yl", t)))
            pe.wait_ge(*at("act_rw", ("u0n", t)))
            for i, par, c, h, ph in heads():
                mm(PS[ph, 4, c * m:(c + 1) * m], TOK[0:m, 3, hs(h)], a4t(i), start=True, stop=False,
                   skip_group_check=True)
                ins = mm(PS[ph, 4, c * m:(c + 1) * m], U0n[0:m, hs(h)], a3t(i), start=False, stop=True,
                         skip_group_check=True)
            ins.then_inc(*inc("pe_rw", ("y0", t)))
            if t == 2:
                return
            for cc in range(4):
                bank = (2, 3, 6, 7)[cc]
                rows = slice(CH * cc, CH * cc + CH)
                for i, par, c, h, ph in heads():
                    mm(PS[ph, bank, c * HD:(c + 1) * HD], WA[rows, 0, hs(h)], TOK[rows, 1, hs(h)],
                       start=True, stop=True, skip_group_check=True)
                    mm(PS[ph, bank, P + c * HD:P + (c + 1) * HD], TOK[rows, 2, hs(h)], TOK[rows, 3, hs(h)],
                       start=True, stop=False, skip_group_check=True)
                    ins = mm(PS[ph, bank, P + c * HD:P + (c + 1) * HD], TOK[rows, 1, hs(h)], U0[rows, hs(h)],
                             start=False, stop=True, skip_group_check=True)
                ins.then_inc(*inc("pe_rw", ("mn", t, cc)))

        def rw_scan():
            pe.wait_ge(*at("dve_rw", ("mn", 1)))
            pe.wait_ge(*at("pool_rw", "zero"))
            for n in range(8):
                if n:
                    pe.wait_ge(*at("dve_st", n - 1))
                for c in range(2):
                    ins = mm(PS[:, 2 + n % 2, c * HD:(c + 1) * HD], MT[:, n, c, :], ST[:, n, c, :],
                             start=True, stop=True)
                ins.then_inc(*inc("pe_rw", ("st", n)))

        def rw_sample():
            hs = lambda h: slice(h * HD, (h + 1) * HD)
            pe.wait_ge(*at("dve_rw", ("T", 2)))
            for c in range(2):
                pe.wait_ge(*at("pool_rw", ("x", c)))
                for par in range(2):
                    h, ph, fs = 2 * c + par, slice(HD * par, HD * par + HD), slice(HD * par, HD * par + HD)
                    mm(PS[ph, 2 + c, :], WA[0:TS, 0, hs(h)], XB[:, :, fs], start=True, stop=True,
                       skip_group_check=True)
                    mm(PS[ph, 6 + c, :], TOK[0:TS, 2, hs(h)], XV[:, :, fs], start=True, stop=False,
                       skip_group_check=True)
                    ins = mm(PS[ph, 6 + c, :], TOK[0:TS, 1, hs(h)], XU[:, :, fs], start=False, stop=True,
                             skip_group_check=True)
                ins.then_inc(*inc("pe_rw", ("smn", c)))
            for c in range(2):
                pe.wait_ge(*at("dve_rw", ("smn", c)))
                if c == 0:
                    pe.wait_ge(*at("act_rw", ("y0", 2)))
                    pe.wait_ge(*at("dve_rw", ("yl", 2)))
                for b in range(B):
                    ins = mm(PS[:, 4 + c, b * HD:(b + 1) * HD], MT[:, b, c, :], S0T[:, b, c, :],
                             start=True, stop=True)
                ins.then_inc(*inc("pe_rw", ("ss", c)))

        def rw_out():
            pe.wait_ge(*at("dve_rw", ("smn", 1)))
            for i, par, c, h, ph in heads():
                for n in range(8):
                    ins = mm(PS[ph, 2 + par, c * T + n * CH:c * T + (n + 1) * CH], ST[ph, n, c, :],
                             YLT[ph, c, n * CH:(n + 1) * CH], start=True, stop=True, skip_group_check=True)
            ins.then_inc(*inc("pe_rw", "yst"))
            for i, par, c, h, ph in heads():
                for b in range(B):
                    ins = mm(PS[ph, 6 + par, c * TS + b * Q:c * TS + (b + 1) * Q], S0T[ph, b, c, :],
                             YLT[ph, c, T + b * Q:T + (b + 1) * Q], start=True, stop=True, skip_group_check=True)
            ins.then_inc(*inc("pe_rw", "yss"))
            pe.wait_ge(*at("dve_rw", "swkv"))
            pe.wait_ge(*at("dve_rw", "y"))
            headsum(Y0, 4, "mean")
            pe.wait_ge(*at("act_rw", "ysq"))
            headsum(t1, 2, "var")

        def attn():
            for s in range(NA + 2):
                if s < NA:
                    u = s
                    qc, kc, _, _, h, qb = AUNITS[u]
                    ph, w, ps = slice(HD * (h % 2), HD * (h % 2) + HD), P * (qb + 1), PS[:, 2 + u % 2, :]
                    if u >= 2:
                        pe.wait_ge(*at("dve_at", ("sc", u - 2)))
                    else:
                        pe.wait_ge(*at("dve_y", "a"))
                    fox = qc == BQ
                    ins = mm(ps[:, 0:w], hT[ph, qc + h // 2, qb * P:(qb + 1) * P], hT[ph, kc + h // 2, 0:w],
                             start=True, stop=not fox, skip_group_check=True)
                    if fox:
                        pe.wait_ge(*at("dve_at", ("lfu", u)))
                        ins = mm(ps[:, 0:P], LFU[:, u % 2, 0, :], lstr, start=False, stop=qb == 0,
                                 skip_group_check=True)
                        if qb:
                            ins = mm(ps[:, 0:w], LFU[:, u % 2, 1, :], ones_lstr, start=False, stop=True,
                                     skip_group_check=True)
                    ins.then_inc(*inc("pe_at", ("sc", u)))
                if 1 <= s <= NA:
                    u = s - 1
                    qb = AUNITS[u][5]
                    pe.wait_ge(*at("dve_at", ("p", u)))
                    for kt in range(qb + 1):
                        ins = tr(PS[:, 4 + u % 2, kt * P:(kt + 1) * P], SC[:, u % 2, kt * P:(kt + 1) * P], ident)
                    ins.then_inc(*inc("pe_at", ("pt", u)))
                if s >= 2:
                    u = s - 2
                    _, _, vc, _, h, qb = AUNITS[u]
                    pe.wait_ge(*at("act_at", ("pt", u)))
                    if u >= 2:
                        pe.wait_ge(*at("dve_at", ("o", u - 2)))
                    ph = slice(HD * (h % 2), HD * (h % 2) + HD)
                    for kt in range(qb + 1):
                        ins = mm(PS[ph, 6 + u % 2, 0:P], hTok[:, kt, vc + h * HD:vc + (h + 1) * HD], PT[:, u % 2, kt, :],
                                 start=kt == 0, stop=kt == qb, skip_group_check=True)
                    ins.then_inc(*inc("pe_at", ("o", u)))

        def sgu():
            for t, (t0, m) in enumerate(TILES):
                pe.wait_ge(*at("dve_sg", ("v", t)))
                if t == 0:
                    pe.wait_ge(*at("dve_at", ("o", NA - 1)))
                if t == 2:
                    pe.wait_ge(*at("dve_sg", ("y", 0)))
                for i, par, c, h, ph in heads():
                    ins = mm(PS[ph, 2 + t % 2, c * m:(c + 1) * m], VL[0:m, t, h * HD:(h + 1) * HD],
                             M["wm"][:, h, :] if t < 2 else M["wm4"][:, h, :], start=True, stop=True,
                             skip_group_check=True)
                ins.then_inc(*inc("pe_sg", t))

        def sattn():
            for g, (kc, vc) in enumerate(((BK, TBV), (DK, TDV))):
                ps = PS[:, 2 + g, :]
                if g == 0:
                    pe.wait_ge(*at("dve_sg", ("y", 2)))
                    pe.wait_ge(*at("pool_sa", "q"))
                    pe.wait_ge(*at("dve_sa", "lfn"))
                    pe.wait_ge(S.sem("gath_in"), 16 * 16)
                    mm(ps[:, 0:PAST], M["LFP"][:, 1, :], ones_lstr, start=True, stop=False, skip_group_check=True)
                    mm(ps[:, 0:P], M["LFP"][:, 0, :], lstr, start=False, stop=False, skip_group_check=True)
                    mm(ps[:, 0:PAST + TS], M["LFN"][:], cst("lf_new_r", TS), start=False, stop=False,
                       skip_group_check=True)
                else:
                    pe.wait_ge(S.sem("dk_in"), 16)
                for b in range(B):
                    rows = slice(32 * (b // 2), 32 * (b // 2) + 32)
                    for c in range(2):
                        k = KTB[:, b, :, c, :] if g == 0 else KTD[:, b, c, :]
                        mm(ps[rows, 0:PAST], QB[:, g, b, c, :], k, start=g == 1 and b % 2 == 0 and c == 0,
                           stop=False, skip_group_check=True)
                        ins = mm(ps[rows, PAST:PAST + TS], QB[:, g, b, c, :], hT[:, kc + c, T:N], start=False,
                                 stop=True, skip_group_check=True)
                ins.then_inc(*inc("pe_sa", ("sc", g)))
            for g in range(2):
                pe.wait_ge(*at("dve_sa", ("p", g)))
                for kt in range(2):
                    tr(PS[:, 4 + g, kt * P:(kt + 1) * P], SS[:, g, kt * P:(kt + 1) * P], ident)
                tr(PS[0:TS, 4 + g, 2 * P:3 * P], SS[:, g, PAST:], ident).then_inc(*inc("pe_sa", ("pt", g)))
            for g, vc in enumerate((TBV, TDV)):
                pe.wait_ge(*at("act_sa", ("pt", g)))
                pe.wait_ge(S.sem("gv_in" if g == 0 else "dv_in"), 16 * 16 if g == 0 else 16)
                v = VB if g == 0 else VD
                for c in range(2):
                    for b in range(B):
                        o = PS[:, 6 + g, (c * B + b) * 8:(c * B + b) * 8 + 8]
                        cols = slice(b * 16 + 8 * c, b * 16 + 8 * c + 8)
                        for kt in range(2):
                            mm(o, v[:, b, kt, c * P:(c + 1) * P], PTs[:, g, kt, cols], start=kt == 0, stop=False)
                        ins = mm(o, hTok[0:TS, 2, vc + c * P:vc + (c + 1) * P], PTs[0:TS, g, 2, cols],
                                 start=False, stop=True)
                ins.then_inc(*inc("pe_sa", ("o", g)))

        def gnorm():
            for g in range(4):
                pe.wait_ge(*at("act_gn", ("sq", g)))
                if g == 0:
                    pe.wait_ge(*at("act_sa", ("pt", 1)))
                for j in range(2):
                    ins = mm(PS[:, 2 + g, 0:N], ones, M["SQ"][:, 2 * g + j, :], start=j == 0, stop=j == 1)
                ins.then_inc(*inc("pe_gn", g))

        def norm(i):
            for t, (t0, m) in enumerate(TILES):
                pe.wait_ge(*at("dve_nx", (i, t)))
                for half in range(2):
                    bank = 2 + 2 * t + half
                    for j in range(4):
                        k = 4 * half + j
                        ins = tr(PS[:, bank, j * P:j * P + m], XN[0:m, t, k * P:(k + 1) * P], ident[0:m, 0:m])
                    ins.then_inc(*inc("pe_nx", (i, t, half)))
            pe.wait_ge(*at("act_nx", (i, 2, 1)))
            if i == 1:
                residual([0, 1]).then_inc(S.sem("v_free"), NR)

        def cross(_):
            nu = len(CUNITS)
            for s in range(nu + 2):
                if s < nu:
                    h, qb = CUNITS[s]
                    if s == 0:
                        pe.wait_ge(*at("act_lin", ("unit", LAST[27])))
                        pe.wait_ge(S.sem("mk_in"), 16)
                    else:
                        if s >= 2:
                            pe.wait_ge(*at("act_cx", ("p", s - 2)))
                    for c in range(2):
                        ins = mm(PS[:, 2 + s % 2, 0:MEM], hX[:, 2 * h + c, qb * P:(qb + 1) * P], MK[:, 2 * h + c, :],
                                 start=c == 0, stop=c == 1)
                    ins.then_inc(*inc("pe_cx", ("sc", s)))
                if 1 <= s <= nu:
                    u = s - 1
                    pe.wait_ge(*at("dve_cx", ("p", u)))
                    if u >= 2:
                        pe.wait_ge(*at("act_cx", ("pt", u - 2)))
                    for kt in range(2):
                        ins = tr(PS[:, 4 + u % 2, kt * P:(kt + 1) * P], SCx[:, u % 2, kt * P:(kt + 1) * P], ident)
                    ins.then_inc(*inc("pe_cx", ("pt", u)))
                if s >= 2:
                    u = s - 2
                    h, qb = CUNITS[u]
                    pe.wait_ge(*at("act_cx", ("pt", u)))
                    if u == 0:
                        pe.wait_ge(S.sem("mv_in"), 16)
                    if u >= 2:
                        pe.wait_ge(*at("dve_cx", ("o", u - 2)))
                    for c in range(2):
                        k = 2 * h + c
                        for kt in range(2):
                            ins = mm(PS[:, 6 + u % 2, c * P:(c + 1) * P], MV[:, kt, k * P:(k + 1) * P], PTx[:, u % 2, kt, :],
                                     start=kt == 0, stop=kt == 1)
                    ins.then_inc(*inc("pe_cx", ("o", u)))

        def scross(_):
            pe.wait_ge(*at("pool_cx", "q"))
            for b in range(B):
                rows = slice(32 * (b // 2), 32 * (b // 2) + 32)
                pe.wait_ge(S.sem(f"mr{b % 4}_in"), 16 * (b // 4 + 1))
                for c in range(KC):
                    ins = mm(PS[rows, 2, 0:MEM], QX[:, b, c, :], MR[:, b % 4, c * MEM:(c + 1) * MEM],
                             start=b % 2 == 0 and c == 0, stop=b % 2 == 1 and c == KC - 1, skip_group_check=True)
                ins.then_inc(*inc("pe_mr", ("k", b)))
            pe.wait_ge(*at("dve_cx", "ps"))
            for kt in range(2):
                ins = tr(PS[:, 4, kt * P:(kt + 1) * P], SSx[:, kt * P:(kt + 1) * P], ident)
            ins.then_inc(*inc("pe_cx", "pts"))
            pe.wait_ge(*at("act_cx", "pts"))
            pe.wait_ge(*at("dve_cx", ("o", len(CUNITS) - 1)))
            for b in range(B):
                pe.wait_ge(S.sem(f"mr{b % 4}_in"), 16 * ((b + B) // 4 + 1))
                for c in range(KC):
                    a = b * 16 + c // 2 * Q
                    for kt in range(2):
                        ins = mm(PS[:, 6, (c * B + b) * Q:(c * B + b + 1) * Q],
                                 MR[:, b % 4, kt * D + c * P:kt * D + (c + 1) * P], PTy[:, kt, a:a + Q],
                                 start=kt == 0, stop=kt == 1)
                ins.then_inc(*inc("pe_mr", ("v", b)))

        def residual(tiles):
            for t in tiles:
                m = TILES[t][1]
                for half in range(2):
                    ins = mm(PS[:, 2 + 2 * t + half, :], ident[0:m, :], X1[0:m, t, half * 512:(half + 1) * 512],
                             start=True, stop=False, skip_group_check=True)
            return ins

        def score(h):
            if h == 0:
                pe.wait_ge(S.sem("keys_in"), 16)
            else:
                pe.wait_ge(S.sem("act_s"), h)
            pe.wait_ge(*at("act_lin", ("unit", LAST[32 + h])))
            for c in range(2):
                for t in range(2):
                    mm(PS[:, 6, (2 * t + c) * NK:(2 * t + c + 1) * NK], qP(2 * h + c)[:, t * P:(t + 1) * P],
                       keys[:, 2 * h + c, :], start=True, stop=True)
                rows = slice(32 * (h // 2), 32 * (h // 2) + 32)
                ins = mm(PS[rows, 7, c * NK:(c + 1) * NK], qP(2 * h + c)[:, T:N], keys[:, 2 * h + c, :],
                         start=True, stop=True, skip_group_check=True)
            ins.then_inc(S.sem("pe_s"), 1)

        def peer(_):
            pe.wait_ge(S.sem("act_s"), NIT)
            residual([2])

            def rounds(t, it, j):
                for k in range(TOPK):
                    pe.wait_ge(S.sem(f"v{k % NR}_in"), (it * (TOPK // NR) + k // NR + 1) * 16)
                    pe.wait_ge(S.sem("act_dg"), it * TOPK + k + 1)
                    for half in range(2):
                        ins = mm(PS[:, 2 + 2 * t + half, :], dg[:, k % 4, :], VR[:, k % NR, half * 512:(half + 1) * 512],
                                 start=False, stop=False, skip_group_check=True)
                    ins.then_inc(S.sem("v_free"), 1)

            for t, it0, n in peer_tiles():
                if t < 2:
                    with pe.Fori(0, n // 2) as i:
                        for j in range(2):
                            rounds(t, i * 2 + (it0 + j), j)
                else:
                    for j in range(n):
                        rounds(t, it0 + j, j)
            pe.wait_ge(*at("dve_fin", "copy"))
            for half in range(2):
                ins = mm(PS[0:TS, half, :], cst("groupsum"), M["VR"][:, 0, half * 512:(half + 1) * 512],
                         start=True, stop=True)
            ins.then_inc(*inc("pe_fin", "sum"))

        EXTRA = {"norm": norm, "cross": cross, "scross": scross, "score": score, "peer": peer}
        pe.wait_ge(*at("dve_xT", 5))
        for stage_name, arg in ORDER:
            if stage_name == "lin":
                if arg == 12:
                    pe.wait_ge(*at("dve_xT", 9))
                if arg == 20:
                    pe.wait_ge(*at("dve_gn", 3))
                elif arg == 28:
                    pe.wait_ge(*at("act_cx", "ys"))
                    pe.wait_ge(*at("dve_cx", ("o", len(CUNITS) - 1)))
                linear(arg, x_of_block(arg))
            elif stage_name in EXTRA:
                EXTRA[stage_name](arg)
            elif stage_name == "attn":
                attn()
            elif stage_name == "sgu":
                sgu()
            elif stage_name == "sattn":
                sattn()
            elif stage_name == "gnorm":
                gnorm()
            elif stage_name == "rw_pre":
                rw_pre()
            elif stage_name == "rw_kk":
                rw_kk()
            elif stage_name == "rw_vec":
                rw_vec()
            elif stage_name == "rw_tile":
                rw_tile(arg)
            elif stage_name == "rw_scan":
                rw_scan()
            elif stage_name == "rw_sample":
                rw_sample()
            elif stage_name == "rw_out":
                rw_out()

    @block.scalar
    def _(act):
        A = nc.scalar.activation
        act.wait_ge(S.sem("const_in"), 16)
        for i, (kind, t) in enumerate(NORMS0):
            m = rows_of(kind, t)
            act.wait_ge(S.sem(f"{kind}{t}_in"), 16)
            if i >= 2:
                act.wait_ge(*at("act_sq", i - 2))
            A(YT[0:m].rearrange("p a b -> p (a b)")[:, i % 2 * D:(i % 2 + 1) * D],
              M[kind][0:m, t, :], ACT.Square, accum_out=stat[0:m, i:i + 1]).then_inc(*inc("act_sq", i))
        for i, (kind, t) in enumerate(NORMS0):
            m = rows_of(kind, t)
            act.wait_ge(*at("act_sq", i))
            A(stat[0:m, 8 + i:9 + i], stat[0:m, i:i + 1], ACT.Sqrt, scale=1.0 / D,
              bias=cst("eps", m, 1)).then_inc(*inc("act_rms", i))

        def evacuate(b):
            name = BLOCKS[b][0]
            if name in ADDS:
                return
            for u in range(LAST[b - 1] if b else 0, LAST[b]):
                _, cc, nn, t = UNITS[u]
                c0 = BLOCKS[b][1] + cc
                act.wait_ge(*at("pe_lin", ("unit", u + 1)))
                src, scale = PS[:, u % 2, 0:N], 1.0
                if name == "w_in" and t is None:
                    j = c0 // P if c0 < 1536 else (c0 - 1796) // P + CU if c0 < 2052 else (c0 - 2308) // P + DQ
                    dst = hT[:, j, :]
                    scale = HD ** -0.5 if j in (BQ, BQ + 1, DQ, DQ + 1) else 1.0
                elif name == "ca_wq":
                    dst, scale = hX[:, c0 // P, :], 256 ** -0.5
                elif name == "peer_wq":
                    dst = qP(c0 // P)
                elif name == "w_in":
                    m = TILES[t][1]
                    off = {1536: TBV, 2052: TCV, 2820: TDV}[c0]
                    dst, src = hTok[0:m, t, off:off + nn], PS[0:m, u % 2, 0:nn]
                else:
                    k = u - LAST[11]
                    dst, src = stage[:, k % 2, :], PS[:, u % 2, 0:256]
                    if k >= 2:
                        act.wait_ge(S.sem(f"out_stage{k % 2}"), 16 * (k // 2))
                ins = A(dst, src, ACT.Copy, scale=scale)
                ins.then_inc(*inc("act_lin", ("unit", u + 1)))
                if 12 <= b < 20:
                    act.wait_ge(*at("act_lin", ("unit", u + 1)))
                    out = io["o_memk"][c0:c0 + P, :] if t is None else io["o_memv"][t * P:(t + 1) * P, c0:c0 + 256]
                    act.dma_start(out, stage[:, k % 2, :]).then_inc(S.sem(f"out_stage{k % 2}"), 16)

        def rw_pre():
            act.wait_ge(*at("dve_rw", "xs"))
            A(t1[0:64, 0, :], hT[0:64, 6, :], ACT.Tanh).then_inc(*inc("act_rw", "tanh"))
            A(t1[:, 1, :], hT[:, 7, :], ACT.Sigmoid).then_inc(*inc("act_rw", "sigg"))
            for step, name, bank, dst in (("sigw", "w0", 2, lw), ("siga", "a0", 4, aa)):
                act.wait_ge(*at("pe_rw", "lora_w" if bank == 2 else "lora_a"))
                for c in range(2):
                    ins = A(dst[:, c, :], PS[:, bank + c, 0:N], ACT.Sigmoid, bias=col(name, c))
                ins.then_inc(*inc("act_rw", step))
            act.wait_ge(*at("pe_rw", "lora_g"))
            A(gg[:], PS[:, 6:8, 0:N], ACT.Copy).then_inc(*inc("act_rw", "g"))

        def rw_kk():
            act.wait_ge(*at("dve_rw", "kkm"))
            A(t2, t2, ACT.Sqrt).then_inc(*inc("act_rw", "kkr"))
            act.wait_ge(*at("dve_rw", "Gx"))
            A(Pi, Gc, ACT.Exp, scale=-1.0).then_inc(*inc("act_rw", "Pi"))
            A(t1[:], t1[:], ACT.Exp).then_inc(*inc("act_rw", "Pex"))
            A(Pp, Gc, ACT.Exp).then_inc(*inc("act_rw", "P"))

        def rw_tile(t):
            m = TILES[t][1]

            def take(dst, bank, step):
                act.wait_ge(*at("pe_rw", (step, t)))
                A(quad(dst, m), PS[0:m, bank, 0:4 * m].rearrange("p (a b) -> p a b", a=4), ACT.Copy)\
                    .then_inc(*inc("act_rw", (step, t)))

            act.wait_ge(*at("pe_rw", ("tok", t)))
            if t:
                act.wait_ge(*at("pe_rw", ("mn", t - 1, 3)))
            A(TOK[0:m, 0, :], PS[0:m, 6, 0:GW], ACT.Copy)
            A(TOK[0:m, 1, :], PS[0:m, 6, GW:], ACT.Copy, scale=-1.0)
            A(TOK[0:m, 2:4, :], PS[0:m, 7, :].rearrange("p (a b) -> p a b", a=2), ACT.Copy)\
                .then_inc(*inc("act_rw", ("tok", t)))
            take("PA", 2, "P2")
            if t < 2:
                take("PTA", 3, "P2T")
                take("PB", 5, "P4")
                take("PTB", 2, "P4T")
                take("PA", 4, "P8")
                act.wait_ge(*at("pe_rw", ("R3", t)))
                take("PTA", 5, "T16")
                take("PB", 4, "Q")
            act.wait_ge(*at("pe_rw", ("wa", t)))
            A(WA[0:m], PS[0:m, 6, :].rearrange("p (a b) -> p a b", a=2), ACT.Copy).then_inc(*inc("act_rw", ("wa", t)))
            act.wait_ge(*at("pe_rw", ("u0", t)))
            A(U0[0:m], PS[0:m, 7, 0:GW], ACT.Copy)
            A(U0n[0:m], PS[0:m, 7, 0:GW], ACT.Copy, scale=-1.0).then_inc(*inc("act_rw", ("u0n", t)))
            act.wait_ge(*at("pe_rw", ("y0", t)))
            t0 = TILES[t][0]
            A(Y0[:, :, t0:t0 + m], PS[:, 4, 0:2 * m].rearrange("p (a b) -> p a b", a=2), ACT.Copy)\
                .then_inc(*inc("act_rw", ("y0", t)))

        def rw_out():
            act.wait_ge(*at("dve_rw", "yc"))
            A(t1[:], Y0[:], ACT.Square).then_inc(*inc("act_rw", "ysq"))
            act.wait_ge(*at("pe_rw", "var"))
            A(t2, PS[:, 2:4, 0:N], ACT.Sqrt, scale=1.0 / HD, bias=cst("eps")[:, 1:2]).then_inc(*inc("act_rw", "yrs"))

        def log_forget():
            act.wait_ge(*at("dve_lf", "x"))
            for step, src, dst, kw in (("abs", 0, 12, {}), ("exp", 12, 12, {"scale": -1.0}), ("ln", 12, 12, {"bias": 1.0})):
                f = {"abs": ACT.Abs, "exp": ACT.Exp, "ln": ACT.Ln}[step]
                A(soft[:, dst:dst + 12], soft[:, src:src + 12], f, **kw).then_inc(*inc("act_lf", step))
                act.wait_ge(*now("act_lf"))

        def attn():
            for s in range(NA + 1):
                if s < NA:
                    w = P * (AUNITS[s][5] + 1)
                    act.wait_ge(*at("dve_at", ("sc", s)))
                    A(SC[:, s % 2, 0:w], SC[:, s % 2, 0:w], ACT.Exp, bias=soft[:, 24 + s % 2:25 + s % 2],
                      accum_out=soft[:, 26 + s % 2:27 + s % 2]).then_inc(*inc("act_at", ("p", s)))
                if s >= 1:
                    u = s - 1
                    w = P * (AUNITS[u][5] + 1)
                    act.wait_ge(*at("pe_at", ("pt", u)))
                    if u >= 2:
                        act.wait_ge(*at("pe_at", ("o", u - 2)))
                    A(PT[:, u % 2, :, :].rearrange("p a b -> p (a b)")[:, 0:w], PS[:, 4 + u % 2, 0:w], ACT.Copy)\
                        .then_inc(*inc("act_at", ("pt", u)))

        def sgu():
            act.wait_ge(*at("dve_y", "a"))
            for t, (t0, m) in enumerate(TILES):
                A(VL[0:m, t, :], hTok[0:m, t, TCV:TCV + GW], ACT.Gelu, accum_out=soft[0:m, 32 + t:33 + t])\
                    .then_inc(*inc("act_sg", ("v", t)))
            A(hT[:, CU:CU + 2, :], hT[:, CU:CU + 2, :], ACT.Gelu).then_inc(*inc("act_sg", "u"))
            for t, (t0, m) in enumerate(TILES):
                act.wait_ge(*at("dve_sg", ("var", t)))
                A(soft[0:m, 44 + t:45 + t], soft[0:m, 38 + t:39 + t], ACT.Sqrt, scale=1.0 / GW,
                  bias=cst("eps", m, 1)).then_inc(*inc("act_sg", ("rms", t)))

        def sattn():
            for g in range(2):
                act.wait_ge(*at("dve_sa", ("sc", g)))
                A(SS[:, g, :], SS[:, g, :], ACT.Exp, bias=soft[:, 48 + g:49 + g], accum_out=soft[:, 50 + g:51 + g])\
                    .then_inc(*inc("act_sa", ("p", g)))
            for g in range(2):
                act.wait_ge(*at("pe_sa", ("pt", g)))
                A(PTs[:, g, 0:2, :].rearrange("p a b -> p (a b)"), PS[:, 4 + g, 0:2 * P], ACT.Copy)
                A(PTs[0:TS, g, 2, :], PS[0:TS, 4 + g, 2 * P:3 * P], ACT.Copy).then_inc(*inc("act_sa", ("pt", g)))

        def gnorm():
            act.wait_ge(*at("dve_y", "d"))
            for g, done in enumerate(("a", "b", "c", "d")):
                act.wait_ge(*(at("dve_sg", ("y", 2)) if done == "c" else at("dve_y", done)))
                A(M["SQ"][:, 2 * g:2 * g + 2, :], YT[:, 2 * g:2 * g + 2, :], ACT.Square).then_inc(*inc("act_gn", ("sq", g)))
            for g in range(4):
                act.wait_ge(*at("pe_gn", g))
                A(M["RS"][:, g, :], PS[:, 2 + g, 0:N], ACT.Sqrt, scale=1.0 / GW, bias=cst("eps")[:, 0:1])\
                    .then_inc(*inc("act_gn", ("rms", g)))

        def norm(i):
            for t, (t0, m) in enumerate(TILES):
                act.wait_ge(S.sem("dve_lin"), 12 * i + 10 + t)
                A(XN[0:m, t, :], X1[0:m, t, :], ACT.Square, accum_out=softx[0:m, t:t + 1]).then_inc(*inc("act_nq", (i, t)))
            for t, (t0, m) in enumerate(TILES):
                act.wait_ge(*at("act_nq", (i, t)))
                A(softx[0:m, 3 + t:4 + t], softx[0:m, t:t + 1], ACT.Sqrt, scale=1.0 / D, bias=cst("eps", m, 1))\
                    .then_inc(*inc("act_nr", (i, t)))
            for t, (t0, m) in enumerate(TILES):
                for half in range(2):
                    act.wait_ge(*at("pe_nx", (i, t, half)))
                    A(xT[:, 4 * half:4 * half + 4, t0:t0 + m],
                      PS[:, 2 + 2 * t + half, :].rearrange("p (k m) -> p k m", k=4)[:, :, 0:m], ACT.Copy)\
                        .then_inc(*inc("act_nx", (i, t, half)))

        def cross(_):
            nu = len(CUNITS)
            for s in range(nu + 1):
                if s < nu:
                    act.wait_ge(*at("dve_cx", ("mx", s)))
                    if s >= 2:
                        act.wait_ge(*at("pe_cx", ("pt", s - 2)))
                    A(SCx[:, s % 2, :], PS[:, 2 + s % 2, 0:MEM], ACT.Exp, bias=softx[:, 8 + s % 2:9 + s % 2],
                      accum_out=softx[:, 10 + s % 2:11 + s % 2]).then_inc(*inc("act_cx", ("p", s)))
                if s >= 1:
                    u = s - 1
                    act.wait_ge(*at("pe_cx", ("pt", u)))
                    if u >= 2:
                        act.wait_ge(*at("pe_cx", ("o", u - 2)))
                    A(PTx[:, u % 2, :, :].rearrange("p a b -> p (a b)"), PS[:, 4 + u % 2, 0:2 * P], ACT.Copy)\
                        .then_inc(*inc("act_cx", ("pt", u)))

        def scross(_):
            act.wait_ge(*at("dve_cx", "mxs"))
            A(SSx[:], PS[:, 2, 0:MEM], ACT.Exp, bias=softx[:, 16:17], accum_out=softx[:, 17:18])\
                .then_inc(*inc("act_cx", "p_s"))
            act.wait_ge(*at("pe_cx", "pts"))
            A(PTy[:].rearrange("p a b -> p (a b)"), PS[:, 4, 0:2 * P], ACT.Copy).then_inc(*inc("act_cx", "pts"))
            act.wait_ge(*at("pe_mr", ("v", B - 1)))
            A(YT[:, :, T:N], PS[:, 6, 0:KC * TS].rearrange("p (c m) -> p c m", c=KC), ACT.Copy)\
                .then_inc(*inc("act_cx", "ys"))

        def score(h):
            act.wait_ge(S.sem("pe_s"), h + 1)
            rows = slice(32 * (h // 2), 32 * (h // 2) + 32)
            A(SA[rows, 16 + h % 2, :, :].rearrange("p a b -> p (a b)"), PS[rows, 7, 0:2 * NK], ACT.Copy)
            A(SA[:, h:h + 9:8, :, :].rearrange("p t a b -> p t (a b)"), PS[:, 6, :].rearrange("p (t n) -> p t n", t=2),
              ACT.Copy).then_inc(S.sem("act_s"), 1 if h < 7 else NIT - 7)

        def peer(_):
            def weights(it, par):
                act.wait_ge(S.sem("topk_done"), it + 1)
                A(M["ge"][:, par, :], M["bs"][:, par, :], ACT.Exp, bias=M["gs"][:, par:par + 1],
                  accum_out=M["gs"][:, 2 + par:3 + par]).then_inc(S.sem("act_g"), 1)
                act.wait_ge(S.sem("u_free"), it * TOPK + NR + TOPK)
                A(M["gl"][:, par, :], M["act"][:, par, :], ACT.Gelu).then_inc(S.sem("act_gl"), 1)
                act.wait_ge(S.sem("dve_w"), it + 1)
                for k in range(TOPK):
                    act.wait_ge(S.sem("v_free"), it * TOPK + (k + NR - 3))
                    A(dg[:, k % 4, :], ident, ACT.Copy, scale=M["wv"][:, par, k:k + 1]).then_inc(S.sem("act_dg"), 1)

            def finish(t):
                src = PS[:, 2 + 2 * t:4 + 2 * t, :] if t < 2 else PS[0:TS, 0:2, :]
                m = TILES[t][1]
                if t < 2:
                    act.wait_ge(S.sem("v_free"), NR + P * (t + 1))
                else:
                    act.wait_ge(*at("pe_fin", "sum"))
                A(XN[0:m, t, :].rearrange("p (a b) -> p a b", a=2), src, ACT.Square,
                  accum_out=M["gs"][0:m, 4 + t:5 + t]).then_inc(*inc("act_fin", ("sq", t)))
                act.wait_ge(*now("act_fin"))
                A(M["gs"][0:m, 8 + t:9 + t], M["gs"][0:m, 4 + t:5 + t], ACT.Sqrt, scale=1.0 / D, bias=cst("eps", m, 1))\
                    .then_inc(*inc("act_fin", ("rms", t)))

            for t, it0, n in peer_tiles():
                if t < 2:
                    with act.Fori(0, n // 2) as i:
                        for j in range(2):
                            weights(i * 2 + (it0 + j), j)
                else:
                    for j in range(n):
                        finish(j)
                        weights(it0 + j, j)
            finish(2)

        EXTRA = {"norm": norm, "cross": cross, "scross": scross, "score": score, "peer": peer}
        for stage_name, arg in ORDER:
            if stage_name == "lin":
                evacuate(arg)
            elif stage_name in EXTRA:
                EXTRA[stage_name](arg)
            elif stage_name == "lf":
                log_forget()
            elif stage_name == "attn":
                attn()
            elif stage_name == "sgu":
                sgu()
            elif stage_name == "sattn":
                sattn()
            elif stage_name == "gnorm":
                gnorm()
            elif stage_name == "rw_pre":
                rw_pre()
            elif stage_name == "rw_kk":
                rw_kk()
            elif stage_name == "rw_tile":
                rw_tile(arg)
            elif stage_name == "rw_out":
                rw_out()
        nst = LAST[19] - LAST[11]
        for j in range(2):
            act.wait_ge(S.sem(f"out_stage{j}"), 16 * ((nst + 1 - j) // 2))

    @block.vector
    def _(dve):
        V = nc.vector
        for i, (kind, t) in enumerate(NORMS0):
            m = rows_of(kind, t)
            dve.wait_ge(*at("act_rms", i))
            V.reciprocal(stat[0:m, 16 + i:17 + i], stat[0:m, 8 + i:9 + i]).then_inc(*inc("dve_rstd", i))
        dve.wait_ge(S.sem("cols_in"), 16)

        def feature_major(n, src_xn, kind, t, dst, gain, done):
            m = rows_of(kind, t)
            t0 = TILES[t][0]
            for half in range(2):
                dve.wait_ge(*at("pe_xT", n + half))
                V.tensor_tensor(dst[:, 4 * half:4 * half + 4, t0:t0 + m],
                                xpose_bank(n + half).rearrange("p (k m) -> p k m", k=4)[:, :, 0:m],
                                colb(gain, 4 * half, 4 * half + 4, m), ALU.mult).then_inc(*inc(done, n + half))

        for i, (kind, t) in enumerate(NORMS0):
            m = rows_of(kind, t)
            if i == 0:
                dve.wait_ge(*at("dve_rstd", 4))
            if i >= 2:
                dve.wait_ge(*at("pe_xT", 2 * i - 3))
            V.tensor_scalar(M["xn"][0:m, i % 2, :], M[kind][0:m, t, :], stat[0:m, 16 + i:17 + i], None, ALU.mult)\
                .then_inc(*inc("dve_xn", (kind, t)))
            if i >= 1:
                kd, tt = NORMS0[i - 1]
                feature_major(2 * i - 2, None, kd, tt, M["xT"] if kd == "x" else M["xmT"], "g0" if kd == "x" else "gm", "dve_xT")
        feature_major(8, None, "xm", 1, M["xmT"], "gm", "dve_xT")

        def link(ins, sem="dve_seq", step=None):
            ins.then_inc(*inc(sem, step))
            dve.wait_ge(*now(sem))

        TT = V.tensor_tensor
        STT = V.scalar_tensor_tensor

        def rw_pre():
            pa = hT[:, 0:8, :]
            dve.wait_ge(*at("act_lin", ("unit", LAST[3])))
            dve.wait_ge(S.sem("rwp_in"), 16 * 5)
            V.tensor_copy(M["shiftc"][:, :, 0:1], pa[:, :, T - 1:T])
            link(V.tensor_copy(M["shiftc"][:, :, 1:], pa[:, :, T + Q - 1::Q]), "dve_rw", "shiftc")
            TT(dlt[:, :, 1:T], pa[:, :, 0:T - 1], pa[:, :, 1:T], ALU.subtract)
            V.tensor_scalar(dlt[:, :, 0:1], pa[:, :, 0:1], -1.0, None, ALU.mult)
            ds, ps = (a[:, :, T:N].rearrange("p c (b q) -> p c b q", q=Q) for a in (dlt, pa))
            TT(ds[:, :, :, 1:Q], ps[:, :, :, 0:Q - 1], ps[:, :, :, 1:Q], ALU.subtract)
            link(TT(ds[:, :, :, 0], M["shift"][:], ps[:, :, :, 0], ALU.subtract))
            for c in (6, 7, 2, 3, 0, 1, 4, 5):
                ins = STT(hT[:, c, :], dlt[:, c, :], col("mu", c), hT[:, c, :], ALU.mult, ALU.add)
            link(ins, "dve_rw", "xs")

        def rw_kk():
            for c in range(2):
                ins = V.tensor_scalar(kk[:, c, :], kT[:, c, :], col("kks", c), None, ALU.mult)
            link(ins)
            TT(t2, kk[:], kk[:], ALU.mult).then_inc(*inc("dve_rw", "kksq"))
            dve.wait_ge(*at("act_rw", "sigw"))
            link(V.tensor_scalar(lw[:], lw[:], -float(np.exp(-0.5)), None, ALU.mult))
            for c in range(2):
                ins = V.tensor_tensor_scan(Gc[:, c, :], cst("reset"), lw[:, c, :], 0.0, ALU.mult, ALU.add)
            link(ins)
            dve.wait_ge(*at("pe_rw", "lora_g"))
            TT(t1[:], Gc, lw[:], ALU.subtract).then_inc(*inc("dve_rw", "Gx"))
            dve.wait_ge(*at("pe_rw", "kkn"))
            V.tensor_scalar(t2, PS[:, 2:4, 0:N], 1e-24, None, ALU.max).then_inc(*inc("dve_rw", "kkm"))
            dve.wait_ge(*at("act_rw", "siga"))
            for c in range(2):
                ins = V.tensor_scalar(kp[:, c, :], aa[:, c, :], -1.0, col("ka", c), ALU.add, ALU.mult)
            link(ins)
            link(STT(kp[:], kp[:], 1.0, kT, ALU.add, ALU.mult))
            dve.wait_ge(*at("act_rw", "kkr"))
            link(V.reciprocal(t2, t2))
            link(TT(kk[:], kk[:], t2, ALU.mult))
            link(TT(bh[:], kk[:], aa[:], ALU.mult))
            for c in range(2):
                ins = STT(t2[:, c, :], rT[:, c, :], col("rk", c), kp[:, c, :], ALU.mult, ALU.mult)
            ins.then_inc(*inc("dve_rw", "bon"))

        def rw_vec():
            dve.wait_ge(*at("act_rw", "Pi"))
            TT(bh[:], bh[:], Pi, ALU.mult)
            TT(kh[:], kp[:], Pi, ALU.mult)
            dve.wait_ge(*at("act_rw", "P"))
            TT(KR[:, :, 0, :], t1[:], kk[:], ALU.mult)
            TT(KR[:, :, 1, :], Pp, rT, ALU.mult).then_inc(*inc("dve_rw", "kh"))
            dve.wait_ge(*at("pe_rw", "bonus"))
            link(TT(aa[:], PS[:, 4:6, 0:N], vT, ALU.mult), "dve_rw", "bonus")

        def rw_tile(t):
            t0, m = TILES[t]
            a1t, a3t, a2t, a4t, a16, off = tile_mats(t)
            prompt = t < 2
            R = quad("R", m)

            def masked(dst, bank, mask, step):
                dve.wait_ge(*at("pe_rw", (step, t)))
                for par in range(2):
                    ins = TT(dst[:, 2 * par:2 * par + 2, :],
                             PS[0:m, bank + par, 0:4 * m].rearrange("p (c s) -> p c s", c=2),
                             cst(mask, m).unsqueeze(1).to_broadcast([m, 2, 2 * m]), ALU.mult)
                return ins

            if t:
                dve.wait_ge(*at("pe_rw", ("y0", t - 1)))
            ins = masked(M["AB"] if prompt else M["sAB"], 2, "m_ab" if prompt else "s_ab", "x1")
            link(ins)
            TT(R, ident[0:m, 0:m].unsqueeze(1).to_broadcast([m, 4, m]),
               (M["AB"] if prompt else M["sAB"])[:, :, 0:m], ALU.subtract)
            masked(M["AK"] if prompt else M["sAK"], 4, "m_ak" if prompt else "s_ab", "x2")
            dve.wait_ge(*at("pe_rw", ("x3", t)))
            for par in range(2):
                src = PS[0:m, 6 + par, 0:2 * m].rearrange("p (c s) -> p c s", c=2)
                if prompt:
                    for half in range(2):
                        ins = TT(M["A1"][:, 2 * par:2 * par + 2, half * P:(half + 1) * P], src,
                                 cst("m_a")[:, half * P:(half + 1) * P].unsqueeze(1).to_broadcast([P, 2, P]), ALU.mult)
                else:
                    ins = TT(M["sA1"][:, 2 * par:2 * par + 2, :], src,
                             cst("s_a", m).unsqueeze(1).to_broadcast([m, 2, m]), ALU.mult)
            link(ins, "dve_rw", ("R0", t))

            def add_R(bank, step, done, op=ALU.add):
                dve.wait_ge(*at("pe_rw", (step, t)))
                link(TT(R, R, PS[0:m, bank, 0:4 * m].rearrange("p (a b) -> p a b", a=4), op), "dve_rw", (done, t))

            if prompt:
                add_R(4, "R1", "R1")
                add_R(3, "R2", "R2")
                add_R(2, "R3", "R3")
                add_R(3, "Z", "T", ALU.subtract)
            else:
                add_R(4, "R1", "T")
            dve.wait_ge(*at("pe_rw", ("yl", t)))
            TT(YLT[:, :, t0:t0 + m], KR[:, :, 1, t0:t0 + m],
               PS[:, 5, 0:2 * m].rearrange("p (a b) -> p a b", a=2), ALU.subtract).then_inc(*inc("dve_rw", ("yl", t)))
            if not prompt:
                return
            if t == 0:
                dve.wait_ge(*at("pool_rw", "zero"))
            for cc in range(4):
                bank = (2, 3, 6, 7)[cc]
                n = 4 * t + cc
                dve.wait_ge(*at("pe_rw", ("mn", t, cc)))
                for ph in (slice(0, HD), slice(HD, P)):
                    TT(MT[ph, n, :, ph], PS[ph, bank, 0:P].rearrange("p (c j) -> p c j", c=2),
                       ident[ph, ph].unsqueeze(1).to_broadcast([HD, 2, HD]), ALU.add)
                last = t0 + cc * CH + CH - 1
                ins = TT(NPr[:, n, :, :], PS[:, bank, P:2 * P].rearrange("p (c j) -> p c j", c=2),
                         Pp[:, :, last:last + 1].to_broadcast([P, 2, HD]), ALU.mult)
            link(ins, "dve_rw", ("mn", t))

        def rw_scan():
            for n in range(8):
                dve.wait_ge(*at("pe_rw", ("st", n)))
                for c in range(2):
                    last = n * CH + CH - 1
                    ins = STT(ST[:, n + 1, c, :], PS[:, 2 + n % 2, c * HD:(c + 1) * HD], Pp[:, c, last:last + 1],
                              NPr[:, n, c, :], ALU.mult, ALU.add)
                link(ins, "dve_st", n)

        def rw_sample():
            for c in range(2):
                dve.wait_ge(*at("pe_rw", ("smn", c)))
                for ph in (slice(0, HD), slice(HD, P)):
                    TT(MT[ph, :, c, ph], PS[ph, 2 + c, :].rearrange("p (b j) -> p b j", b=B),
                       ident[ph, ph].unsqueeze(1).to_broadcast([HD, B, HD]), ALU.add)
                pl = Pp[:, c, T + Q - 1::Q].unsqueeze(2).to_broadcast([P, B, HD])
                TT(NPr[:, :, c, :], PS[:, 6 + c, :].rearrange("p (b j) -> p b j", b=B), pl, ALU.mult)\
                    .then_inc(*inc("dve_rw", ("smn", c)))
            for c in range(2):
                dve.wait_ge(*at("pe_rw", ("ss", c)))
                tmp = M["PTB"][:].rearrange("p a b -> p (a b)").rearrange("p (b j) -> p b j", b=B)
                pl = Pp[:, c, T + Q - 1::Q].unsqueeze(2).to_broadcast([P, B, HD])
                link(TT(tmp, PS[:, 4 + c, :].rearrange("p (b j) -> p b j", b=B), pl, ALU.mult))
                link(TT(NPr[:, :, c, :], NPr[:, :, c, :], tmp, ALU.add), "dve_rw", "swkv" if c else "swkv0")

        def rw_out():
            dve.wait_ge(*at("act_rw", ("y0", 2)))
            dve.wait_ge(*at("pe_rw", "yst"))
            for par in range(2):
                ph = slice(par * HD, par * HD + HD)
                TT(Y0[ph, :, 0:T], Y0[ph, :, 0:T], PS[ph, 2 + par, :].rearrange("p (c t) -> p c t", c=2), ALU.add)
            dve.wait_ge(*at("pe_rw", "yss"))
            for par in range(2):
                ph = slice(par * HD, par * HD + HD)
                ins = TT(Y0[ph, :, T:N], Y0[ph, :, T:N],
                         PS[ph, 6 + par, 0:2 * TS].rearrange("p (c t) -> p c t", c=2), ALU.add)
            link(ins, "dve_rw", "y")
            dve.wait_ge(*at("pe_rw", "mean"))
            link(STT(Y0[:], PS[:, 4:6, 0:N], -1.0 / HD, Y0[:], ALU.mult, ALU.add), "dve_rw", "yc")
            dve.wait_ge(*at("act_rw", "yrs"))
            link(V.reciprocal(t2, t2))
            link(TT(Y0[:], Y0[:], t2, ALU.mult))
            for c in range(2):
                ins = V.tensor_scalar(Y0[:, c, :], Y0[:, c, :], col("lnw", c), col("lnb", c), ALU.mult, ALU.add)
            link(ins)
            link(TT(Y0[:], Y0[:], aa[:], ALU.add))
            link(TT(YT[:, 0:2, :], Y0[:], gg[:], ALU.mult), "dve_y", "a")

        def log_forget():
            dve.wait_ge(*at("act_lin", ("unit", LAST[6])))
            dve.wait_ge(S.sem("rows_in"), 16 * 3)
            x = soft[:, 0:12].rearrange("p (t h) -> p t h", h=4)
            link(V.memset(soft[:, 0:12], 0.0))
            bf = M["rows"][:, 512:516]
            TT(x[:, 0:2, :], hTok[:, 0:2, TLF:TLF + 4], bf.unsqueeze(1).to_broadcast([P, 2, 4]), ALU.add)
            link(TT(x[0:TS, 2, :], hTok[0:TS, 2, TLF:TLF + 4], bf[0:TS], ALU.add), "dve_lf", "x")
            dve.wait_ge(*at("act_lf", "ln"))
            STT(lf[:].rearrange("p t h -> p (t h)"), soft[:, 0:12], 0.0, soft[:, 12:24], ALU.min, ALU.subtract)\
                .then_inc(*inc("dve_lf", "lf"))
            dve.wait_ge(*now("dve_lf"))

        def attn():
            for s in range(NA + 2):
                if s < NA:
                    qc, _, _, _, h, qb = AUNITS[s]
                    w = P * (qb + 1)
                    if qc == BQ:
                        if s >= 2:
                            dve.wait_ge(*at("pe_at", ("sc", s - 2)))
                        if qb == 0:
                            ins = V.tensor_scalar(LFU[:, s % 2, 0, :], upinc, lf[:, 0, h:h + 1], None, ALU.mult)
                        else:
                            V.tensor_scalar(LFU[:, s % 2, 0, :], ones, lf[:, 0, h:h + 1], None, ALU.mult)
                            ins = V.tensor_scalar(LFU[:, s % 2, 1, :], upinc, lf[:, 1, h:h + 1], None, ALU.mult)
                        ins.then_inc(*inc("dve_at", ("lfu", s)))
                        bias = cst("caus")[:, 256 - w:256]
                    else:
                        bias = cst(f"d_bias{h}{qb}")
                    dve.wait_ge(*at("pe_at", ("sc", s)))
                    if s >= 2:
                        dve.wait_ge(*at("pe_at", ("pt", s - 2)))
                    link(TT(SC[:, s % 2, 0:w], PS[:, 2 + s % 2, 0:w], bias, ALU.add))
                    link(V.tensor_reduce(soft[:, 24 + s % 2:25 + s % 2], SC[:, s % 2, 0:w], X, ALU.max, negate=True),
                         "dve_at", ("sc", s))
                if 1 <= s <= NA:
                    u = s - 1
                    w = P * (AUNITS[u][5] + 1)
                    dve.wait_ge(*at("act_at", ("p", u)))
                    link(V.reciprocal(soft[:, 28 + u % 2:29 + u % 2], soft[:, 26 + u % 2:27 + u % 2]))
                    V.tensor_scalar(SC[:, u % 2, 0:w], SC[:, u % 2, 0:w], soft[:, 28 + u % 2:29 + u % 2], None, ALU.mult)\
                        .then_inc(*inc("dve_at", ("p", u)))
                if s >= 2:
                    u = s - 2
                    _, _, _, yc, h, qb = AUNITS[u]
                    ph = slice(HD * (h % 2), HD * (h % 2) + HD)
                    dve.wait_ge(*at("pe_at", ("o", u)))
                    V.tensor_copy(YT[ph, yc + h // 2, qb * P:(qb + 1) * P], PS[ph, 6 + u % 2, 0:P])\
                        .then_inc(*inc("dve_at", ("o", u)))

        def sgu():
            dve.wait_ge(S.sem("sgu_in"), 16 * 3)
            for h in range(4):
                V.tensor_tensor(M["wm"][:, h, :], M["wm"][:, h, :], upinc, ALU.mult)
            link(TT(M["wm4"][:], M["wm4"][:], cst("s_ab", TS)[:, TS:].unsqueeze(1).to_broadcast([TS, 4, TS]), ALU.mult))
            for t, (t0, m) in enumerate(TILES):
                v = VL[0:m, t, :]
                junk = M["sg"][0:m].rearrange("p a b -> p (a b)")
                dve.wait_ge(*at("act_sg", ("v", t)))
                link(V.tensor_scalar(soft[0:m, 36:37], soft[0:m, 32 + t:33 + t], 1.0 / GW, None, ALU.mult))
                link(V.tensor_scalar(v, v, soft[0:m, 36:37], None, ALU.subtract))
                link(V.tensor_tensor_reduce(out=junk, in0=v, in1=v, scale=1.0, scalar=0.0, op0=ALU.mult, op1=ALU.add,
                                            accum_out=soft[0:m, 38 + t:39 + t]), "dve_sg", ("var", t))
                dve.wait_ge(*at("act_sg", ("rms", t)))
                link(V.reciprocal(soft[0:m, 42:43], soft[0:m, 44 + t:45 + t]))
                link(STT(v, v, soft[0:m, 42:43], M["rows"][0:m, 0:GW], ALU.mult, ALU.mult))
                link(TT(v, v, M["rows"][0:m, GW:2 * GW], ALU.add), "dve_sg", ("v", t))
            dve.wait_ge(*at("act_sg", "u"))
            for t, (t0, m) in enumerate(TILES):
                dve.wait_ge(*at("pe_sg", t))
                mix = PS[:, 2 + t % 2, 0:2 * m].rearrange("p (c t) -> p c t", c=2)
                if t < 2:
                    link(TT(M["sg"][:, :, 0:m], mix, M["bsr"][:], ALU.add))
                else:
                    for c in range(2):
                        ins = TT(M["sg"][:, c, 0:m].rearrange("p (b q) -> p b q", q=Q),
                                 mix[:, c, :].rearrange("p (b q) -> p b q", q=Q),
                                 M["bsr"][:, c, 0:Q].unsqueeze(1).to_broadcast([P, B, Q]), ALU.add)
                    link(ins)
                link(TT(YT[:, 4:6, t0:t0 + m], M["sg"][:, :, 0:m], hT[:, CU:CU + 2, t0:t0 + m], ALU.mult),
                     "dve_sg", ("y", t))

        def sattn():
            dve.wait_ge(S.sem("pt_in"), 16)
            link(V.tensor_scalar(M["idx"][:], M["pt"][:], float(PAGE), cst("prow"), ALU.mult, ALU.add), "dve_sa", "idx")
            dve.wait_ge(S.sem("glf_in"), 16 * 16)
            lfg = M["lfg"][:].rearrange("p (b g) h -> p b g h", g=2)
            for pg in range(2):
                V.tensor_copy(M["LFP"][:, pg, :].rearrange("p (b h t) -> p b h t", b=B, h=4),
                              lfg[:, :, pg, :].unsqueeze(3).to_broadcast([P, B, 4, Q]))
            for b in range(B):
                ins = TT(M["LFN"][:, b * 16:(b + 1) * 16].rearrange("p (h t) -> p h t", h=4),
                         lf[0:TS, 2, :].unsqueeze(2).to_broadcast([TS, 4, Q]),
                         cst("lf_new_l", TS)[:, b * 16:(b + 1) * 16].rearrange("p (h t) -> p h t", h=4), ALU.mult)
            link(ins, "dve_sa", "lfn")
            for g, bias in enumerate(("sb_bias", "sd_bias")):
                dve.wait_ge(*at("pe_sa", ("sc", g)))
                link(TT(SS[:, g, :], PS[:, 2 + g, 0:PAST + TS], cst(bias), ALU.add))
                link(V.tensor_reduce(soft[:, 48 + g:49 + g], SS[:, g, :], X, ALU.max, negate=True), "dve_sa", ("sc", g))
            for g in range(2):
                dve.wait_ge(*at("act_sa", ("p", g)))
                link(V.reciprocal(soft[:, 52 + g:53 + g], soft[:, 50 + g:51 + g]))
                V.tensor_scalar(SS[:, g, :], SS[:, g, :], soft[:, 52 + g:53 + g], None, ALU.mult)\
                    .then_inc(*inc("dve_sa", ("p", g)))
            for g, yc in enumerate((2, 6)):
                dve.wait_ge(*at("pe_sa", ("o", g)))
                for par in range(2):
                    ph = slice(HD * par, HD * par + HD)
                    for c in range(2):
                        ins = V.tensor_copy(YT[ph, yc + c, T:N].rearrange("p (b q) -> p b q", q=Q),
                                            PS[ph, 6 + g, c * 64:(c + 1) * 64].rearrange("p (b x) -> p b x", b=B)
                                            [:, :, Q * par:Q * par + Q])
                link(ins, "dve_y", "bd"[g])

        def gnorm():
            for g in range(4):
                dve.wait_ge(*at("act_gn", ("rms", g)))
                link(V.reciprocal(M["RS"][:, g, :], M["RS"][:, g, :]))
                for j in range(2):
                    k = 2 * g + j
                    ins = STT(YT[:, k, :], YT[:, k, :], col("gout", k), M["RS"][:, g, :], ALU.mult, ALU.mult)
                ins.then_inc(*inc("dve_gn", g))

        def linear_add(b):
            if BLOCKS[b][0] not in ADDS:
                return
            if b == 20:
                dve.wait_ge(S.sem("X1_in"), 16 * 3)
            for u in range(LAST[b - 1], LAST[b]):
                _, cc, nn, t = UNITS[u]
                m, c0 = TILES[t][1], BLOCKS[b][1]
                dve.wait_ge(*at("pe_lin", ("unit", u + 1)))
                x = X1[0:m, t, c0:c0 + nn]
                TT(x, x, PS[0:m, u % 2, 0:nn], ALU.add).then_inc(S.sem("dve_lin"), 1)

        def norm(i):
            if i == 0:
                dve.wait_ge(S.sem("gr_in"), 16 * 3)
            for t, (t0, m) in enumerate(TILES):
                dve.wait_ge(*at("act_nr", (i, t)))
                link(V.reciprocal(softx[0:m, 24 + t:25 + t], softx[0:m, 3 + t:4 + t]))
                STT(XN[0:m, t, :], X1[0:m, t, :], softx[0:m, 24 + t:25 + t], gr[0:m, i, :], ALU.mult, ALU.mult)\
                    .then_inc(*inc("dve_nx", (i, t)))

        def cross(_):
            nu = len(CUNITS)
            for s in range(nu + 2):
                if s < nu:
                    dve.wait_ge(*at("pe_cx", ("sc", s)))
                    V.tensor_reduce(softx[:, 8 + s % 2:9 + s % 2], PS[:, 2 + s % 2, 0:MEM], X, ALU.max, negate=True)\
                        .then_inc(*inc("dve_cx", ("mx", s)))
                if 1 <= s <= nu:
                    u = s - 1
                    dve.wait_ge(*at("act_cx", ("p", u)))
                    link(V.reciprocal(softx[:, 12 + u % 2:13 + u % 2], softx[:, 10 + u % 2:11 + u % 2]))
                    V.tensor_scalar(SCx[:, u % 2, :], SCx[:, u % 2, :], softx[:, 12 + u % 2:13 + u % 2], None, ALU.mult)\
                        .then_inc(*inc("dve_cx", ("p", u)))
                if s >= 2:
                    u = s - 2
                    h, qb = CUNITS[u]
                    dve.wait_ge(*at("pe_cx", ("o", u)))
                    V.tensor_copy(YT[:, 2 * h:2 * h + 2, qb * P:(qb + 1) * P],
                                  PS[:, 6 + u % 2, 0:2 * P].rearrange("p (c q) -> p c q", c=2))\
                        .then_inc(*inc("dve_cx", ("o", u)))

        def scross(_):
            dve.wait_ge(*at("pe_mr", ("k", B - 1)))
            V.tensor_reduce(softx[:, 16:17], PS[:, 2, 0:MEM], X, ALU.max, negate=True).then_inc(*inc("dve_cx", "mxs"))
            dve.wait_ge(*at("act_cx", "p_s"))
            link(V.reciprocal(softx[:, 18:19], softx[:, 17:18]))
            V.tensor_scalar(SSx[:], SSx[:], softx[:, 18:19], None, ALU.mult).then_inc(*inc("dve_cx", "ps"))

        def peer(_):
            cur, cur2, cand, cand2, eq, ts, ti, tif, bj, bji, bjf, ef, idxu, idxv, bs, gs = (
                M[k] for k in ("cur", "cur2", "cand", "cand2", "eq", "ts", "ti", "tif", "bj", "bji", "bjf", "ef",
                               "idxu", "idxv", "bs", "gs"))
            linked = dve.alloc_register("linked")
            dve.wait_ge(*at("act_cx", "ys"))
            V.memset(gs[:], 0.0).then_inc(S.sem("u_free"), NR)

            def topk(n, par, then):
                dve.wait_ge(S.sem("act_s"), n + 1)
                then(V.tensor_copy(cur[:].rearrange("p a b -> p (a b)"),
                                   SA[:].rearrange("p n a b -> p (n a b)")[:, bass.ds(n * 2 * NK, 2 * NK)]))
                for c in range(2):
                    ins = V.max(ts[:, c, 0:8], cur[:, c, :])
                then(ins)
                for c in range(2):
                    V.max_index(ti[:, c, 0:8], ts[:, c, 0:8], cur[:, c, :])
                    ins = V.match_replace(cur2[:, c, :], ts[:, c, 0:8], cur[:, c, :], -3e38)
                then(ins)
                for c in range(2):
                    ins = V.max(ts[:, c, 8:16], cur2[:, c, :])
                then(ins)
                for c in range(2):
                    V.max_index(ti[:, c, 8:16], ts[:, c, 8:16], cur2[:, c, :])
                then(TT(cand[:], ts[:, 0, :].unsqueeze(2).to_broadcast([P, TOPK, TOPK]),
                        ts[:, 1, :].unsqueeze(1).to_broadcast([P, TOPK, TOPK]), ALU.add))
                V.tensor_copy(tif[:], ti[:])
                flat, flat2 = (a[:].rearrange("p a b -> p (a b)") for a in (cand, cand2))
                then(V.max(bs[:, par, 0:8], flat))
                V.max_index(bj[:, 0, 0:8], bs[:, par, 0:8], flat)
                then(V.match_replace(flat2, bs[:, par, 0:8], flat, -3e38))
                then(V.max(bs[:, par, 8:16], flat2))
                then(V.max_index(bj[:, 0, 8:16], bs[:, par, 8:16], flat2))
                V.tensor_scalar(bji[:, 0, :], bj[:, 0, :], 4, None, ALU.logical_shift_right)
                then(V.tensor_scalar(bji[:, 1, :], bj[:, 0, :], 15, None, ALU.bitwise_and))
                then(V.tensor_copy(bjf[:], bji[:]))
                for c in range(2):
                    ins = TT(eq[:, c, :, :], bjf[:, c, :].unsqueeze(2).to_broadcast([P, TOPK, TOPK]),
                             cst("iota16").unsqueeze(1).to_broadcast([P, TOPK, TOPK]), ALU.is_equal)
                then(ins)
                for c in range(2):
                    ins = TT(eq[:, c, :, :], eq[:, c, :, :], tif[:, c, :].unsqueeze(1).to_broadcast([P, TOPK, TOPK]), ALU.mult)
                then(ins)
                then(V.tensor_reduce(ef[:], eq[:], X, ALU.add))
                V.tensor_scalar(gs[:, par:par + 1], bs[:, par, 0:1], -1.0, None, ALU.mult)
                STT(idxu[:, par, :], ef[:, 0, :], float(NK), ef[:, 1, :], ALU.mult, ALU.add)\
                    .then_inc(S.sem("topk_done"), 1)

            def body(it, par, x, last=False):
                local = [0]

                def then(ins):
                    local[0] += 1
                    ins.then_inc(S.sem("dve_loop"), 1)
                    dve.reg_mov(linked, it * LINKS + local[0])
                    dve.wait_ge(S.sem("keys_in"), 16)
                    dve.wait_ge(S.sem("dve_loop"), linked)

                if last:
                    then = link
                for k in range(TOPK):
                    dve.wait_ge(S.sem(f"u{k % NR}_in"), (it * (TOPK // NR) + k // NR + 1) * 16)
                    V.tensor_tensor_reduce(out=UR[:, k % NR, :], in0=UR[:, k % NR, :], in1=x, scale=1.0, scalar=0.0,
                                           op0=ALU.mult, op1=ALU.add, accum_out=M["act"][:, par, k:k + 1])\
                        .then_inc(S.sem("u_free"), 1)
                dve.wait_ge(S.sem("v_free"), it * TOPK + 1)
                V.tensor_copy(idxv[:, par, :], idxu[:, par, :])
                dve.wait_ge(S.sem("act_gl"), it + 1)
                V.reciprocal(gs[:, 12 + par:13 + par], gs[:, 2 + par:3 + par])
                then(TT(M["wv"][:, par, :], M["ge"][:, par, :], M["gl"][:, par, :], ALU.mult))
                V.tensor_scalar(M["wv"][:, par, :], M["wv"][:, par, :], gs[:, 12 + par:13 + par], None, ALU.mult)\
                    .then_inc(S.sem("dve_w"), 1)
                if not last:
                    topk(it + 2, par, then)
                    assert local[0] == LINKS, local[0]

            def finish(t):
                m = TILES[t][1]
                dve.wait_ge(*at("act_fin", ("rms", t)))
                src = PS[:, 2 + 2 * t:4 + 2 * t, :] if t < 2 else PS[0:TS, 0:2, :]
                link(V.reciprocal(gs[0:m, 14:15], gs[0:m, 8 + t:9 + t]))
                ins = STT(X1[0:m, t, :].rearrange("p (a b) -> p a b", a=2), src, gs[0:m, 14:15],
                          gr[0:m, 2, :].rearrange("p (a b) -> p a b", a=2), ALU.mult, ALU.mult)
                ins.then_inc(*inc("dve_fin", ("y", t)))
                dve.wait_ge(*now("dve_fin"))

            dve.wait_ge(*now("dve_seq"))
            for n in range(2):
                topk(n, n, link)
            for t, it0, n in peer_tiles():
                if t < 2:
                    with dve.Fori(0, n // 2) as i:
                        for j in range(2):
                            body(i * 2 + (it0 + j), j, XN[:, t, :])
                else:
                    dve.wait_ge(S.sem("xs_in"), 16 * 4)
                    for j in range(n):
                        body(it0 + j, j, gr[:, 0, :], last=True)
                        finish(j)
            dve.wait_ge(S.sem("v_free"), NR + NIT * TOPK)
            V.tensor_copy(VR[:, 0, :].rearrange("p (a b) -> p a b", a=2), PS[:, 6:8, :]).then_inc(*inc("dve_fin", "copy"))
            finish(2)

        EXTRA = {"norm": norm, "cross": cross, "scross": scross, "peer": peer, "lin": linear_add}
        for stage_name, arg in ORDER:
            if stage_name in EXTRA:
                EXTRA[stage_name](arg)
            elif stage_name == "lf":
                log_forget()
            elif stage_name == "attn":
                attn()
            elif stage_name == "sgu":
                sgu()
            elif stage_name == "sattn":
                sattn()
            elif stage_name == "gnorm":
                gnorm()
            elif stage_name == "rw_pre":
                rw_pre()
            elif stage_name == "rw_kk":
                rw_kk()
            elif stage_name == "rw_vec":
                rw_vec()
            elif stage_name == "rw_tile":
                rw_tile(arg)
            elif stage_name == "rw_scan":
                rw_scan()
            elif stage_name == "rw_sample":
                rw_sample()
            elif stage_name == "rw_out":
                rw_out()

    @block.gpsimd
    def _(pool):
        G = nc.gpsimd
        pool.wait_ge(*at("dve_xn", ("xm", 1)))
        pool.wait_ge(*at("act_lin", ("unit", 1)))
        G.memset(MT[:], 0.0)
        G.memset(ST[:, 0, :, :], 0.0).then_inc(*inc("pool_rw", "zero"))
        for c in range(2):
            pool.wait_ge(*at("act_rw", ("u0n", 2)))
            if c:
                pool.wait_ge(*at("pe_rw", ("smn", c - 1)))
            for dst, src in ((XB, TOK[0:TS, 1, c * P:(c + 1) * P]), (XV, TOK[0:TS, 3, c * P:(c + 1) * P]),
                             (XU, U0[0:TS, c * P:(c + 1) * P])):
                ins = G.tensor_tensor(dst, src.unsqueeze(1).to_broadcast([TS, B, P]),
                                      cst("batch", TS).unsqueeze(2).to_broadcast([TS, B, P]), ALU.mult)
            ins.then_inc(*inc("pool_rw", ("x", c)))

        pool.wait_ge(*at("dve_y", "a"))
        G.memset(QB[:], 0.0).then_inc(*inc("pool_sa", "z"))
        pool.wait_ge(*now("pool_sa"))
        for g, qc in enumerate((BQ, DQ)):
            for h in range(4):
                ph = slice(HD * (h % 2), HD * (h % 2) + HD)
                for par in range(2):
                    a = par * 16 + h * Q
                    ins = G.tensor_copy(QB[ph, g, par::2, h // 2, a:a + Q],
                                        hT[ph, qc + h // 2, T:N].rearrange("p (b q) -> p b q", q=Q)[:, par::2, :])
        ins.then_inc(*inc("pool_sa", "q"))
        pool.wait_ge(*now("pool_sa"))
        pool.wait_ge(*at("dve_sa", "idx"))
        for name, dst, pool_rows, width in (("glf_in", M["lfg"][:], "lf_pool", 4), ("gath_in", KTB[:], "k_pool", 256),
                                            ("gv_in", VB[:], "v_pool", 256)):
            for i in range(B * 2):
                b, pg = divmod(i, 2)
                d = dst[:, i, :] if width == 4 else \
                    (dst[:, b, pg, :, :].rearrange("p a b -> p (a b)") if name == "gath_in" else dst[:, b, pg, :])
                G.indirect_dma_start(d, None, io[pool_rows], bass.IndirectOffsetOnAxis(ap=M["idx"][:, i:i + 1], axis=0))\
                    .then_inc(S.sem(name), 16)

        pool.wait_ge(*at("dve_gn", 3))
        G.memset(QX[:], 0.0).then_inc(*inc("pool_cx", "z"))
        pool.wait_ge(*now("pool_cx"))
        pool.wait_ge(*at("act_lin", ("unit", LAST[27])))
        for c in range(KC):
            for par in range(2):
                a = par * 16 + c // 2 * Q
                ins = G.tensor_copy(QX[:, par::2, c, a:a + Q], hX[:, c, T:N].rearrange("p (b q) -> p b q", q=Q)[:, par::2, :])
        ins.then_inc(*inc("pool_cx", "q"))

        pool.wait_ge(*at("act_cx", "ys"))
        free_slots = pool.alloc_register("free_slots")

        def gather(name, it, k, par):
            ring, idx = (UR, M["idxu"]) if name == "u" else (VR, M["idxv"])
            pool.reg_mov(free_slots, it * TOPK + (k + 1))
            pool.wait_ge(S.sem("keys_in"), 16)
            pool.wait_ge(S.sem(f"{name}_free"), free_slots)
            G.indirect_dma_start(ring[:, k % NR, :], None, io[f"peer_{name}"],
                                 bass.IndirectOffsetOnAxis(ap=idx[:, par, k:k + 1], axis=0))\
                .then_inc(S.sem(f"{name}{k % NR}_in"), 16)

        def gathers(it, par, left=2):
            for k in range(TOPK):
                if k + AHEAD == TOPK and left == 2:
                    pool.wait_ge(S.sem("topk_done"), it + 3)
                if k + AHEAD < TOPK and left >= 1:
                    gather("u", it + 1, k + AHEAD, 1 - par)
                elif k + AHEAD >= TOPK and left == 2:
                    gather("u", it + 2, k + AHEAD - TOPK, par)
                if k == 0:
                    pool.wait_ge(S.sem("dve_w"), it + 1)
                gather("v", it, k, par)

        for n in range(TOPK + AHEAD):
            if n % TOPK == 0:
                pool.wait_ge(S.sem("topk_done"), n // TOPK + 1)
            gather("u", n // TOPK, n % TOPK, n // TOPK)
        with pool.Fori(0, (NIT - 2) // 2) as i:
            for j in range(2):
                gathers(i * 2 + j, j)
        for j in range(2):
            gathers(NIT - 2 + j, j, left=1 - j)


def feature_columns(a):
    return np.ascontiguousarray(np.asarray(a, np.float32).reshape(-1, P).T)


def kernel(**inputs):
    import concourse.bacc as bacc
    from concourse.bass_utils import run_bass_kernel_spmd

    f = {k: np.asarray(v) for k, v in inputs.items()}
    ins, outs = {}, {}
    ins["x_all"] = np.concatenate([f["x_prompt"].reshape(T, D), f["x_sample"].reshape(TS, D)])
    ins["mem_prompt"] = f["mem_prompt"].reshape(MEM, D)
    ins["const"] = CONST
    params = {"g0": f["norm_g"][0, 0], "g1": f["norm_g"][0, 1], "g2": f["norm_g"][0, 2], "gm": f["ca_mem_g"],
              "gout": f["out_g"], "mu": f["a_mu"], "w0": f["a_w0"], "a0": f["a_a0"], "kks": f["a_kk"],
              "ka": f["a_ka"], "rk": f["a_rk"], "lnw": f["a_lnw"], "lnb": f["a_lnb"]}
    ins["cols"] = np.hstack([feature_columns(params[k]) for k in COLS])
    for k in ("w_in", "ca_wk", "ca_wv", "w_out", "ca_wq", "ca_wo", "peer_wq"):
        ins[k] = f[k][0]
    ins["a_w2"], ins["a_a2"], ins["a_g2"] = f["a_w2"][0], f["a_a2"][0], f["a_g2"][0]
    ins["shift"] = f["state_a_shift"][0].reshape(B, KC, P).transpose(2, 1, 0)
    ins["s0T"] = f["state_a_wkv"][0].reshape(B, 2, 2, HD, HD).transpose(2, 4, 0, 1, 3).reshape(P, B, 2, HD)
    ins["c_lng"], ins["c_lnb"], ins["b_f"] = f["c_lng"], f["c_lnb"], f["b_f"]
    ws = f["c_ws"][0].transpose(2, 0, 1)
    ins["wsT"] = ws
    ins["ws4"] = np.tile(ws[:Q, :, :Q], (B, 1, B))
    ins["bsr"] = np.repeat(f["c_bs"][0].reshape(2, 2, P).transpose(1, 0, 2), HD, axis=0)
    ins["page_table"] = f["page_table"].reshape(1, -1)
    n_phys = f["cache_b_k"].shape[1]
    ins["k_pool"] = f["cache_b_k"][0].reshape(n_phys, P, 2, P).transpose(0, 3, 2, 1).reshape(n_phys * P, 2 * P)
    ins["v_pool"] = f["cache_b_v"][0].reshape(n_phys * P, GW)
    ins["lf_pool"] = f["cache_b_logf"][0].reshape(n_phys * P, 4)
    ins["dkT"] = f["cache_d_k"][0].reshape(B, PAST, 2, P).transpose(3, 0, 2, 1)
    ins["dv"] = f["cache_d_v"][0].reshape(B, 2, P, GW).transpose(2, 0, 1, 3)
    ins["gains"] = np.stack([f["norm_g"][0, 1], f["norm_g"][0, 2], f["final_g"]])
    ins["mk_s"] = f["cache_mem_k"][0].reshape(B, MEM, KC, P).transpose(0, 3, 2, 1).reshape(B, P, KC * MEM)
    ins["mv_s"] = f["cache_mem_v"][0].reshape(B, 2, P, D).transpose(0, 2, 1, 3).reshape(B, P, 2 * D)
    ins["keysT"] = f["peer_keys"][0].transpose(3, 0, 1, 2).reshape(P, 16, NK)
    ins["peer_u"], ins["peer_v"] = f["peer_u"][0], f["peer_v"][0]
    outs["o_y"] = (N, D)
    outs["o_lf"] = (P, 3, 4)
    outs["o_cv"] = (TS, GW)
    outs["o_shift"] = (P, KC, 1 + B)
    outs["o_pwkv"] = (P, 2, HD)
    outs["o_swkv"] = (P, B, 2, HD)
    outs["o_bk"] = (P, 2, N)
    outs["o_dk"] = (P, 2, N)
    outs["o_tok0"] = (P, TW)
    outs["o_tok1"] = (P, TW)
    outs["o_tok2"] = (TS, TW)
    outs["o_memk"] = (D, MEM)
    outs["o_memv"] = (MEM, D)

    def declare(nc):
        io = {}
        for k, a in ins.items():
            io[k] = nc.dram_tensor(k, a.shape, mybir.dt.from_np(a.dtype), kind="ExternalInput").ap()
        for k, s in outs.items():
            io[k] = nc.dram_tensor(k, s, F32, kind="ExternalOutput").ap()
        return io

    steps = None
    for _ in range(2):
        nc = bacc.Bacc("TRN2", target_bir_lowering=False, num_devices=1)
        steps = build(nc, declare(nc), steps)
    arrays = {k: np.ascontiguousarray(a) for k, a in ins.items()}
    r = run_bass_kernel_spmd(nc, [arrays], core_ids=[0]).results[0]
    fm = {k: r[k].transpose(2, 1, 0).reshape(N, 4, HD) for k in ("o_bk", "o_dk")}
    tok = np.concatenate([r[f"o_tok{t}"] for t in range(3)])
    bv, dv = tok[:, TBV:TBV + GW].reshape(N, 4, HD), tok[:, TDV:TDV + GW].reshape(N, 4, HD)
    lf = r["o_lf"].transpose(1, 0, 2).reshape(3 * P, 4)
    shift = r["o_shift"].transpose(2, 1, 0).reshape(1 + B, D)
    pwkv = r["o_pwkv"].reshape(2, HD, 2, HD).transpose(2, 0, 3, 1).reshape(1, 1, 4, HD, HD)
    swkv = r["o_swkv"].reshape(2, HD, B, 2, HD).transpose(2, 3, 0, 4, 1).reshape(1, B, 4, HD, HD)
    p = lambda a: a[:T].reshape(1, 1, T, *a.shape[1:])
    s = lambda a: a[T:N].reshape(1, B, Q, *a.shape[1:])
    out = (r["o_y"][:T].reshape(1, T, D), r["o_y"][T:].reshape(B, Q, D),
           pwkv, shift[:1].reshape(1, 1, D), p(fm["o_bk"]), p(bv), p(lf), p(fm["o_dk"]), p(dv),
           r["o_memk"].T.reshape(1, 1, MEM, 4, 256), r["o_memv"].reshape(1, 1, MEM, 4, 256),
           swkv, shift[1:].reshape(1, B, D), s(fm["o_bk"]), s(bv), s(lf), r["o_cv"].reshape(1, B, Q, GW),
           s(fm["o_dk"]), s(dv))
    return tuple(np.ascontiguousarray(a) for a in out)
```

```python
from contextlib import ExitStack

import concourse.bass as bass
import numpy as np
from concourse import mybir

ALU = mybir.AluOpType
ACT = mybir.ActivationFunctionType
F32 = mybir.dt.float32
I32 = mybir.dt.int32
U32 = mybir.dt.uint32
X = mybir.AxisListType.X

P = 128
D = 1024
KC = D // P
T = 256
B, Q = 8, 4
TS = B * Q
N = T + TS
TILES = [(0, P), (P, P), (T, TS)]
HD = 64
PAST = 256
PAGE = 128
MEM = 256
GW = 256
CH = 32
HEADS, TOPK, NK = 8, 16, 128
NEG = -1e30
EPS, GN_EPS = 1e-6, 64e-5
DIL = ((128, 1), (512, 4), (2048, 16))

BLOCKS = (
    [("w_in", 256 * i, 256, "F") for i in range(6)]
    + [("w_in", 1536, 260, "T"), ("w_in", 1796, 256, "F"), ("w_in", 2052, 256, "T"),
       ("w_in", 2308, 256, "F"), ("w_in", 2564, 256, "F"), ("w_in", 2820, 256, "T")]
    + [("ca_wk", 256 * i, 256, "F") for i in range(4)]
    + [("ca_wv", 256 * i, 256, "T") for i in range(4)]
    + [("w_out", 256 * i, 256, "T") for i in range(4)]
    + [("ca_wq", 256 * i, 256, "F") for i in range(4)]
    + [("ca_wo", 256 * i, 256, "T") for i in range(4)]
    + [("peer_wq", 256 * i, 256, "F") for i in range(8)]
)
RING = 3
NR = 8
GAP = 3
AHEAD = 4
NIT = 18
LINKS = 15
WCOLS = 260
BQ, BK, CU, DQ, DK = 8, 10, 12, 14, 16
TBV, TLF, TCV, TDV, TW = 0, 256, 260, 516, 772


def linear_units():
    units, last = [], []
    for b, (name, c0, n, form) in enumerate(BLOCKS):
        if form == "F":
            units += [(b, 128 * j, 128, None) for j in range(2)]
        else:
            units += [(b, 0, n, t) for t in range(2 if name == "ca_wv" else 3)]
        last.append(len(units))
    return units, last


UNITS, LAST = linear_units()
ADDS = ("w_out", "ca_wo")
EVAC = []
for _u in UNITS:
    _v = BLOCKS[_u[0]][0] in ADDS
    EVAC.append((_v, 1 + sum(e[0] == _v for e in EVAC)))


def constants():
    i = np.arange(P)
    r, c = i[:, None], i[None, :]
    cols = {}
    cols["ident"] = (r == c) * 1.0
    cols["eps"] = np.tile([EPS, GN_EPS] * 8, (P, 1))
    cols["headsum"] = (r // HD == c // HD) * 1.0
    cols["upinc"] = (r <= c) * 1.0
    cols["ones_lstr"] = np.hstack([np.ones((P, P)), r > c])
    cols["caus"] = np.hstack([np.zeros((P, P)), np.where(c <= r, 0.0, NEG)])
    m16t = (r < c) & (r // 16 == c // 16)
    mi32t = (r <= c) & (r // CH == c // CH)
    ms32t = (r < c) & (r // CH == c // CH)
    cols["m_ab"] = np.hstack([m16t, mi32t])
    cols["m_ak"] = np.hstack([ms32t, mi32t])
    m16 = (r > c) & (r // 16 == c // 16)
    mo = (r > c) & (r // CH == c // CH) & (r // 16 != c // 16)
    cols["m_a"] = np.hstack([m16, mo])
    q4 = (r // Q == c // Q)[:, :TS]
    ms4t, mi4t = ((r < c)[:, :TS] & q4), ((r <= c)[:, :TS] & q4)
    cols["s_ab"] = np.hstack([ms4t, mi4t])
    cols["s_a"] = (r > c)[:, :TS] & q4
    cols["batch"] = (r // Q == np.arange(B)[None]) * 1.0
    reset = np.ones((P, N))
    reset[:, 0:T:CH] = 0
    reset[:, T::Q] = 0
    cols["reset"] = reset
    m = np.arange(P)
    mb, mt = m // 16, m % Q
    nb, nt = np.arange(TS) // Q, np.arange(TS) % Q
    cols["lf_new_l"] = np.tile((nb[:, None] == mb[None]) & (nt[:, None] <= mt[None]), (4, 1)) * 1.0
    rhs = np.ones((TS, PAST + TS))
    rhs[:, PAST:] = nt[:, None] > nt[None]
    cols["lf_new_r"] = np.tile(rhs, (4, 1))
    newmask = np.where((nb[None] == mb[:, None]) & (nt[None] <= mt[:, None]), 0.0, NEG)
    cols["sb_bias"] = np.hstack([np.zeros((P, PAST)), newmask])
    slopes = 2.0 ** (-8.0 * np.arange(1, 5) / 4)

    def dil(off, slope):
        mult = sum(((off >= 0) & (off <= w) & (off % d == 0)) * 1.0 for w, d in DIL)
        return np.where(mult > 0, -slope * off + np.log(np.maximum(mult, 1)), NEG)

    mh = m // Q % 4
    cols["sd_bias"] = np.hstack([
        dil((PAST + mt)[:, None] - np.arange(PAST)[None], slopes[mh][:, None]),
        np.where(newmask == 0, dil(mt[:, None] - nt[None], slopes[mh][:, None]), NEG)])
    for h in range(4):
        cols[f"d_bias{h}0"] = dil(r - c, slopes[h])
        cols[f"d_bias{h}1"] = dil(P + r - np.arange(T)[None], slopes[h])
    cols["iota16"] = np.tile(np.arange(16.0), (P, 1))
    cols["prow"] = i[:, None] * 1.0
    cols["groupsum"] = (r % TS == np.arange(TS)[None]) * 1.0
    where, at = {}, 0
    for k, v in cols.items():
        where[k] = (at, v.shape[1])
        at += v.shape[1]
    return np.hstack([np.asarray(v, np.float32) for v in cols.values()]), where


CONST, CONST_AT = constants()
CFIRST = P + 16

COLS = {}
_n = 0
for _k, _c in (("g0", 8), ("g1", 8), ("g2", 8), ("gm", 8), ("gout", 8), ("mu", 8), ("w0", 2), ("a0", 2),
               ("kks", 2), ("ka", 2), ("rk", 2), ("lnw", 2), ("lnb", 2)):
    COLS[_k] = (_n, _c)
    _n += _c
NCOLS = _n


class Steps:

    def __init__(self, new_semaphore, known=None):
        self.new, self.known = new_semaphore, known or {}
        self.sems, self.order = {}, {}

    def sem(self, name):
        if name not in self.sems:
            self.sems[name] = self.new(name)
            self.order.setdefault(name, [])
        return self.sems[name]

    def inc(self, name, step=None):
        s = self.sem(name)
        self.order[name].append(step)
        return s, 1

    def at(self, name, step):
        s = self.sem(name)
        order = self.known.get(name)
        return s, 1 if order is None else order.index(step) + 1

    def now(self, name):
        return self.sem(name), len(self.order[name])


def sbuf_map(nc):
    m = {}
    at = [(nc.sbuf_base + 63) // 64 * 64]
    places = {}

    def put(name, *shape, dt=F32, rows=P):
        size = int(np.prod(shape)) * 4
        places[name] = at[0]
        m[name] = nc.alloc_sbuf_tensor_at(name, [rows, *shape], dt, offset=at[0])
        at[0] += (size + 63) // 64 * 64
        return m[name]

    put("const", CONST.shape[1])
    put("cols", NCOLS)
    put("xT", KC, N)
    put("W", RING, KC, WCOLS)
    put("YT", KC, N)
    put("stat", 32)
    put("stage", 2, 256)
    put("rows", 776)
    put("lfg", B * 2, 4)
    put("pt", B * 2, dt=I32)
    put("idx", B * 2, dt=U32)
    base = at[0]
    put("x", 3, D)
    put("xn", 2, D)
    put("xm", 2, D)
    norms_end = at[0]
    at[0] = base
    put("hT", 18, N)
    put("hTok", 3, TW)
    at[0] = max(at[0], norms_end)
    put("xmT", KC, MEM)
    mix = at[0]
    put("dlt", KC, N)
    for name in ("lw", "aa", "gg", "kk", "kp", "bh", "kh", "t1"):
        put(name, 2, N)
    put("KR", 2, 2, N)
    put("lora", 2 * GW)
    put("shiftc", KC, 1 + B)
    put("shift", KC, B)
    for name in ("AB", "AK", "A1"):
        put(name, 4, 2 * P)
    for name in ("R", "PA", "PTA", "PB", "PTB"):
        put(name, 4, P)
    put("TOK", 4, GW)
    put("WA", 2, GW)
    put("U0", GW)
    put("U0n", GW)
    put("YLT", 2, N)
    put("Y0", 2, N)
    put("MT", 8, 2, P)
    put("NP", 8, 2, HD)
    put("ST", 9, 2, HD)
    put("S0T", B, 2, HD)
    put("sAB", 4, 2 * TS, rows=TS)
    put("sAK", 4, 2 * TS, rows=TS)
    put("sA1", 4, TS, rows=TS)
    put("SC", 3, 256)
    put("PT", 2, 2, P)
    put("LFU", 2, 2, P)
    put("lf", 3, 4)
    put("soft", 64)
    assert at[0] <= nc.sbuf_usable_end, at[0]
    end, at[0] = at[0], mix
    put("KTB", B, 2, 2, P)
    put("VB", B, 2, GW)
    put("KTD", B, 2, PAST)
    put("VD", B, 2, GW)
    put("VL", 3, GW)
    put("wm", 4, P)
    put("wm4", 4, TS, rows=TS)
    put("bsr", 2, P)
    put("sg", 2, P)
    put("QB", 2, B, 2, 32)
    put("SS", 2, PAST + TS)
    put("PTs", 2, 3, P)
    put("OS", 2, 2 * GW)
    put("LFP", 2, P)
    put("LFN", P, rows=TS)
    put("SQ", 4, N)
    put("RS", 4, N)
    assert at[0] <= places["lf"], at[0]
    assert at[0] <= nc.sbuf_usable_end, at[0]
    at[0] = max(at[0], end)
    at[0] = base
    put("X1", 3, D)
    put("XN", 3, D)
    put("gr", 3, D)
    put("softx", 64)
    peer = at[0]
    put("hX", KC, N)
    put("QX", B, KC, 32)
    put("MK", KC, MEM)
    put("MV", 2, D)
    put("MR", B, KC * MEM)
    put("SCx", 3, 256)
    put("PTx", 2, 2, P)
    put("SSx", 256)
    put("PTy", 2, P)
    assert at[0] <= nc.sbuf_usable_end, at[0]
    at[0] = peer
    put("UR", NR, D)
    put("VR", NR, D)
    put("keys", 16, NK)
    put("SA", NIT, 2, NK)
    put("dg", 4, P)
    put("cur", 2, NK)
    put("cur2", 2, NK)
    put("cand", TOPK, TOPK)
    put("cand2", TOPK, TOPK)
    put("eq", 2, TOPK, TOPK)
    put("ts", 2, TOPK)
    put("ti", 2, TOPK, dt=U32)
    put("tif", 2, TOPK)
    put("bj", 2, TOPK, dt=U32)
    put("bji", 2, TOPK, dt=U32)
    put("bjf", 2, TOPK)
    put("ef", 2, TOPK)
    put("idxu", 2, TOPK, dt=U32)
    put("idxv", 2, TOPK, dt=U32)
    for name in ("bs", "ge", "act", "gl", "wv"):
        put(name, 2, TOPK)
    put("gs", 16)
    assert at[0] <= nc.sbuf_usable_end, at[0]
    at[0] = places["YT"]
    put("qPa", KC, N)
    at[0] = places["const"] + 4 * CONST_AT["m_ab"][0]
    put("qPb", KC, N)
    assert at[0] <= places["const"] + 4 * CONST_AT["iota16"][0]
    return m


def build(nc, io, steps_known=None):
    ctx = ExitStack()
    with ctx:
        S = Steps(lambda n: ctx.enter_context(nc.semaphore(n)), steps_known)
        M = sbuf_map(nc)
        PS = ctx.enter_context(nc.psum_tensor("ps", [P, 8, 512], F32))
        block = ctx.enter_context(nc.Block())
        program(nc, io, S, M, PS, block)
    return S.order


def program(nc, io, S, M, PS, block):
    inc, at, now = S.inc, S.at, S.now

    def cst(name, rows=P, cols=None):
        a, n = CONST_AT[name]
        return M["const"][0:rows, a:a + (cols or n)]

    def col(name, chunk, p0=0, p1=P):
        a = COLS[name][0] + chunk
        return M["cols"][p0:p1, a:a + 1]

    def colb(name, c0, c1, n):
        a = COLS[name][0]
        return M["cols"][:, a + c0:a + c1].unsqueeze(2).to_broadcast([P, c1 - c0, n])

    xT, W, YT, stat, stage = M["xT"], M["W"], M["YT"], M["stat"], M["stage"]
    hT, hTok = M["hT"], M["hTok"]
    ident = cst("ident")

    lw, aa, gg, kk, kp, bh, kh, t1, KR = (M[k] for k in ("lw", "aa", "gg", "kk", "kp", "bh", "kh", "t1", "KR"))
    dlt, lora = M["dlt"], M["lora"]
    Gc, Pp, Pi, t2 = (dlt[:, 2 * j:2 * j + 2, :] for j in range(4))
    TOK, WA, U0, U0n, YLT, Y0 = (M[k] for k in ("TOK", "WA", "U0", "U0n", "YLT", "Y0"))
    MT, NPr, ST, S0T = M["MT"], M["NP"], M["ST"], M["S0T"]
    rT, kT, vT = hT[:, 0:2, :], hT[:, 2:4, :], hT[:, 4:6, :]

    ORDER = (
        [("lin", 0), ("mem_stat", None), ("lin", 1), ("lin", 2), ("mem_turn", None), ("lin", 3), ("rw_pre", None), ("rw_kk", None), ("rw_vec", None), ("rw_tile", 0), ("rw_tile", 1),
         ("rw_scan", None), ("rw_tile", 2), ("rw_sample", None), ("rw_out", None), ("fill", 11), ("lf", None), ("attn", None),
         ("sgu", None), ("gnorm", (0, 2)), ("sattn", None), ("gnorm", (1, 3)), ("fill", 19)]
        + [("lin", b) for b in range(20, 24)] + [("norm", 0)] + [("lin", b) for b in range(24, 28)]
        + [("scross_k", None), ("cross", None), ("scross_v", None)] + [("lin", b) for b in range(28, 32)] + [("norm", 1)]
        + [("lin", 32), ("score", 0), ("lin", 33)]
        + [s for h in range(1, 7) for s in (("lin", 33 + h), ("score", h))] + [("score", 7), ("peer", None)])
    X1, XN, gr, hX, QX, MK, MV, MR, SCx, PTx, SSx, PTy, softx = (
        M[k] for k in ("X1", "XN", "gr", "hX", "QX", "MK", "MV", "MR", "SCx", "PTx", "SSx", "PTy", "softx"))
    UR, VR, keys, SA, dg = (M[k] for k in ("UR", "VR", "keys", "SA", "dg"))

    def qP(chunk):
        return M["qPa" if chunk < KC else "qPb"][:, chunk % KC, :]

    OX = MK[:].rearrange("p c m -> p (c m)").rearrange("p (j n) -> p j n", j=2)
    CUNITS = [(h, qb) for h in range(4) for qb in range(2)]

    PART = hX[:].rearrange("p k n -> p (k n)")[:, 0:D]
    GN_BANK = (6, 2, 7, 3)

    def x_of_block(b):
        return "xT" if b < 12 or 24 <= b < 28 or b >= 32 else "xmT" if b < 20 else "YT"

    def peer_tiles():
        return ((0, 0, 8), (1, 8, 8), (2, 16, 2))

    AUNITS = [(BQ, BK, TBV, 2, h, qb) for h in range(4) for qb in range(2)] \
        + [(DQ, DK, TDV, 6, h, qb) for h in range(4) for qb in range(2)]
    NA = len(AUNITS)
    SC, PT, LFU, lf, soft = (M[k] for k in ("SC", "PT", "LFU", "lf", "soft"))
    KTB, VB, KTD, VD, VL, QB, SS, PTs = (M[k] for k in ("KTB", "VB", "KTD", "VD", "VL", "QB", "SS", "PTs"))
    upinc, ones_lstr = cst("upinc"), cst("ones_lstr")
    ones, lstr = ones_lstr[:, 0:P], ones_lstr[:, P:]

    def heads():
        for par in range(2):
            for c in range(2):
                yield 2 * par + c, par, c, 2 * c + par, slice(HD * par, HD * par + HD)

    def tile_mats(t):
        m = TILES[t][1]
        if t < 2:
            ab, ak, a1 = M["AB"], M["AK"], M["A1"]
            return (lambda i: ab[:, i, 0:m], lambda i: ab[:, i, m:2 * m], lambda i: ak[:, i, 0:m],
                    lambda i: ak[:, i, m:2 * m], lambda i: a1[:, i, 0:m], lambda i: a1[:, i, m:2 * m])
        ab, ak, a1 = M["sAB"], M["sAK"], M["sA1"]
        return (lambda i: ab[:, i, 0:m], lambda i: ab[:, i, m:2 * m], lambda i: ak[:, i, 0:m],
                lambda i: ak[:, i, m:2 * m], lambda i: a1[:, i, :], None)

    def quad(name, m):
        return M[name][0:m].rearrange("p a b -> p (a b)")[:, 0:4 * m].rearrange("p (a b) -> p a b", a=4)

    XB, XV, XU = (M[k][0:TS].rearrange("p a b -> p (a b)").rearrange("p (b f) -> p b f", b=B)
                  for k in ("AB", "AK", "A1"))

    def xpose_bank(j):
        return PS[:, 2 + j % 6, :]

    paced = {}

    NORMS0 = [("x", t) for t in range(3)] + [("xm", t) for t in range(2)]

    def rows_of(kind, t):
        return TILES[t][1] if kind == "x" else P

    def follow(stages):
        for name, argument in ORDER:
            if name in stages:
                stages[name](*(() if argument is None else (argument,)))

    @block.sync
    def _(sp):
        sp.dma_start(M["x"][:, 0, :], io["x_all"][0:P, :]).then_inc(S.sem("x0_in"), 16)
        sp.dma_start(M["const"][:, 0:CFIRST], io["const"][:, 0:CFIRST]).then_inc(S.sem("const0_in"), 16)
        sp.dma_start(M["x"][:, 1, :], io["x_all"][P:T, :]).then_inc(S.sem("x1_in"), 16)
        sp.dma_start(M["x"][0:TS, 2, :], io["x_all"][T:N, :]).then_inc(S.sem("x2_in"), 16)
        sp.dma_start(M["cols"][:], io["cols"]).then_inc(S.sem("cols_in"), 16)

        sp.dma_start(M["pt"][:], io["page_table"].to_broadcast([P, B * 2])).then_inc(S.sem("pt_in"), 16)

        def load_block(b):
            name, c0, n, _ = BLOCKS[b]
            if b >= RING:
                sp.wait_ge(S.sem("pe_lin"), LAST[b - RING])
            sp.dma_start(W[:, b % RING, :, 0:n], io[name].rearrange("(k p) n -> p k n", p=P)[:, :, c0:c0 + n])\
                .then_inc(S.sem(f"w{b % RING}_in"), 16)

        load_block(0)
        for t in range(2):
            sp.dma_start(M["xm"][:, t, :], io["mem_prompt"][t * P:(t + 1) * P, :]).then_inc(S.sem(f"xm{t}_in"), 16)
        load_block(1)
        load_block(2)
        sp.dma_start(M["const"][:, CFIRST:], io["const"][:, CFIRST:]).then_inc(S.sem("const_in"), 16)
        sp.dma_start(lora[0:64, 0:GW], io["a_w2"]).then_inc(S.sem("rwp_in"), 16)
        sp.dma_start(lora[64:128, 0:GW], io["a_a2"]).then_inc(S.sem("rwp_in"), 16)
        sp.dma_start(lora[:, GW:], io["a_g2"]).then_inc(S.sem("rwp_in"), 16)
        sp.dma_start(M["shift"][:], io["shift"]).then_inc(S.sem("rwp_in"), 16)
        sp.dma_start(S0T[:], io["s0T"]).then_inc(S.sem("rwp_in"), 16)
        for a, n, name in ((0, GW, "c_lng"), (GW, GW, "c_lnb"), (2 * GW, 4, "b_f")):
            sp.dma_start(M["rows"][:, a:a + n], io[name].to_broadcast([P, n])).then_inc(S.sem("rows_in"), 16)
        for b in range(3, 15):
            load_block(b)

        sp.wait_ge(*at("act_lin", ("unit", LAST[11])))
        n_out = 0
        for name, src in (("o_bk", hT[:, BK:BK + 2, :]), ("o_dk", hT[:, DK:DK + 2, :]),
                          ("o_tok0", hTok[:, 0, :]), ("o_tok1", hTok[:, 1, :]), ("o_tok2", hTok[0:TS, 2, :])):
            sp.dma_start(io[name], src).then_inc(S.sem("out_sp"), 16)
            n_out += 1
        sp.wait_ge(*at("dve_rw", "shiftc"))
        sp.dma_start(io["o_shift"], M["shiftc"][:]).then_inc(S.sem("out_sp"), 16)
        sp.wait_ge(*at("dve_st", 7))
        sp.dma_start(io["o_pwkv"], ST[:, 8, :, :]).then_inc(S.sem("out_sp"), 16)
        sp.wait_ge(*at("dve_rw", "swkv"))
        sp.dma_start(io["o_swkv"], NPr[:]).then_inc(S.sem("out_sp"), 16)
        for b in range(15, 17):
            load_block(b)
        sp.wait_ge(*at("dve_y", "a"))
        sp.dma_start(M["wm"][:], io["wsT"]).then_inc(S.sem("sgu_in"), 16)
        sp.dma_start(M["wm4"][:], io["ws4"]).then_inc(S.sem("sgu_in"), 16)
        sp.dma_start(M["bsr"][:], io["bsr"]).then_inc(S.sem("sgu_in"), 16)
        sp.dma_start(KTD[:], io["dkT"]).then_inc(S.sem("dk_in"), 16)
        sp.dma_start(VD[:], io["dv"]).then_inc(S.sem("dv_in"), 16)
        for b in range(17, 20):
            load_block(b)
        sp.wait_ge(*at("dve_lf", "lf"))
        sp.dma_start(io["o_lf"], lf[:]).then_inc(S.sem("out_sp"), 16)
        sp.wait_ge(*at("dve_sg", ("v", 2)))
        sp.dma_start(io["o_cv"], VL[0:TS, 2, :]).then_inc(S.sem("out_sp"), 16)
        for b in range(20, 23):
            load_block(b)
        sp.wait_ge(*at("dve_gn", 3))
        for j in range(2):
            sp.wait_ge(S.sem(f"out_stage{j}"), 16 * 8)
        for t, (t0, m) in enumerate(TILES):
            sp.dma_start(X1[0:m, t, :], io["x_all"][t0:t0 + m, :]).then_inc(S.sem("X1_in"), 16)
        for r in range(3):
            sp.dma_start(gr[:, r, :], io["gains"][r:r + 1, :].to_broadcast([P, D])).then_inc(S.sem("gr_in"), 16)
        sp.dma_start(MK[:], io["o_memk"].rearrange("(c p) m -> p c m", p=P)).then_inc(S.sem("mk_in"), 16)
        sp.dma_start(MV[:], io["o_memv"].rearrange("(k p) n -> p k n", p=P)).then_inc(S.sem("mv_in"), 16)
        for b in range(23, 28):
            load_block(b)
        for i in range(2 * B):
            if i >= B:
                sp.wait_ge(*at("pe_mr", ("k", i - B)))
            sp.dma_start(MR[:, i % B, :], io["mk_s" if i < B else "mv_s"][i % B]).then_inc(S.sem(f"mr{i % B}_in"), 16)
        for b in range(28, 31):
            load_block(b)
        sp.wait_ge(*at("dve_cx", "ys"))
        sp.dma_start(keys[:], io["keysT"]).then_inc(S.sem("keys_in"), 16)
        for b in range(31, 40):
            load_block(b)
        sp.wait_ge(*at("dve_nx", (1, 2)))
        for g in range(4):
            sp.dma_start(gr[32 * g:32 * g + 32, 0, :], XN[0:TS, 2, :]).then_inc(S.sem("xs_in"), 16)
        for t, (t0, m) in enumerate(TILES):
            sp.wait_ge(*at("dve_fin", ("y", t)))
            sp.dma_start(io["o_y"][t0:t0 + m, :], X1[0:m, t, :]).then_inc(S.sem("out_sp"), 16)
        sp.wait_ge(S.sem("out_sp"), 16 * (n_out + 8))

    @block.tensor
    def _(pe):
        mm, tr = nc.tensor.matmul, nc.tensor.transpose
        npose, filled = [0], [KC * LAST[3]]

        def transposes(kind, t, src, m, done):
            for half in range(2):
                if npose[0] >= 6:
                    pe.wait_ge(*at("dve_xT", npose[0] - 6))
                for j in range(4):
                    k = 4 * half + j
                    ins = tr(xpose_bank(npose[0])[:, j * P:j * P + m], src[0:m, k * P:(k + 1) * P], ident[0:m, 0:m])
                ins.then_inc(*inc(done, npose[0]))
                npose[0] += 1

        def turn(first, end):
            for i in range(first, end):
                kind, t = NORMS0[i]
                pe.wait_ge(*at("dve_xn", (kind, t)))
                transposes(kind, t, M["xn"][:, i % 2, :], rows_of(kind, t), "pe_xT")

        pe.wait_ge(S.sem("const0_in"), 16)
        turn(0, 3)

        def product(u, k):
            b, cc, nn, t = UNITS[u]
            src = x_of_block(b)
            if k == 0:
                if u == LAST[b - 1] or u == 0:
                    pe.wait_ge(S.sem(f"w{b % RING}_in"), 16 * (b // RING + 1))
                if u == LAST[11]:
                    pe.wait_ge(*at("dve_xT", 9))
                if u >= 2:
                    dve, count = EVAC[u - 2]
                    pe.wait_ge(S.sem("dve_lin" if dve else "act_lin"), count)
            a, w = M[src], W[:, b % RING, k, :]
            if t is None:
                ins = mm(PS[:, u % 2, 0:a.shape[2]], w[:, cc:cc + nn], a[:, k, :], start=k == 0, stop=k == KC - 1)
            elif t == 2 and BLOCKS[b][0] in ADDS:
                q, part = k % 4, k // 4
                ins = mm(PS[TS * q:TS * q + TS, u % 2, 0:nn], a[:, 2 * q + part, T:N],
                         W[:, b % RING, 2 * q + part, 0:nn], start=part == 0, stop=part == 1, skip_group_check=True)
            else:
                t0, m = TILES[t]
                ins = mm(PS[0:m, u % 2, 0:nn], a[:, k, t0:t0 + m], w[:, 0:nn], start=k == 0, stop=k == KC - 1)
            if k == KC - 1:
                ins.then_inc(*inc("pe_lin", ("unit", u + 1)))

        def linear(b):
            if b == 20:
                pe.wait_ge(*at("dve_gn", 3))
            elif b == 28:
                pe.wait_ge(*at("dve_cx", "ys"))
                pe.wait_ge(*at("dve_cx", ("o", len(CUNITS) - 1)))
            for u in range(LAST[b - 1] if b else 0, LAST[b]):
                for k in range(KC):
                    product(u, k)

        def gap(label, n=GAP):
            for _ in range(min(n, KC * LAST[19] - filled[0])):
                product(*divmod(filled[0], KC))
                filled[0] += 1
            paced[label] = filled[0] // KC

        def fill(b):
            gap(("fill", b), max(0, KC * LAST[b] - filled[0]))

        def rw_pre():
            pe.wait_ge(S.sem("rwp_in"), 16 * 5)
            pe.wait_ge(S.sem("const_in"), 16)
            pe.wait_ge(*at("dve_xT", 9))
            gap("xs", 16)
            gap("tanh", 12)
            pe.wait_ge(*at("act_rw", "tanh"))
            for c in range(2):
                ins = mm(PS[:, 2 + c, 0:N], lora[0:64, c * P:(c + 1) * P], t1[0:64, 0, :], start=True, stop=True)
            ins.then_inc(*inc("pe_rw", "lora_w"))
            for c in range(2):
                ins = mm(PS[:, 4 + c, 0:N], lora[64:128, c * P:(c + 1) * P], hT[64:128, 6, :], start=True, stop=True)
            ins.then_inc(*inc("pe_rw", "lora_a"))
            pe.wait_ge(*at("act_rw", "sigg"))
            for c in range(2):
                ins = mm(PS[:, 6 + c, 0:N], lora[:, GW + c * P:GW + (c + 1) * P], t1[:, 1, :], start=True, stop=True)
            ins.then_inc(*inc("pe_rw", "lora_g"))

        def headsum(src, bank, step):
            for c in range(2):
                ins = mm(PS[:, bank + c, 0:N], cst("headsum"), src[:, c, :], start=True, stop=True)
            ins.then_inc(*inc("pe_rw", step))

        def rw_kk():
            gap("kksq", 12)
            pe.wait_ge(*at("dve_rw", "kksq"))
            pe.wait_ge(*at("act_rw", "sigw"))
            headsum(t2, 2, "kkn")

        def rw_vec():
            gap("bon", 24)
            pe.wait_ge(*at("dve_rw", "bon"))
            pe.wait_ge(*at("act_rw", "siga"))
            headsum(t2, 4, "bonus")

        def rw_tile(t):
            t0, m = TILES[t]
            a1t, a3t, a2t, a4t, a16, off = tile_mats(t)
            if t == 0:
                pe.wait_ge(*at("act_rw", "g"))
                gap("kh", 8)
                pe.wait_ge(*at("dve_rw", "kh"))
            else:
                pe.wait_ge(*at("dve_rw", ("mn", t - 1)))
                pe.wait_ge(*at("act_rw", ("y0", t - 1)))
            for j, src in enumerate((KR[:, :, 0, :], bh, kh, vT)):
                for c in range(2):
                    ins = tr(PS[0:m, 6 + j // 2, (j % 2) * 256 + c * P:(j % 2) * 256 + (c + 1) * P],
                             src[:, c, t0:t0 + m], ident)
            ins.then_inc(*inc("pe_rw", ("tok", t)))
            if t == 0:
                pe.wait_ge(*at("dve_rw", "kkm"))
                pe.wait_ge(*at("dve_rw", "bonus"))
            if t == 2:
                pe.wait_ge(*at("dve_st", 7))
            for i, par, c, h, ph in heads():
                ins = mm(PS[0:m, 2 + par, c * 2 * m:(c + 1) * 2 * m], bh[ph, c, t0:t0 + m],
                         KR[ph, c, 0:2, t0:t0 + m], start=True, stop=True)
            ins.then_inc(*inc("pe_rw", ("x1", t)))
            for i, par, c, h, ph in heads():
                ins = mm(PS[0:m, 4 + par, c * 2 * m:(c + 1) * 2 * m], kh[ph, c, t0:t0 + m],
                         KR[ph, c, 0:2, t0:t0 + m], start=True, stop=True)
            ins.then_inc(*inc("pe_rw", ("x2", t)))
            gap(("tok", t))
            pe.wait_ge(*at("act_rw", ("tok", t)))
            for i, par, c, h, ph in heads():
                ins = mm(PS[0:m, 6 + par, c * m:(c + 1) * m], KR[ph, c, 0, t0:t0 + m],
                         bh[ph, c, t0:t0 + m], start=True, stop=True)
            ins.then_inc(*inc("pe_rw", ("x3", t)))

            def four(bank, lhs, rhs, step):
                for i in range(4):
                    ins = mm(PS[0:m, bank, i * m:(i + 1) * m], lhs(i), rhs(i), start=True, stop=True)
                ins.then_inc(*inc("pe_rw", (step, t)))

            R, PA, PTA, PB, PTB = ((lambda i, q=quad(k, m): q[:, i, :]) for k in ("R", "PA", "PTA", "PB", "PTB"))
            gap(("R0", t))
            pe.wait_ge(*at("dve_rw", ("R0", t)))
            four(2, a1t, a16, "P2")
            if t == 2:
                pe.wait_ge(*at("act_rw", ("P2", t)))
                four(4, PA, R, "R1")
            else:
                four(3, a16, a1t, "P2T")
                gap(("P2T", t))
                pe.wait_ge(*at("act_rw", ("P2", t)))
                four(4, PA, R, "R1")
                pe.wait_ge(*at("act_rw", ("P2T", t)))
                four(5, PTA, PA, "P4")
                four(2, PA, PTA, "P4T")
                gap(("P4T", t))
                pe.wait_ge(*at("act_rw", ("P4", t)))
                pe.wait_ge(*at("dve_rw", ("R1", t)))
                four(3, PB, R, "R2")
                pe.wait_ge(*at("act_rw", ("P4T", t)))
                four(4, PTB, PB, "P8")
                gap(("P8", t))
                pe.wait_ge(*at("act_rw", ("P8", t)))
                pe.wait_ge(*at("dve_rw", ("R2", t)))
                four(2, PA, R, "R3")
                gap(("R3", t))
                pe.wait_ge(*at("dve_rw", ("R3", t)))
                for i in range(4):
                    ins = tr(PS[:, 5, i * P:(i + 1) * P], R(i), ident)
                ins.then_inc(*inc("pe_rw", ("T16", t)))
                four(4, off, R, "Q")
                gap(("Q", t))
                pe.wait_ge(*at("act_rw", ("T16", t)))
                pe.wait_ge(*at("act_rw", ("Q", t)))
                four(3, PTA, PB, "Z")
            gap(("T", t))
            pe.wait_ge(*at("dve_rw", ("T", t)))
            hs = lambda h: slice(h * HD, (h + 1) * HD)
            for i, par, c, h, ph in heads():
                mm(PS[0:m, 6, hs(h)], R(i), TOK[0:m, 0, hs(h)], start=True, stop=True)
                ins = mm(PS[0:m, 6, 256 + h * HD:256 + (h + 1) * HD], a2t(i), TOK[0:m, 3, hs(h)],
                         start=True, stop=True)
            ins.then_inc(*inc("pe_rw", ("wa", t)))
            gap(("wa", t))
            pe.wait_ge(*at("act_rw", ("wa", t)))
            for i, par, c, h, ph in heads():
                ins = mm(PS[0:m, 7, hs(h)], R(i), WA[0:m, 1, hs(h)], start=True, stop=True)
            ins.then_inc(*inc("pe_rw", ("u0", t)))
            for i, par, c, h, ph in heads():
                ins = mm(PS[ph, 5, c * m:(c + 1) * m], WA[0:m, 0, hs(h)], a3t(i), start=True, stop=True)
            ins.then_inc(*inc("pe_rw", ("yl", t)))
            pe.wait_ge(*at("act_rw", ("u0n", t)))
            for i, par, c, h, ph in heads():
                mm(PS[ph, 4, c * m:(c + 1) * m], TOK[0:m, 3, hs(h)], a4t(i), start=True, stop=False,
                   skip_group_check=True)
                ins = mm(PS[ph, 4, c * m:(c + 1) * m], U0n[0:m, hs(h)], a3t(i), start=False, stop=True,
                         skip_group_check=True)
            ins.then_inc(*inc("pe_rw", ("y0", t)))
            if t == 2:
                return
            for cc in range(4):
                bank = (2, 3, 6, 7)[cc]
                rows = slice(CH * cc, CH * cc + CH)
                for i, par, c, h, ph in heads():
                    mm(PS[ph, bank, c * HD:(c + 1) * HD], WA[rows, 0, hs(h)], TOK[rows, 1, hs(h)],
                       start=True, stop=True, skip_group_check=True)
                    mm(PS[ph, bank, P + c * HD:P + (c + 1) * HD], TOK[rows, 2, hs(h)], TOK[rows, 3, hs(h)],
                       start=True, stop=False, skip_group_check=True)
                    ins = mm(PS[ph, bank, P + c * HD:P + (c + 1) * HD], TOK[rows, 1, hs(h)], U0[rows, hs(h)],
                             start=False, stop=True, skip_group_check=True)
                ins.then_inc(*inc("pe_rw", ("mn", t, cc)))

        def rw_scan():
            pe.wait_ge(*at("dve_rw", ("mn", 1)))
            pe.wait_ge(*at("pool_rw", "zero"))
            for n in range(8):
                if n:
                    gap(("st", n))
                    pe.wait_ge(*at("dve_st", n - 1))
                for c in range(2):
                    ins = mm(PS[:, 2 + n % 2, c * HD:(c + 1) * HD], MT[:, n, c, :], ST[:, n, c, :],
                             start=True, stop=True)
                ins.then_inc(*inc("pe_rw", ("st", n)))

        def rw_sample():
            hs = lambda h: slice(h * HD, (h + 1) * HD)
            pe.wait_ge(*at("dve_rw", ("T", 2)))
            for c in range(2):
                gap(("x", c), 11)
                pe.wait_ge(*at("pool_rw", ("x", c)))
                for par in range(2):
                    h, ph, fs = 2 * c + par, slice(HD * par, HD * par + HD), slice(HD * par, HD * par + HD)
                    mm(PS[ph, 2 + c, :], WA[0:TS, 0, hs(h)], XB[:, :, fs], start=True, stop=True,
                       skip_group_check=True)
                    mm(PS[ph, 6 + c, :], TOK[0:TS, 2, hs(h)], XV[:, :, fs], start=True, stop=False,
                       skip_group_check=True)
                    ins = mm(PS[ph, 6 + c, :], TOK[0:TS, 1, hs(h)], XU[:, :, fs], start=False, stop=True,
                             skip_group_check=True)
                ins.then_inc(*inc("pe_rw", ("smn", c)))
            for c in range(2):
                pe.wait_ge(*at("dve_rw", ("smn", c)))
                if c == 0:
                    pe.wait_ge(*at("act_rw", ("y0", 2)))
                    pe.wait_ge(*at("dve_rw", ("yl", 2)))
                for b in range(B):
                    ins = mm(PS[:, 4 + c, b * HD:(b + 1) * HD], MT[:, b, c, :], S0T[:, b, c, :],
                             start=True, stop=True)
                ins.then_inc(*inc("pe_rw", ("ss", c)))

        def rw_out():
            pe.wait_ge(*at("dve_rw", ("smn", 1)))
            for i, par, c, h, ph in heads():
                for n in range(8):
                    ins = mm(PS[ph, 2 + par, c * T + n * CH:c * T + (n + 1) * CH], ST[ph, n, c, :],
                             YLT[ph, c, n * CH:(n + 1) * CH], start=True, stop=True, skip_group_check=True)
            ins.then_inc(*inc("pe_rw", "yst"))
            for i, par, c, h, ph in heads():
                for b in range(B):
                    ins = mm(PS[ph, 6 + par, c * TS + b * Q:c * TS + (b + 1) * Q], S0T[ph, b, c, :],
                             YLT[ph, c, T + b * Q:T + (b + 1) * Q], start=True, stop=True, skip_group_check=True)
            ins.then_inc(*inc("pe_rw", "yss"))
            pe.wait_ge(*at("dve_rw", "swkv"))
            pe.wait_ge(*at("dve_rw", "y"))
            headsum(Y0, 4, "mean")
            gap("ysq", 4)
            pe.wait_ge(*at("act_rw", "ysq"))
            headsum(t1, 2, "var")
            gap("var", 16)

        def attn():
            for s in range(NA + 3):
                if s < NA:
                    u = s
                    qc, kc, _, _, h, qb = AUNITS[u]
                    ph, w, ps = slice(HD * (h % 2), HD * (h % 2) + HD), P * (qb + 1), PS[:, 2 + u % 2, :]
                    if u >= 2:
                        pe.wait_ge(*at("dve_at", ("sc", u - 2)))
                    else:
                        pe.wait_ge(*at("dve_y", "a"))
                    fox = qc == BQ
                    ins = mm(ps[:, 0:w], hT[ph, qc + h // 2, qb * P:(qb + 1) * P], hT[ph, kc + h // 2, 0:w],
                             start=True, stop=not fox, skip_group_check=True)
                    if fox:
                        pe.wait_ge(*at("dve_at", ("lfu", u)))
                        ins = mm(ps[:, 0:P], LFU[:, u % 2, 0, :], lstr, start=False, stop=qb == 0,
                                 skip_group_check=True)
                        if qb:
                            ins = mm(ps[:, 0:w], LFU[:, u % 2, 1, :], ones_lstr, start=False, stop=True,
                                     skip_group_check=True)
                    ins.then_inc(*inc("pe_at", ("sc", u)))
                if 2 <= s < NA + 2:
                    u = s - 2
                    qb = AUNITS[u][5]
                    gap(("p", u))
                    pe.wait_ge(*at("dve_at", ("p", u)))
                    for kt in range(qb + 1):
                        ins = tr(PS[:, 4 + u % 2, kt * P:(kt + 1) * P], SC[:, u % 3, kt * P:(kt + 1) * P], ident)
                    ins.then_inc(*inc("pe_at", ("pt", u)))
                if s >= 3:
                    u = s - 3
                    _, _, vc, _, h, qb = AUNITS[u]
                    pe.wait_ge(*at("act_at", ("pt", u)))
                    if u >= 2:
                        pe.wait_ge(*at("dve_at", ("o", u - 2)))
                    ph = slice(HD * (h % 2), HD * (h % 2) + HD)
                    for kt in range(qb + 1):
                        ins = mm(PS[ph, 6 + u % 2, 0:P], hTok[:, kt, vc + h * HD:vc + (h + 1) * HD], PT[:, u % 2, kt, :],
                                 start=kt == 0, stop=kt == qb, skip_group_check=True)
                    ins.then_inc(*inc("pe_at", ("o", u)))

        def sgu():
            for t, (t0, m) in enumerate(TILES):
                gap(("sg", t), 6)
                pe.wait_ge(*at("dve_sg", ("v", t)))
                if t == 0:
                    pe.wait_ge(*at("dve_at", ("o", NA - 1)))
                if t == 2:
                    pe.wait_ge(*at("dve_sg", ("y", 0)))
                for i, par, c, h, ph in heads():
                    ins = mm(PS[ph, 2 + t % 2, c * m:(c + 1) * m], VL[0:m, t, h * HD:(h + 1) * HD],
                             M["wm"][:, h, :] if t < 2 else M["wm4"][:, h, :], start=True, stop=True,
                             skip_group_check=True)
                ins.then_inc(*inc("pe_sg", t))

        def sattn():
            for g, (kc, vc) in enumerate(((BK, TBV), (DK, TDV))):
                ps = PS[:, 2 + g, :]
                if g == 0:
                    pe.wait_ge(*at("dve_sg", ("y", 2)))
                    pe.wait_ge(*at("pool_sa", "q"))
                    pe.wait_ge(*at("dve_sa", "lfn"))
                    pe.wait_ge(S.sem("gath_in"), 16 * 16)
                    mm(ps[:, 0:PAST], M["LFP"][:, 1, :], ones_lstr, start=True, stop=False, skip_group_check=True)
                    mm(ps[:, 0:P], M["LFP"][:, 0, :], lstr, start=False, stop=False, skip_group_check=True)
                    mm(ps[:, 0:PAST + TS], M["LFN"][:], cst("lf_new_r", TS), start=False, stop=False,
                       skip_group_check=True)
                else:
                    pe.wait_ge(S.sem("dk_in"), 16)
                for b in range(B):
                    rows = slice(32 * (b // 2), 32 * (b // 2) + 32)
                    for c in range(2):
                        k = KTB[:, b, :, c, :] if g == 0 else KTD[:, b, c, :]
                        mm(ps[rows, 0:PAST], QB[:, g, b, c, :], k, start=g == 1 and b % 2 == 0 and c == 0,
                           stop=False, skip_group_check=True)
                        ins = mm(ps[rows, PAST:PAST + TS], QB[:, g, b, c, :], hT[:, kc + c, T:N], start=False,
                                 stop=True, skip_group_check=True)
                ins.then_inc(*inc("pe_sa", ("sc", g)))
            for g in range(2):
                pe.wait_ge(*at("dve_sa", ("p", g)))
                for kt in range(2):
                    tr(PS[:, 4 + g, kt * P:(kt + 1) * P], SS[:, g, kt * P:(kt + 1) * P], ident)
                tr(PS[0:TS, 4 + g, 2 * P:3 * P], SS[:, g, PAST:], ident).then_inc(*inc("pe_sa", ("pt", g)))
            for g, vc in enumerate((TBV, TDV)):
                pe.wait_ge(*at("act_sa", ("pt", g)))
                pe.wait_ge(S.sem("gv_in" if g == 0 else "dv_in"), 16 * 16 if g == 0 else 16)
                pe.wait_ge(*at("act_gn", ("rms", 2 * g)))
                v = VB if g == 0 else VD
                for b in range(B):
                    pair, rows = slice(b // 2 * 32, b // 2 * 32 + 32), slice(32 * (b % 4), 32 * (b % 4) + 32)
                    o = PS[rows, 6 + g, b // 4 * GW:(b // 4 + 1) * GW]
                    for kt in range(2):
                        mm(o, PTs[:, g, kt, pair], v[:, b, kt, :], start=kt == 0, stop=False, skip_group_check=True)
                    ins = mm(o, PTs[0:TS, g, 2, pair], hTok[0:TS, 2, vc:vc + GW], start=False, stop=True,
                             skip_group_check=True)
                ins.then_inc(*inc("pe_sa", ("o", g)))
            for g in range(2):
                pe.wait_ge(*at("act_sa", ("o", g)))
                for j in range(4):
                    ins = tr(PS[:, 4 + g, j * P:(j + 1) * P], M["OS"][:, g, j * P:(j + 1) * P], ident)
                ins.then_inc(*inc("pe_sa", ("ot", g)))

        def gnorm(groups):
            for g in groups:
                pe.wait_ge(*at("act_gn", ("sq", g)))
                for j in range(2):
                    ins = mm(PS[:, GN_BANK[g], 0:N], ones, M["SQ"][:, g // 2 * 2 + j, :], start=j == 0, stop=j == 1)
                ins.then_inc(*inc("pe_gn", g))

        def norm(i):
            pe.wait_ge(S.sem("dve_lin"), 12 * (i + 1))
            for half in range(2):
                ins = mm(PS[0:TS, 2 + half, :], cst("groupsum"), PART[:, half * 512:(half + 1) * 512], start=True, stop=True)
            ins.then_inc(*inc("pe_part", i))
            for t, (t0, m) in enumerate(TILES):
                pe.wait_ge(*at("dve_nx", (i, t)))
                for half in range(2):
                    bank = 2 + 2 * t + half
                    for j in range(4):
                        k = 4 * half + j
                        ins = tr(PS[:, bank, j * P:j * P + m], XN[0:m, t, k * P:(k + 1) * P], ident[0:m, 0:m])
                    ins.then_inc(*inc("pe_nx", (i, t, half)))
            pe.wait_ge(*at("act_nx", (i, 2, 1)))
            if i == 1:
                residual([0, 1]).then_inc(S.sem("v_free"), NR)

        def cross():
            nu = len(CUNITS)
            for s in range(nu + 3):
                if s < nu:
                    h, qb = CUNITS[s]
                    if s == 0:
                        pe.wait_ge(*at("act_lin", ("unit", LAST[27])))
                        pe.wait_ge(S.sem("mk_in"), 16)
                    else:
                        if s >= 2:
                            pe.wait_ge(*at("act_cx", ("p", s - 2)))
                    for c in range(2):
                        ins = mm(PS[:, 2 + s % 2, 0:MEM], hX[:, 2 * h + c, qb * P:(qb + 1) * P], MK[:, 2 * h + c, :],
                                 start=c == 0, stop=c == 1)
                    ins.then_inc(*inc("pe_cx", ("sc", s)))
                if 2 <= s < nu + 2:
                    u = s - 2
                    pe.wait_ge(*at("dve_cx", ("p", u)))
                    if u >= 2:
                        pe.wait_ge(*at("act_cx", ("pt", u - 2)))
                    for kt in range(2):
                        ins = tr(PS[:, 4 + u % 2, kt * P:(kt + 1) * P], SCx[:, u % 3, kt * P:(kt + 1) * P], ident)
                    ins.then_inc(*inc("pe_cx", ("pt", u)))
                if s >= 3:
                    u = s - 3
                    h, qb = CUNITS[u]
                    pe.wait_ge(*at("act_cx", ("pt", u)))
                    if u == 0:
                        pe.wait_ge(S.sem("mv_in"), 16)
                    if u >= 2:
                        pe.wait_ge(*at("dve_cx", ("o", u - 2)))
                    for c in range(2):
                        k = 2 * h + c
                        for kt in range(2):
                            ins = mm(PS[:, 6 + u % 2, c * P:(c + 1) * P], MV[:, kt, k * P:(k + 1) * P], PTx[:, u % 2, kt, :],
                                     start=kt == 0, stop=kt == 1)
                    ins.then_inc(*inc("pe_cx", ("o", u)))

        def scross_k():
            pe.wait_ge(*at("pool_cx", "q"))
            pe.wait_ge(*at("act_lin", ("unit", LAST[27])))
            for b in range(B):
                rows = slice(32 * (b // 2), 32 * (b // 2) + 32)
                pe.wait_ge(S.sem(f"mr{b}_in"), 16)
                for c in range(KC):
                    ins = mm(PS[rows, 0, 0:MEM], QX[:, b, c, :], MR[:, b, c * MEM:(c + 1) * MEM],
                             start=b % 2 == 0 and c == 0, stop=b % 2 == 1 and c == KC - 1, skip_group_check=True)
                ins.then_inc(*inc("pe_mr", ("k", b)))

        def scross_v():
            pe.wait_ge(*at("dve_cx", "ps"))
            pe.wait_ge(*at("act_cx", ("pt", len(CUNITS) - 1)))
            for kt in range(2):
                ins = tr(PS[:, 1, kt * P:(kt + 1) * P], SSx[:, kt * P:(kt + 1) * P], ident)
            ins.then_inc(*inc("pe_cx", "pts"))
            pe.wait_ge(*at("act_cx", "pts"))
            for b in range(B):
                pair, rows = slice(b // 2 * 32, b // 2 * 32 + 32), slice(32 * (b % 4), 32 * (b % 4) + 32)
                pe.wait_ge(S.sem(f"mr{b}_in"), 16 * 2)
                for half in range(2):
                    for kt in range(2):
                        a = kt * D + half * 512
                        ins = mm(PS[rows, 2 + 2 * (b // 4) + half, :], PTy[:, kt, pair], MR[:, b, a:a + 512],
                                 start=kt == 0, stop=kt == 1, skip_group_check=True)
                ins.then_inc(*inc("pe_mr", ("v", b)))
            pe.wait_ge(*at("dve_cx", ("o", len(CUNITS) - 1)))
            for j in range(2):
                pe.wait_ge(*at("act_cx", ("ox", j)))
            for c in range(KC):
                for j in range(2):
                    ins = tr(PS[:, (6 + c // 2) % 8, (c % 2 * 2 + j) * P:(c % 2 * 2 + j + 1) * P],
                             OX[:, j, c * P:(c + 1) * P], ident)
                if c % 2:
                    ins.then_inc(*inc("pe_cx", ("oxt", c // 2)))

        def residual(tiles):
            for t in tiles:
                m = TILES[t][1]
                for half in range(2):
                    ins = mm(PS[:, 2 + 2 * t + half, :], ident[0:m, :], X1[0:m, t, half * 512:(half + 1) * 512],
                             start=True, stop=False, skip_group_check=True)
            return ins

        def score(h):
            if h == 0:
                pe.wait_ge(S.sem("keys_in"), 16)
            else:
                pe.wait_ge(S.sem("act_s"), h)
            pe.wait_ge(*at("act_lin", ("unit", LAST[32 + h])))
            for c in range(2):
                for t in range(2):
                    mm(PS[:, 6, (2 * t + c) * NK:(2 * t + c + 1) * NK], qP(2 * h + c)[:, t * P:(t + 1) * P],
                       keys[:, 2 * h + c, :], start=True, stop=True)
                rows = slice(32 * (h // 2), 32 * (h // 2) + 32)
                ins = mm(PS[rows, 7, c * NK:(c + 1) * NK], qP(2 * h + c)[:, T:N], keys[:, 2 * h + c, :],
                         start=True, stop=True, skip_group_check=True)
            ins.then_inc(S.sem("pe_s"), 1)

        def peer():
            pe.wait_ge(S.sem("act_s"), NIT)
            residual([2])

            def rounds(t, it, j):
                for k in range(TOPK):
                    pe.wait_ge(S.sem(f"v{k % NR}_in"), (it * (TOPK // NR) + k // NR + 1) * 16)
                    pe.wait_ge(S.sem("act_dg"), it * TOPK + k + 1)
                    for half in range(2):
                        ins = mm(PS[:, 2 + 2 * t + half, :], dg[:, k % 4, :], VR[:, k % NR, half * 512:(half + 1) * 512],
                                 start=False, stop=False, skip_group_check=True)
                    ins.then_inc(S.sem("v_free"), 1)

            for t, it0, n in peer_tiles():
                if t < 2:
                    with pe.Fori(0, n // 2) as i:
                        for j in range(2):
                            rounds(t, i * 2 + (it0 + j), j)
                else:
                    for j in range(n):
                        rounds(t, it0 + j, j)
            pe.wait_ge(*at("dve_fin", "copy"))
            for half in range(2):
                ins = mm(PS[0:TS, half, :], cst("groupsum"), M["VR"][:, 0, half * 512:(half + 1) * 512],
                         start=True, stop=True)
            ins.then_inc(*inc("pe_fin", "sum"))

        pe.wait_ge(*at("dve_xT", 5))
        STAGES = {
            "lin": linear, "mem_turn": lambda: turn(3, 5), "fill": fill, "rw_pre": rw_pre, "rw_kk": rw_kk,
            "rw_vec": rw_vec, "rw_tile": rw_tile, "rw_scan": rw_scan, "rw_sample": rw_sample, "rw_out": rw_out,
            "attn": attn, "sgu": sgu, "sattn": sattn, "gnorm": gnorm, "norm": norm, "cross": cross,
            "scross_k": scross_k, "scross_v": scross_v, "score": score, "peer": peer}
        follow(STAGES)

    @block.scalar
    def _(act):
        A = nc.scalar.activation
        act.wait_ge(S.sem("const0_in"), 16)

        def norm_stat(first, end):
            for i in range(first, end):
                kind, t = NORMS0[i]
                m = rows_of(kind, t)
                act.wait_ge(S.sem(f"{kind}{t}_in"), 16)
                if i >= 2:
                    act.wait_ge(*at("act_sq", i - 2))
                A(YT[0:m].rearrange("p a b -> p (a b)")[:, i % 2 * D:(i % 2 + 1) * D],
                  M[kind][0:m, t, :], ACT.Square, accum_out=stat[0:m, i:i + 1]).then_inc(*inc("act_sq", i))
            for i in range(first, end):
                m = rows_of(*NORMS0[i])
                act.wait_ge(*at("act_sq", i))
                A(stat[0:m, 8 + i:9 + i], stat[0:m, i:i + 1], ACT.Sqrt, scale=1.0 / D,
                  bias=cst("eps", m, 1)).then_inc(*inc("act_rms", i))

        norm_stat(0, 3)
        taken = [LAST[3]]

        def catch_up(label):
            while taken[0] < paced[label]:
                evacuate_units(taken[0], taken[0] + 1)
                taken[0] += 1

        def fill(b):
            catch_up(("fill", b))

        def evacuate(b):
            if BLOCKS[b][0] not in ADDS:
                evacuate_units(LAST[b - 1] if b else 0, LAST[b])

        def evacuate_units(first, end):
            for u in range(first, end):
                b, cc, nn, t = UNITS[u]
                name = BLOCKS[b][0]
                c0 = BLOCKS[b][1] + cc
                act.wait_ge(*at("pe_lin", ("unit", u + 1)))
                src, scale = PS[:, u % 2, 0:N], 1.0
                if name == "w_in" and t is None:
                    j = c0 // P if c0 < 1536 else (c0 - 1796) // P + CU if c0 < 2052 else (c0 - 2308) // P + DQ
                    dst = hT[:, j, :]
                    scale = HD ** -0.5 if j in (BQ, BQ + 1, DQ, DQ + 1) else 1.0
                elif name == "ca_wq":
                    dst, scale = hX[:, c0 // P, :], 256 ** -0.5
                elif name == "peer_wq":
                    dst = qP(c0 // P)
                elif name == "w_in":
                    m = TILES[t][1]
                    off = {1536: TBV, 2052: TCV, 2820: TDV}[c0]
                    dst, src = hTok[0:m, t, off:off + nn], PS[0:m, u % 2, 0:nn]
                else:
                    k = u - LAST[11]
                    dst, src = stage[:, k % 2, :], PS[:, u % 2, 0:256]
                    if k >= 2:
                        act.wait_ge(S.sem(f"out_stage{k % 2}"), 16 * (k // 2))
                ins = A(dst, src, ACT.Copy, scale=scale)
                ins.then_inc(*inc("act_lin", ("unit", u + 1)))
                if 12 <= b < 20:
                    act.wait_ge(*at("act_lin", ("unit", u + 1)))
                    out = io["o_memk"][c0:c0 + P, :] if t is None else io["o_memv"][t * P:(t + 1) * P, c0:c0 + 256]
                    act.dma_start(out, stage[:, k % 2, :]).then_inc(S.sem(f"out_stage{k % 2}"), 16)

        def rw_pre():
            catch_up("xs")
            act.wait_ge(*at("dve_rw", "xs"))
            A(t1[0:64, 0, :], hT[0:64, 6, :], ACT.Tanh).then_inc(*inc("act_rw", "tanh"))
            A(t1[:, 1, :], hT[:, 7, :], ACT.Sigmoid).then_inc(*inc("act_rw", "sigg"))
            catch_up("tanh")
            for step, name, bank, dst in (("sigw", "w0", 2, lw), ("siga", "a0", 4, aa)):
                act.wait_ge(*at("pe_rw", "lora_w" if bank == 2 else "lora_a"))
                for c in range(2):
                    ins = A(dst[:, c, :], PS[:, bank + c, 0:N], ACT.Sigmoid, bias=col(name, c))
                ins.then_inc(*inc("act_rw", step))
            act.wait_ge(*at("pe_rw", "lora_g"))
            A(gg[:], PS[:, 6:8, 0:N], ACT.Copy).then_inc(*inc("act_rw", "g"))

        def rw_kk():
            catch_up("kksq")
            act.wait_ge(*at("dve_rw", "kkm"))
            A(t2, t2, ACT.Sqrt).then_inc(*inc("act_rw", "kkr"))
            act.wait_ge(*at("dve_rw", "Gx"))
            A(Pi, Gc, ACT.Exp, scale=-1.0).then_inc(*inc("act_rw", "Pi"))
            A(t1[:], t1[:], ACT.Exp).then_inc(*inc("act_rw", "Pex"))
            A(Pp, Gc, ACT.Exp).then_inc(*inc("act_rw", "P"))
            catch_up("bon")

        def rw_tile(t):
            m = TILES[t][1]

            def take(dst, bank, step):
                act.wait_ge(*at("pe_rw", (step, t)))
                A(quad(dst, m), PS[0:m, bank, 0:4 * m].rearrange("p (a b) -> p a b", a=4), ACT.Copy)\
                    .then_inc(*inc("act_rw", (step, t)))

            if t == 0:
                catch_up("kh")
            act.wait_ge(*at("pe_rw", ("tok", t)))
            if t:
                act.wait_ge(*at("pe_rw", ("mn", t - 1, 3)))
            A(TOK[0:m, 0, :], PS[0:m, 6, 0:GW], ACT.Copy)
            A(TOK[0:m, 1, :], PS[0:m, 6, GW:], ACT.Copy, scale=-1.0)
            A(TOK[0:m, 2:4, :], PS[0:m, 7, :].rearrange("p (a b) -> p a b", a=2), ACT.Copy)\
                .then_inc(*inc("act_rw", ("tok", t)))
            catch_up(("R0", t))
            take("PA", 2, "P2")
            if t < 2:
                take("PTA", 3, "P2T")
                catch_up(("P2T", t))
                take("PB", 5, "P4")
                take("PTB", 2, "P4T")
                catch_up(("P4T", t))
                take("PA", 4, "P8")
                catch_up(("P8", t))
                act.wait_ge(*at("pe_rw", ("R3", t)))
                catch_up(("R3", t))
                take("PTA", 5, "T16")
                take("PB", 4, "Q")
                catch_up(("Q", t))
            catch_up(("T", t))
            act.wait_ge(*at("pe_rw", ("wa", t)))
            A(WA[0:m], PS[0:m, 6, :].rearrange("p (a b) -> p a b", a=2), ACT.Copy).then_inc(*inc("act_rw", ("wa", t)))
            catch_up(("wa", t))
            act.wait_ge(*at("pe_rw", ("u0", t)))
            A(U0[0:m], PS[0:m, 7, 0:GW], ACT.Copy)
            A(U0n[0:m], PS[0:m, 7, 0:GW], ACT.Copy, scale=-1.0).then_inc(*inc("act_rw", ("u0n", t)))
            act.wait_ge(*at("pe_rw", ("y0", t)))
            t0 = TILES[t][0]
            A(Y0[:, :, t0:t0 + m], PS[:, 4, 0:2 * m].rearrange("p (a b) -> p a b", a=2), ACT.Copy)\
                .then_inc(*inc("act_rw", ("y0", t)))

        def rw_scan():
            for n in range(1, 8):
                catch_up(("st", n))

        def rw_out():
            for c in range(2):
                catch_up(("x", c))
            act.wait_ge(*at("dve_rw", "yc"))
            A(t1[:], Y0[:], ACT.Square).then_inc(*inc("act_rw", "ysq"))
            catch_up("ysq")
            act.wait_ge(*at("pe_rw", "var"))
            A(t2, PS[:, 2:4, 0:N], ACT.Sqrt, scale=1.0 / HD, bias=cst("eps")[:, 1:2]).then_inc(*inc("act_rw", "yrs"))
            catch_up("var")

        def log_forget():
            act.wait_ge(*at("dve_lf", "x"))
            for step, src, dst, kw in (("abs", 0, 12, {}), ("exp", 12, 12, {"scale": -1.0}), ("ln", 12, 12, {"bias": 1.0})):
                f = {"abs": ACT.Abs, "exp": ACT.Exp, "ln": ACT.Ln}[step]
                A(soft[:, dst:dst + 12], soft[:, src:src + 12], f, **kw).then_inc(*inc("act_lf", step))
                act.wait_ge(*now("act_lf"))

        def attn():
            for s in range(NA + 2):
                if s < NA:
                    w = P * (AUNITS[s][5] + 1)
                    act.wait_ge(*at("dve_at", ("sc", s)))
                    A(SC[:, s % 3, 0:w], SC[:, s % 3, 0:w], ACT.Exp, bias=soft[:, 24 + s % 2:25 + s % 2],
                      accum_out=soft[:, 26 + s % 2:27 + s % 2]).then_inc(*inc("act_at", ("p", s)))
                if s >= 2:
                    u = s - 2
                    w = P * (AUNITS[u][5] + 1)
                    act.wait_ge(*at("pe_at", ("pt", u)))
                    if u >= 2:
                        act.wait_ge(*at("pe_at", ("o", u - 2)))
                    A(PT[:, u % 2, :, :].rearrange("p a b -> p (a b)")[:, 0:w], PS[:, 4 + u % 2, 0:w], ACT.Copy)\
                        .then_inc(*inc("act_at", ("pt", u)))
                    catch_up(("p", u))

        def sgu():
            act.wait_ge(*at("dve_y", "a"))
            for t, (t0, m) in enumerate(TILES):
                A(VL[0:m, t, :], hTok[0:m, t, TCV:TCV + GW], ACT.Gelu, accum_out=soft[0:m, 32 + t:33 + t])\
                    .then_inc(*inc("act_sg", ("v", t)))
            A(hT[:, CU:CU + 2, :], hT[:, CU:CU + 2, :], ACT.Gelu).then_inc(*inc("act_sg", "u"))
            for t, (t0, m) in enumerate(TILES):
                catch_up(("sg", t))
                act.wait_ge(*at("dve_sg", ("var", t)))
                A(soft[0:m, 44 + t:45 + t], soft[0:m, 38 + t:39 + t], ACT.Sqrt, scale=1.0 / GW,
                  bias=cst("eps", m, 1)).then_inc(*inc("act_sg", ("rms", t)))

        def sattn():
            for g in range(2):
                act.wait_ge(*at("dve_sa", ("sc", g)))
                A(SS[:, g, :], SS[:, g, :], ACT.Exp, bias=soft[:, 48 + g:49 + g], accum_out=soft[:, 50 + g:51 + g])\
                    .then_inc(*inc("act_sa", ("p", g)))
            for g in range(2):
                act.wait_ge(*at("pe_sa", ("pt", g)))
                A(PTs[:, g, 0:2, :].rearrange("p a b -> p (a b)"), PS[:, 4 + g, 0:2 * P], ACT.Copy)
                A(PTs[0:TS, g, 2, :], PS[0:TS, 4 + g, 2 * P:3 * P], ACT.Copy).then_inc(*inc("act_sa", ("pt", g)))
            for g in range(2):
                act.wait_ge(*at("pe_sa", ("o", g)))
                A(M["OS"][:, g, :], PS[:, 6 + g, :], ACT.Copy).then_inc(*inc("act_sa", ("o", g)))

        def gnorm(groups):
            for g in groups:
                act.wait_ge(*(at("dve_y", "a"), at("dve_y", "b"), at("dve_sg", ("y", 2)), at("dve_y", "d"))[g])
                A(M["SQ"][:, g // 2 * 2:g // 2 * 2 + 2, :], YT[:, 2 * g:2 * g + 2, :], ACT.Square).then_inc(*inc("act_gn", ("sq", g)))
            for g in groups:
                act.wait_ge(*at("pe_gn", g))
                A(M["RS"][:, g, :], PS[:, GN_BANK[g], 0:N], ACT.Sqrt, scale=1.0 / GW, bias=cst("eps")[:, 0:1])\
                    .then_inc(*inc("act_gn", ("rms", g)))

        def norm(i):
            for t, (t0, m) in enumerate(TILES):
                act.wait_ge(*((S.sem("dve_lin"), 12 * i + 10 + t) if t < 2 else at("dve_part", i)))
                A(XN[0:m, t, :], X1[0:m, t, :], ACT.Square, accum_out=softx[0:m, t:t + 1]).then_inc(*inc("act_nq", (i, t)))
            for t, (t0, m) in enumerate(TILES):
                act.wait_ge(*at("act_nq", (i, t)))
                A(softx[0:m, 3 + t:4 + t], softx[0:m, t:t + 1], ACT.Sqrt, scale=1.0 / D, bias=cst("eps", m, 1))\
                    .then_inc(*inc("act_nr", (i, t)))
            for t, (t0, m) in enumerate(TILES):
                for half in range(2):
                    act.wait_ge(*at("pe_nx", (i, t, half)))
                    A(xT[:, 4 * half:4 * half + 4, t0:t0 + m],
                      PS[:, 2 + 2 * t + half, :].rearrange("p (k m) -> p k m", k=4)[:, :, 0:m], ACT.Copy)\
                        .then_inc(*inc("act_nx", (i, t, half)))

        def cross():
            nu = len(CUNITS)
            for s in range(nu + 2):
                if s < nu:
                    act.wait_ge(*at("dve_cx", ("mx", s)))
                    if s >= 3:
                        act.wait_ge(*at("pe_cx", ("pt", s - 3)))
                    A(SCx[:, s % 3, :], PS[:, 2 + s % 2, 0:MEM], ACT.Exp, bias=softx[:, 8 + s % 2:9 + s % 2],
                      accum_out=softx[:, 10 + s % 2:11 + s % 2]).then_inc(*inc("act_cx", ("p", s)))
                if s >= 2:
                    u = s - 2
                    act.wait_ge(*at("pe_cx", ("pt", u)))
                    if u >= 2:
                        act.wait_ge(*at("pe_cx", ("o", u - 2)))
                    A(PTx[:, u % 2, :, :].rearrange("p a b -> p (a b)"), PS[:, 4 + u % 2, 0:2 * P], ACT.Copy)\
                        .then_inc(*inc("act_cx", ("pt", u)))

        def scross_k():
            act.wait_ge(*at("dve_cx", "mxs"))
            A(SSx[:], PS[:, 0, 0:MEM], ACT.Exp, bias=softx[:, 16:17], accum_out=softx[:, 17:18])\
                .then_inc(*inc("act_cx", "p_s"))

        def scross_v():
            act.wait_ge(*at("pe_cx", "pts"))
            A(PTy[:].rearrange("p a b -> p (a b)"), PS[:, 1, 0:2 * P], ACT.Copy).then_inc(*inc("act_cx", "pts"))
            for j in range(2):
                act.wait_ge(*at("pe_mr", ("v", 4 * j + 3)))
                A(OX[:, j, :].rearrange("p (a n) -> p a n", a=2), PS[:, 2 + 2 * j:4 + 2 * j, :], ACT.Copy)\
                    .then_inc(*inc("act_cx", ("ox", j)))

        def score(h):
            act.wait_ge(S.sem("pe_s"), h + 1)
            rows = slice(32 * (h // 2), 32 * (h // 2) + 32)
            A(SA[rows, 16 + h % 2, :, :].rearrange("p a b -> p (a b)"), PS[rows, 7, 0:2 * NK], ACT.Copy)
            A(SA[:, h:h + 9:8, :, :].rearrange("p t a b -> p t (a b)"), PS[:, 6, :].rearrange("p (t n) -> p t n", t=2),
              ACT.Copy).then_inc(S.sem("act_s"), 1 if h < 7 else NIT - 7)
            if h == 5:
                gate(0, 0)

        def gate(it, par):
            act.wait_ge(S.sem("topk_done"), it + 1)
            A(M["ge"][:, par, :], M["bs"][:, par, :], ACT.Exp, bias=M["gs"][:, par:par + 1],
              accum_out=M["gs"][:, 2 + par:3 + par]).then_inc(S.sem("act_g"), 1)
            act.wait_ge(S.sem("u_free"), it * TOPK + NR + TOPK)
            A(M["gl"][:, par, :], M["act"][:, par, :], ACT.Gelu).then_inc(S.sem("act_gl"), 1)

        def peer():
            def weights(it, par):
                act.wait_ge(S.sem("dve_w"), it + 1)
                for k in range(TOPK):
                    act.wait_ge(S.sem("v_free"), it * TOPK + (k + NR - 3))
                    A(dg[:, k % 4, :], ident, ACT.Copy, scale=M["wv"][:, par, k:k + 1]).then_inc(S.sem("act_dg"), 1)

            def finish(t):
                src = PS[:, 2 + 2 * t:4 + 2 * t, :] if t < 2 else PS[0:TS, 0:2, :]
                m = TILES[t][1]
                if t < 2:
                    act.wait_ge(S.sem("v_free"), NR + P * (t + 1))
                else:
                    act.wait_ge(*at("pe_fin", "sum"))
                A(XN[0:m, t, :].rearrange("p (a b) -> p a b", a=2), src, ACT.Square,
                  accum_out=M["gs"][0:m, 4 + t:5 + t]).then_inc(*inc("act_fin", ("sq", t)))
                act.wait_ge(*now("act_fin"))
                A(M["gs"][0:m, 8 + t:9 + t], M["gs"][0:m, 4 + t:5 + t], ACT.Sqrt, scale=1.0 / D, bias=cst("eps", m, 1))\
                    .then_inc(*inc("act_fin", ("rms", t)))

            for t, it0, n in peer_tiles():
                if t < 2:
                    with act.Fori(0, n // 2) as i:
                        for j in range(2):
                            weights(i * 2 + (it0 + j), j)
                            gate(i * 2 + (it0 + j + 1), 1 - j)
                else:
                    for j in range(n):
                        finish(j)
                        weights(it0 + j, j)
                        if j == 0:
                            gate(it0 + 1, 1)
            finish(2)

        STAGES = {
            "lin": evacuate, "mem_stat": lambda: norm_stat(3, 5), "fill": fill, "rw_pre": rw_pre, "rw_kk": rw_kk,
            "rw_tile": rw_tile, "rw_scan": rw_scan, "rw_out": rw_out, "lf": log_forget, "attn": attn, "sgu": sgu,
            "sattn": sattn, "gnorm": gnorm, "norm": norm, "cross": cross, "scross_k": scross_k,
            "scross_v": scross_v, "score": score, "peer": peer}
        follow(STAGES)
        nst = LAST[19] - LAST[11]
        for j in range(2):
            act.wait_ge(S.sem(f"out_stage{j}"), 16 * ((nst + 1 - j) // 2))

    @block.vector
    def _(dve):
        V = nc.vector
        dve.wait_ge(S.sem("cols_in"), 16)

        def feature_major(n, kind, t, dst, gain, done):
            m = rows_of(kind, t)
            t0 = TILES[t][0]
            for half in range(2):
                dve.wait_ge(*at("pe_xT", n + half))
                V.tensor_tensor(dst[:, 4 * half:4 * half + 4, t0:t0 + m],
                                xpose_bank(n + half).rearrange("p (k m) -> p k m", k=4)[:, :, 0:m],
                                colb(gain, 4 * half, 4 * half + 4, m), ALU.mult).then_inc(*inc(done, n + half))

        def normed(i):
            kind, t = NORMS0[i]
            m = rows_of(kind, t)
            dve.wait_ge(*at("act_rms", i))
            V.reciprocal(stat[0:m, 16 + i:17 + i], stat[0:m, 8 + i:9 + i]).then_inc(*inc("dve_rstd", i))
            dve.wait_ge(*at("dve_rstd", i))
            if i >= 2:
                dve.wait_ge(*at("pe_xT", 2 * i - 3))
            V.tensor_scalar(M["xn"][0:m, i % 2, :], M[kind][0:m, t, :], stat[0:m, 16 + i:17 + i], None, ALU.mult)\
                .then_inc(*inc("dve_xn", (kind, t)))

        for first, end in ((0, 3), (3, 5)):
            normed(first)
            for i in range(first + 1, end + 1):
                if i < end:
                    normed(i)
                kind, t = NORMS0[i - 1]
                feature_major(2 * i - 2, kind, t, M["xT"] if kind == "x" else M["xmT"], "g0" if kind == "x" else "gm",
                              "dve_xT")

        def link(ins, sem="dve_seq", step=None):
            ins.then_inc(*inc(sem, step))
            dve.wait_ge(*now(sem))

        TT = V.tensor_tensor
        STT = V.scalar_tensor_tensor
        dve.wait_ge(S.sem("pt_in"), 16)
        dve.wait_ge(S.sem("const_in"), 16)
        link(V.tensor_scalar(M["idx"][:], M["pt"][:], float(PAGE), cst("prow"), ALU.mult, ALU.add), "dve_sa", "idx")

        def rw_pre():
            pa = hT[:, 0:8, :]
            dve.wait_ge(*at("act_lin", ("unit", LAST[3])))
            dve.wait_ge(S.sem("rwp_in"), 16 * 5)
            V.tensor_copy(M["shiftc"][:, :, 0:1], pa[:, :, T - 1:T])
            link(V.tensor_copy(M["shiftc"][:, :, 1:], pa[:, :, T + Q - 1::Q]), "dve_rw", "shiftc")
            TT(dlt[:, :, 1:T], pa[:, :, 0:T - 1], pa[:, :, 1:T], ALU.subtract)
            V.tensor_scalar(dlt[:, :, 0:1], pa[:, :, 0:1], -1.0, None, ALU.mult)
            ds, ps = (a[:, :, T:N].rearrange("p c (b q) -> p c b q", q=Q) for a in (dlt, pa))
            TT(ds[:, :, :, 1:Q], ps[:, :, :, 0:Q - 1], ps[:, :, :, 1:Q], ALU.subtract)
            link(TT(ds[:, :, :, 0], M["shift"][:], ps[:, :, :, 0], ALU.subtract))
            for c in (6, 7, 2, 3, 0, 1, 4, 5):
                ins = STT(hT[:, c, :], dlt[:, c, :], col("mu", c), hT[:, c, :], ALU.mult, ALU.add)
            link(ins, "dve_rw", "xs")

        def rw_kk():
            for c in range(2):
                ins = V.tensor_scalar(kk[:, c, :], kT[:, c, :], col("kks", c), None, ALU.mult)
            link(ins)
            TT(t2, kk[:], kk[:], ALU.mult).then_inc(*inc("dve_rw", "kksq"))
            dve.wait_ge(*at("act_rw", "sigw"))
            link(V.tensor_scalar(lw[:], lw[:], -float(np.exp(-0.5)), None, ALU.mult))
            for c in range(2):
                ins = V.tensor_tensor_scan(Gc[:, c, :], cst("reset"), lw[:, c, :], 0.0, ALU.mult, ALU.add)
            link(ins)
            dve.wait_ge(*at("pe_rw", "lora_g"))
            TT(t1[:], Gc, lw[:], ALU.subtract).then_inc(*inc("dve_rw", "Gx"))
            dve.wait_ge(*at("pe_rw", "kkn"))
            V.tensor_scalar(t2, PS[:, 2:4, 0:N], 1e-24, None, ALU.max).then_inc(*inc("dve_rw", "kkm"))
            dve.wait_ge(*at("act_rw", "siga"))
            for c in range(2):
                ins = V.tensor_scalar(kp[:, c, :], aa[:, c, :], -1.0, col("ka", c), ALU.add, ALU.mult)
            link(ins)
            link(STT(kp[:], kp[:], 1.0, kT, ALU.add, ALU.mult))
            dve.wait_ge(*at("act_rw", "kkr"))
            link(V.reciprocal(t2, t2))
            link(TT(kk[:], kk[:], t2, ALU.mult))
            link(TT(bh[:], kk[:], aa[:], ALU.mult))
            for c in range(2):
                ins = STT(t2[:, c, :], rT[:, c, :], col("rk", c), kp[:, c, :], ALU.mult, ALU.mult)
            ins.then_inc(*inc("dve_rw", "bon"))

        def rw_vec():
            dve.wait_ge(*at("act_rw", "Pi"))
            TT(bh[:], bh[:], Pi, ALU.mult)
            TT(kh[:], kp[:], Pi, ALU.mult)
            dve.wait_ge(*at("act_rw", "P"))
            TT(KR[:, :, 0, :], t1[:], kk[:], ALU.mult)
            TT(KR[:, :, 1, :], Pp, rT, ALU.mult).then_inc(*inc("dve_rw", "kh"))
            dve.wait_ge(*at("pe_rw", "bonus"))
            link(TT(aa[:], PS[:, 4:6, 0:N], vT, ALU.mult), "dve_rw", "bonus")

        def rw_tile(t):
            t0, m = TILES[t]
            a1t, a3t, a2t, a4t, a16, off = tile_mats(t)
            prompt = t < 2
            R = quad("R", m)

            def masked(dst, bank, mask, step):
                dve.wait_ge(*at("pe_rw", (step, t)))
                for par in range(2):
                    ins = TT(dst[:, 2 * par:2 * par + 2, :],
                             PS[0:m, bank + par, 0:4 * m].rearrange("p (c s) -> p c s", c=2),
                             cst(mask, m).unsqueeze(1).to_broadcast([m, 2, 2 * m]), ALU.mult)
                return ins

            if t:
                dve.wait_ge(*at("pe_rw", ("y0", t - 1)))
            ins = masked(M["AB"] if prompt else M["sAB"], 2, "m_ab" if prompt else "s_ab", "x1")
            link(ins)
            TT(R, ident[0:m, 0:m].unsqueeze(1).to_broadcast([m, 4, m]),
               (M["AB"] if prompt else M["sAB"])[:, :, 0:m], ALU.subtract)
            masked(M["AK"] if prompt else M["sAK"], 4, "m_ak" if prompt else "s_ab", "x2")
            dve.wait_ge(*at("pe_rw", ("x3", t)))
            for par in range(2):
                src = PS[0:m, 6 + par, 0:2 * m].rearrange("p (c s) -> p c s", c=2)
                if prompt:
                    for half in range(2):
                        ins = TT(M["A1"][:, 2 * par:2 * par + 2, half * P:(half + 1) * P], src,
                                 cst("m_a")[:, half * P:(half + 1) * P].unsqueeze(1).to_broadcast([P, 2, P]), ALU.mult)
                else:
                    ins = TT(M["sA1"][:, 2 * par:2 * par + 2, :], src,
                             cst("s_a", m).unsqueeze(1).to_broadcast([m, 2, m]), ALU.mult)
            link(ins, "dve_rw", ("R0", t))

            def add_R(bank, step, done, op=ALU.add):
                dve.wait_ge(*at("pe_rw", (step, t)))
                link(TT(R, R, PS[0:m, bank, 0:4 * m].rearrange("p (a b) -> p a b", a=4), op), "dve_rw", (done, t))

            if prompt:
                add_R(4, "R1", "R1")
                add_R(3, "R2", "R2")
                add_R(2, "R3", "R3")
                add_R(3, "Z", "T", ALU.subtract)
            else:
                add_R(4, "R1", "T")
            dve.wait_ge(*at("pe_rw", ("yl", t)))
            TT(YLT[:, :, t0:t0 + m], KR[:, :, 1, t0:t0 + m],
               PS[:, 5, 0:2 * m].rearrange("p (a b) -> p a b", a=2), ALU.subtract).then_inc(*inc("dve_rw", ("yl", t)))
            if not prompt:
                return
            if t == 0:
                dve.wait_ge(*at("pool_rw", "zero"))
            for cc in range(4):
                bank = (2, 3, 6, 7)[cc]
                n = 4 * t + cc
                dve.wait_ge(*at("pe_rw", ("mn", t, cc)))
                for ph in (slice(0, HD), slice(HD, P)):
                    TT(MT[ph, n, :, ph], PS[ph, bank, 0:P].rearrange("p (c j) -> p c j", c=2),
                       ident[ph, ph].unsqueeze(1).to_broadcast([HD, 2, HD]), ALU.add)
                last = t0 + cc * CH + CH - 1
                ins = TT(NPr[:, n, :, :], PS[:, bank, P:2 * P].rearrange("p (c j) -> p c j", c=2),
                         Pp[:, :, last:last + 1].to_broadcast([P, 2, HD]), ALU.mult)
            link(ins, "dve_rw", ("mn", t))

        def rw_scan():
            for n in range(8):
                dve.wait_ge(*at("pe_rw", ("st", n)))
                for c in range(2):
                    last = n * CH + CH - 1
                    ins = STT(ST[:, n + 1, c, :], PS[:, 2 + n % 2, c * HD:(c + 1) * HD], Pp[:, c, last:last + 1],
                              NPr[:, n, c, :], ALU.mult, ALU.add)
                link(ins, "dve_st", n)

        def rw_sample():
            for c in range(2):
                dve.wait_ge(*at("pe_rw", ("smn", c)))
                for ph in (slice(0, HD), slice(HD, P)):
                    TT(MT[ph, :, c, ph], PS[ph, 2 + c, :].rearrange("p (b j) -> p b j", b=B),
                       ident[ph, ph].unsqueeze(1).to_broadcast([HD, B, HD]), ALU.add)
                pl = Pp[:, c, T + Q - 1::Q].unsqueeze(2).to_broadcast([P, B, HD])
                TT(NPr[:, :, c, :], PS[:, 6 + c, :].rearrange("p (b j) -> p b j", b=B), pl, ALU.mult)\
                    .then_inc(*inc("dve_rw", ("smn", c)))
            for c in range(2):
                dve.wait_ge(*at("pe_rw", ("ss", c)))
                tmp = M["PTB"][:].rearrange("p a b -> p (a b)").rearrange("p (b j) -> p b j", b=B)
                pl = Pp[:, c, T + Q - 1::Q].unsqueeze(2).to_broadcast([P, B, HD])
                link(TT(tmp, PS[:, 4 + c, :].rearrange("p (b j) -> p b j", b=B), pl, ALU.mult))
                link(TT(NPr[:, :, c, :], NPr[:, :, c, :], tmp, ALU.add), "dve_rw", "swkv" if c else "swkv0")

        def rw_out():
            dve.wait_ge(*at("act_rw", ("y0", 2)))
            dve.wait_ge(*at("pe_rw", "yst"))
            for par in range(2):
                ph = slice(par * HD, par * HD + HD)
                TT(Y0[ph, :, 0:T], Y0[ph, :, 0:T], PS[ph, 2 + par, :].rearrange("p (c t) -> p c t", c=2), ALU.add)
            dve.wait_ge(*at("pe_rw", "yss"))
            for par in range(2):
                ph = slice(par * HD, par * HD + HD)
                ins = TT(Y0[ph, :, T:N], Y0[ph, :, T:N],
                         PS[ph, 6 + par, 0:2 * TS].rearrange("p (c t) -> p c t", c=2), ALU.add)
            link(ins, "dve_rw", "y")
            dve.wait_ge(*at("pe_rw", "mean"))
            link(STT(Y0[:], PS[:, 4:6, 0:N], -1.0 / HD, Y0[:], ALU.mult, ALU.add), "dve_rw", "yc")
            dve.wait_ge(*at("act_rw", "yrs"))
            link(V.reciprocal(t2, t2))
            link(TT(Y0[:], Y0[:], t2, ALU.mult))
            for c in range(2):
                ins = V.tensor_scalar(Y0[:, c, :], Y0[:, c, :], col("lnw", c), col("lnb", c), ALU.mult, ALU.add)
            link(ins)
            link(TT(Y0[:], Y0[:], aa[:], ALU.add))
            link(TT(YT[:, 0:2, :], Y0[:], gg[:], ALU.mult), "dve_y", "a")

        def log_forget():
            dve.wait_ge(*at("act_lin", ("unit", LAST[6])))
            dve.wait_ge(S.sem("rows_in"), 16 * 3)
            x = soft[:, 0:12].rearrange("p (t h) -> p t h", h=4)
            link(V.memset(soft[:, 0:12], 0.0))
            bf = M["rows"][:, 512:516]
            TT(x[:, 0:2, :], hTok[:, 0:2, TLF:TLF + 4], bf.unsqueeze(1).to_broadcast([P, 2, 4]), ALU.add)
            link(TT(x[0:TS, 2, :], hTok[0:TS, 2, TLF:TLF + 4], bf[0:TS], ALU.add), "dve_lf", "x")
            dve.wait_ge(*at("act_lf", "ln"))
            STT(lf[:].rearrange("p t h -> p (t h)"), soft[:, 0:12], 0.0, soft[:, 12:24], ALU.min, ALU.subtract)\
                .then_inc(*inc("dve_lf", "lf"))
            dve.wait_ge(*now("dve_lf"))

        def attn():
            for s in range(NA + 3):
                if s < NA:
                    qc, _, _, _, h, qb = AUNITS[s]
                    w = P * (qb + 1)
                    if qc == BQ:
                        if s >= 2:
                            dve.wait_ge(*at("pe_at", ("sc", s - 2)))
                        if qb == 0:
                            ins = V.tensor_scalar(LFU[:, s % 2, 0, :], upinc, lf[:, 0, h:h + 1], None, ALU.mult)
                        else:
                            V.tensor_scalar(LFU[:, s % 2, 0, :], ones, lf[:, 0, h:h + 1], None, ALU.mult)
                            ins = V.tensor_scalar(LFU[:, s % 2, 1, :], upinc, lf[:, 1, h:h + 1], None, ALU.mult)
                        ins.then_inc(*inc("dve_at", ("lfu", s)))
                        bias = cst("caus")[:, 256 - w:256]
                    else:
                        bias = cst(f"d_bias{h}{qb}")
                    dve.wait_ge(*at("pe_at", ("sc", s)))
                    if s >= 3:
                        dve.wait_ge(*at("pe_at", ("pt", s - 3)))
                    link(TT(SC[:, s % 3, 0:w], PS[:, 2 + s % 2, 0:w], bias, ALU.add))
                    link(V.tensor_reduce(soft[:, 24 + s % 2:25 + s % 2], SC[:, s % 3, 0:w], X, ALU.max, negate=True),
                         "dve_at", ("sc", s))
                if 1 <= s <= NA:
                    u = s - 1
                    w = P * (AUNITS[u][5] + 1)
                    dve.wait_ge(*at("act_at", ("p", u)))
                    link(V.reciprocal(soft[:, 28 + u % 2:29 + u % 2], soft[:, 26 + u % 2:27 + u % 2]))
                    V.tensor_scalar(SC[:, u % 3, 0:w], SC[:, u % 3, 0:w], soft[:, 28 + u % 2:29 + u % 2], None, ALU.mult)\
                        .then_inc(*inc("dve_at", ("p", u)))
                if s >= 3:
                    u = s - 3
                    _, _, _, yc, h, qb = AUNITS[u]
                    ph = slice(HD * (h % 2), HD * (h % 2) + HD)
                    dve.wait_ge(*at("pe_at", ("o", u)))
                    V.tensor_copy(YT[ph, yc + h // 2, qb * P:(qb + 1) * P], PS[ph, 6 + u % 2, 0:P])\
                        .then_inc(*inc("dve_at", ("o", u)))

        def sgu():
            dve.wait_ge(S.sem("sgu_in"), 16 * 3)
            for h in range(4):
                V.tensor_tensor(M["wm"][:, h, :], M["wm"][:, h, :], upinc, ALU.mult)
            link(TT(M["wm4"][:], M["wm4"][:], cst("s_ab", TS)[:, TS:].unsqueeze(1).to_broadcast([TS, 4, TS]), ALU.mult))
            for t, (t0, m) in enumerate(TILES):
                v = VL[0:m, t, :]
                junk = M["sg"][0:m].rearrange("p a b -> p (a b)")
                dve.wait_ge(*at("act_sg", ("v", t)))
                link(V.tensor_scalar(soft[0:m, 36:37], soft[0:m, 32 + t:33 + t], 1.0 / GW, None, ALU.mult))
                link(V.tensor_scalar(v, v, soft[0:m, 36:37], None, ALU.subtract))
                link(V.tensor_tensor_reduce(out=junk, in0=v, in1=v, scale=1.0, scalar=0.0, op0=ALU.mult, op1=ALU.add,
                                            accum_out=soft[0:m, 38 + t:39 + t]), "dve_sg", ("var", t))
                dve.wait_ge(*at("act_sg", ("rms", t)))
                link(V.reciprocal(soft[0:m, 42:43], soft[0:m, 44 + t:45 + t]))
                link(STT(v, v, soft[0:m, 42:43], M["rows"][0:m, 0:GW], ALU.mult, ALU.mult))
                link(TT(v, v, M["rows"][0:m, GW:2 * GW], ALU.add), "dve_sg", ("v", t))
            dve.wait_ge(*at("act_sg", "u"))
            for t, (t0, m) in enumerate(TILES):
                dve.wait_ge(*at("pe_sg", t))
                mix = PS[:, 2 + t % 2, 0:2 * m].rearrange("p (c t) -> p c t", c=2)
                if t < 2:
                    link(TT(M["sg"][:, :, 0:m], mix, M["bsr"][:], ALU.add))
                else:
                    for c in range(2):
                        ins = TT(M["sg"][:, c, 0:m].rearrange("p (b q) -> p b q", q=Q),
                                 mix[:, c, :].rearrange("p (b q) -> p b q", q=Q),
                                 M["bsr"][:, c, 0:Q].unsqueeze(1).to_broadcast([P, B, Q]), ALU.add)
                    link(ins)
                link(TT(YT[:, 4:6, t0:t0 + m], M["sg"][:, :, 0:m], hT[:, CU:CU + 2, t0:t0 + m], ALU.mult),
                     "dve_sg", ("y", t))

        def own_rows(dst, src, h, odd):
            a = 48 * odd + h * Q
            return V.tensor_copy(dst.rearrange("p (j a o t) -> p j a o t", j=2, a=2, o=2)[:, :, :, odd, :],
                                 src.rearrange("p j (a x) -> p j a x", a=2)[:, :, :, a:a + Q])

        def sattn():
            dve.wait_ge(S.sem("glf_in"), 16 * 16)
            lfg = M["lfg"][:].rearrange("p (b g) h -> p b g h", g=2)
            for pg in range(2):
                V.tensor_copy(M["LFP"][:, pg, :].rearrange("p (b h t) -> p b h t", b=B, h=4),
                              lfg[:, :, pg, :].unsqueeze(3).to_broadcast([P, B, 4, Q]))
            for b in range(B):
                ins = TT(M["LFN"][:, b * 16:(b + 1) * 16].rearrange("p (h t) -> p h t", h=4),
                         lf[0:TS, 2, :].unsqueeze(2).to_broadcast([TS, 4, Q]),
                         cst("lf_new_l", TS)[:, b * 16:(b + 1) * 16].rearrange("p (h t) -> p h t", h=4), ALU.mult)
            link(ins, "dve_sa", "lfn")
            for g, bias in enumerate(("sb_bias", "sd_bias")):
                dve.wait_ge(*at("pe_sa", ("sc", g)))
                link(TT(SS[:, g, :], PS[:, 2 + g, 0:PAST + TS], cst(bias), ALU.add))
                link(V.tensor_reduce(soft[:, 48 + g:49 + g], SS[:, g, :], X, ALU.max, negate=True), "dve_sa", ("sc", g))
            for g in range(2):
                dve.wait_ge(*at("act_sa", ("p", g)))
                link(V.reciprocal(soft[:, 52 + g:53 + g], soft[:, 50 + g:51 + g]))
                V.tensor_scalar(SS[:, g, :], SS[:, g, :], soft[:, 52 + g:53 + g], None, ALU.mult)\
                    .then_inc(*inc("dve_sa", ("p", g)))
            for g, yc in enumerate((2, 6)):
                dve.wait_ge(*at("pe_sa", ("ot", g)))
                for par in range(2):
                    ph = slice(HD * par, HD * par + HD)
                    for c in range(2):
                        for odd in range(2):
                            ins = own_rows(YT[ph, yc + c, T:N], PS[ph, 4 + g, :].rearrange("p (j c x) -> p j c x", j=2, c=2)
                                           [:, :, c, :], 2 * c + par, odd)
                link(ins, "dve_y", "bd"[g])

        def gnorm(groups):
            for g in groups:
                dve.wait_ge(*at("act_gn", ("rms", g)))
                link(V.reciprocal(M["RS"][:, g, :], M["RS"][:, g, :]))
                for j in range(2):
                    k = 2 * g + j
                    ins = STT(YT[:, k, :], YT[:, k, :], col("gout", k), M["RS"][:, g, :], ALU.mult, ALU.mult)
                ins.then_inc(*inc("dve_gn", g))

        def linear_add(b):
            if BLOCKS[b][0] not in ADDS:
                return
            if b == 20:
                dve.wait_ge(S.sem("X1_in"), 16 * 3)
            for u in range(LAST[b - 1], LAST[b]):
                _, cc, nn, t = UNITS[u]
                m, c0 = TILES[t][1], BLOCKS[b][1]
                dve.wait_ge(*at("pe_lin", ("unit", u + 1)))
                if t < 2:
                    x = X1[:, t, c0:c0 + nn]
                    TT(x, x, PS[:, u % 2, 0:nn], ALU.add).then_inc(S.sem("dve_lin"), 1)
                else:
                    V.tensor_copy(PART[:, c0:c0 + nn], PS[:, u % 2, 0:nn]).then_inc(S.sem("dve_lin"), 1)
            if b in (23, 31):
                dve.wait_ge(*at("pe_part", b // 28))
                x = X1[0:TS, 2, :].rearrange("p (a n) -> p a n", a=2)
                TT(x, x, PS[0:TS, 2:4, :], ALU.add).then_inc(*inc("dve_part", b // 28))

        def norm(i):
            if i == 0:
                dve.wait_ge(S.sem("gr_in"), 16 * 3)
            for t, (t0, m) in enumerate(TILES):
                dve.wait_ge(*at("act_nr", (i, t)))
                link(V.reciprocal(softx[0:m, 24 + t:25 + t], softx[0:m, 3 + t:4 + t]))
                STT(XN[0:m, t, :], X1[0:m, t, :], softx[0:m, 24 + t:25 + t], gr[0:m, i, :], ALU.mult, ALU.mult)\
                    .then_inc(*inc("dve_nx", (i, t)))

        def cross():
            nu = len(CUNITS)
            for s in range(nu + 3):
                if s < nu:
                    dve.wait_ge(*at("pe_cx", ("sc", s)))
                    V.tensor_reduce(softx[:, 8 + s % 2:9 + s % 2], PS[:, 2 + s % 2, 0:MEM], X, ALU.max, negate=True)\
                        .then_inc(*inc("dve_cx", ("mx", s)))
                if 1 <= s <= nu:
                    u = s - 1
                    dve.wait_ge(*at("act_cx", ("p", u)))
                    link(V.reciprocal(softx[:, 12 + u % 2:13 + u % 2], softx[:, 10 + u % 2:11 + u % 2]))
                    V.tensor_scalar(SCx[:, u % 3, :], SCx[:, u % 3, :], softx[:, 12 + u % 2:13 + u % 2], None, ALU.mult)\
                        .then_inc(*inc("dve_cx", ("p", u)))
                if s >= 3:
                    u = s - 3
                    h, qb = CUNITS[u]
                    dve.wait_ge(*at("pe_cx", ("o", u)))
                    V.tensor_copy(YT[:, 2 * h:2 * h + 2, qb * P:(qb + 1) * P],
                                  PS[:, 6 + u % 2, 0:2 * P].rearrange("p (c q) -> p c q", c=2))\
                        .then_inc(*inc("dve_cx", ("o", u)))

        def scross_k():
            dve.wait_ge(*at("pe_mr", ("k", B - 1)))
            V.tensor_reduce(softx[:, 16:17], PS[:, 0, 0:MEM], X, ALU.max, negate=True).then_inc(*inc("dve_cx", "mxs"))
            dve.wait_ge(*at("act_cx", "p_s"))
            link(V.reciprocal(softx[:, 18:19], softx[:, 17:18]))
            V.tensor_scalar(SSx[:], SSx[:], softx[:, 18:19], None, ALU.mult).then_inc(*inc("dve_cx", "ps"))

        def scross_v():
            for c in range(KC):
                if c % 2 == 0:
                    dve.wait_ge(*at("pe_cx", ("oxt", c // 2)))
                for odd in range(2):
                    ins = own_rows(YT[:, c, T:N], PS[:, (6 + c // 2) % 8, c % 2 * 2 * P:(c % 2 + 1) * 2 * P]
                                   .rearrange("p (j x) -> p j x", j=2), c // 2, odd)
            ins.then_inc(*inc("dve_cx", "ys"))

        def peer():
            cur, cur2, cand, cand2, eq, ts, ti, tif, bj, bji, bjf, ef, idxu, idxv, bs, gs = (
                M[k] for k in ("cur", "cur2", "cand", "cand2", "eq", "ts", "ti", "tif", "bj", "bji", "bjf", "ef",
                               "idxu", "idxv", "bs", "gs"))
            linked = dve.alloc_register("linked")
            dve.wait_ge(*at("dve_cx", "ys"))
            V.memset(gs[:], 0.0).then_inc(S.sem("u_free"), NR)

            def topk(n, par, then):
                dve.wait_ge(S.sem("act_s"), n + 1)
                then(V.tensor_copy(cur[:].rearrange("p a b -> p (a b)"),
                                   SA[:].rearrange("p n a b -> p (n a b)")[:, bass.ds(n * 2 * NK, 2 * NK)]))
                for c in range(2):
                    ins = V.max(ts[:, c, 0:8], cur[:, c, :])
                then(ins)
                for c in range(2):
                    V.max_index(ti[:, c, 0:8], ts[:, c, 0:8], cur[:, c, :])
                    ins = V.match_replace(cur2[:, c, :], ts[:, c, 0:8], cur[:, c, :], -3e38)
                then(ins)
                for c in range(2):
                    ins = V.max(ts[:, c, 8:16], cur2[:, c, :])
                then(ins)
                for c in range(2):
                    V.max_index(ti[:, c, 8:16], ts[:, c, 8:16], cur2[:, c, :])
                then(TT(cand[:], ts[:, 0, :].unsqueeze(2).to_broadcast([P, TOPK, TOPK]),
                        ts[:, 1, :].unsqueeze(1).to_broadcast([P, TOPK, TOPK]), ALU.add))
                V.tensor_copy(tif[:], ti[:])
                flat, flat2 = (a[:].rearrange("p a b -> p (a b)") for a in (cand, cand2))
                then(V.max(bs[:, par, 0:8], flat))
                V.max_index(bj[:, 0, 0:8], bs[:, par, 0:8], flat)
                then(V.match_replace(flat2, bs[:, par, 0:8], flat, -3e38))
                then(V.max(bs[:, par, 8:16], flat2))
                then(V.max_index(bj[:, 0, 8:16], bs[:, par, 8:16], flat2))
                V.tensor_scalar(bji[:, 0, :], bj[:, 0, :], 4, None, ALU.logical_shift_right)
                then(V.tensor_scalar(bji[:, 1, :], bj[:, 0, :], 15, None, ALU.bitwise_and))
                then(V.tensor_copy(bjf[:], bji[:]))
                for c in range(2):
                    ins = TT(eq[:, c, :, :], bjf[:, c, :].unsqueeze(2).to_broadcast([P, TOPK, TOPK]),
                             cst("iota16").unsqueeze(1).to_broadcast([P, TOPK, TOPK]), ALU.is_equal)
                then(ins)
                for c in range(2):
                    ins = TT(eq[:, c, :, :], eq[:, c, :, :], tif[:, c, :].unsqueeze(1).to_broadcast([P, TOPK, TOPK]), ALU.mult)
                then(ins)
                then(V.tensor_reduce(ef[:], eq[:], X, ALU.add))
                V.tensor_scalar(gs[:, par:par + 1], bs[:, par, 0:1], -1.0, None, ALU.mult)
                STT(idxu[:, par, :], ef[:, 0, :], float(NK), ef[:, 1, :], ALU.mult, ALU.add)\
                    .then_inc(S.sem("topk_done"), 1)

            def body(it, par, x, last=False):
                local = [0]

                def then(ins):
                    local[0] += 1
                    ins.then_inc(S.sem("dve_loop"), 1)
                    dve.reg_mov(linked, it * LINKS + local[0])
                    dve.wait_ge(S.sem("keys_in"), 16)
                    dve.wait_ge(S.sem("dve_loop"), linked)

                if last:
                    then = link
                for k in range(TOPK):
                    dve.wait_ge(S.sem(f"u{k % NR}_in"), (it * (TOPK // NR) + k // NR + 1) * 16)
                    V.tensor_tensor_reduce(out=UR[:, k % NR, :], in0=UR[:, k % NR, :], in1=x, scale=1.0, scalar=0.0,
                                           op0=ALU.mult, op1=ALU.add, accum_out=M["act"][:, par, k:k + 1])\
                        .then_inc(S.sem("u_free"), 1)
                dve.wait_ge(S.sem("v_free"), it * TOPK + 1)
                V.tensor_copy(idxv[:, par, :], idxu[:, par, :])
                dve.wait_ge(S.sem("act_gl"), it + 1)
                V.reciprocal(gs[:, 12 + par:13 + par], gs[:, 2 + par:3 + par])
                then(TT(M["wv"][:, par, :], M["ge"][:, par, :], M["gl"][:, par, :], ALU.mult))
                V.tensor_scalar(M["wv"][:, par, :], M["wv"][:, par, :], gs[:, 12 + par:13 + par], None, ALU.mult)\
                    .then_inc(S.sem("dve_w"), 1)
                if not last:
                    topk(it + 2, par, then)
                    assert local[0] == LINKS, local[0]

            def finish(t):
                m = TILES[t][1]
                dve.wait_ge(*at("act_fin", ("rms", t)))
                src = PS[:, 2 + 2 * t:4 + 2 * t, :] if t < 2 else PS[0:TS, 0:2, :]
                link(V.reciprocal(gs[0:m, 14:15], gs[0:m, 8 + t:9 + t]))
                ins = STT(X1[0:m, t, :].rearrange("p (a b) -> p a b", a=2), src, gs[0:m, 14:15],
                          gr[0:m, 2, :].rearrange("p (a b) -> p a b", a=2), ALU.mult, ALU.mult)
                ins.then_inc(*inc("dve_fin", ("y", t)))
                dve.wait_ge(*now("dve_fin"))

            dve.wait_ge(*now("dve_seq"))
            for n in range(2):
                topk(n, n, link)
            for t, it0, n in peer_tiles():
                if t < 2:
                    with dve.Fori(0, n // 2) as i:
                        for j in range(2):
                            body(i * 2 + (it0 + j), j, XN[:, t, :])
                else:
                    dve.wait_ge(S.sem("xs_in"), 16 * 4)
                    for j in range(n):
                        body(it0 + j, j, gr[:, 0, :], last=True)
                        finish(j)
            dve.wait_ge(S.sem("v_free"), NR + NIT * TOPK)
            V.tensor_copy(VR[:, 0, :].rearrange("p (a b) -> p a b", a=2), PS[:, 6:8, :]).then_inc(*inc("dve_fin", "copy"))
            finish(2)

        STAGES = {
            "lin": linear_add, "rw_pre": rw_pre, "rw_kk": rw_kk, "rw_vec": rw_vec, "rw_tile": rw_tile,
            "rw_scan": rw_scan, "rw_sample": rw_sample, "rw_out": rw_out, "lf": log_forget, "attn": attn,
            "sgu": sgu, "sattn": sattn, "gnorm": gnorm, "norm": norm, "cross": cross, "scross_k": scross_k,
            "scross_v": scross_v, "peer": peer}
        follow(STAGES)

    @block.gpsimd
    def _(pool):
        G = nc.gpsimd
        pool.wait_ge(*at("dve_sa", "idx"))
        for i in range(B * 2):
            G.indirect_dma_start(M["lfg"][:, i, :], None, io["lf_pool"],
                                 bass.IndirectOffsetOnAxis(ap=M["idx"][:, i:i + 1], axis=0)).then_inc(S.sem("glf_in"), 16)
        pool.wait_ge(*at("dve_xn", ("xm", 1)))
        pool.wait_ge(*at("act_lin", ("unit", 1)))
        G.memset(MT[:], 0.0)
        G.memset(ST[:, 0, :, :], 0.0).then_inc(*inc("pool_rw", "zero"))
        for c in range(2):
            pool.wait_ge(*at("act_rw", ("u0n", 2)))
            if c:
                pool.wait_ge(*at("pe_rw", ("smn", c - 1)))
            for dst, src in ((XB, TOK[0:TS, 1, c * P:(c + 1) * P]), (XV, TOK[0:TS, 3, c * P:(c + 1) * P]),
                             (XU, U0[0:TS, c * P:(c + 1) * P])):
                ins = G.tensor_tensor(dst, src.unsqueeze(1).to_broadcast([TS, B, P]),
                                      cst("batch", TS).unsqueeze(2).to_broadcast([TS, B, P]), ALU.mult)
            ins.then_inc(*inc("pool_rw", ("x", c)))

        pool.wait_ge(*at("dve_y", "a"))
        for name, dst, pool_rows in (("gath_in", KTB[:], "k_pool"), ("gv_in", VB[:], "v_pool")):
            for i in range(B * 2):
                b, pg = divmod(i, 2)
                d = dst[:, b, pg, :, :].rearrange("p a b -> p (a b)") if name == "gath_in" else dst[:, b, pg, :]
                G.indirect_dma_start(d, None, io[pool_rows], bass.IndirectOffsetOnAxis(ap=M["idx"][:, i:i + 1], axis=0))\
                    .then_inc(S.sem(name), 16)
        G.memset(QB[:], 0.0).then_inc(*inc("pool_sa", "z"))
        pool.wait_ge(*now("pool_sa"))
        for name in ("gath_in", "gv_in"):
            pool.wait_ge(S.sem(name), 16 * 16)
        for g, qc in enumerate((BQ, DQ)):
            for h in range(4):
                ph = slice(HD * (h % 2), HD * (h % 2) + HD)
                for par in range(2):
                    a = par * 16 + h * Q
                    ins = G.tensor_copy(QB[ph, g, par::2, h // 2, a:a + Q],
                                        hT[ph, qc + h // 2, T:N].rearrange("p (b q) -> p b q", q=Q)[:, par::2, :])
        ins.then_inc(*inc("pool_sa", "q"))

        pool.wait_ge(*at("dve_gn", 3))
        G.memset(QX[:], 0.0).then_inc(*inc("pool_cx", "z"))
        pool.wait_ge(*now("pool_cx"))
        for c in range(KC):
            pool.wait_ge(*at("act_lin", ("unit", LAST[23] + c + 1)))
            for par in range(2):
                a = par * 16 + c // 2 * Q
                ins = G.tensor_copy(QX[:, par::2, c, a:a + Q], hX[:, c, T:N].rearrange("p (b q) -> p b q", q=Q)[:, par::2, :])
        ins.then_inc(*inc("pool_cx", "q"))

        pool.wait_ge(*at("dve_cx", "ys"))
        free_slots = pool.alloc_register("free_slots")

        def gather(name, it, k, par):
            ring, idx = (UR, M["idxu"]) if name == "u" else (VR, M["idxv"])
            pool.reg_mov(free_slots, it * TOPK + (k + 1))
            pool.wait_ge(S.sem("keys_in"), 16)
            pool.wait_ge(S.sem(f"{name}_free"), free_slots)
            G.indirect_dma_start(ring[:, k % NR, :], None, io[f"peer_{name}"],
                                 bass.IndirectOffsetOnAxis(ap=idx[:, par, k:k + 1], axis=0))\
                .then_inc(S.sem(f"{name}{k % NR}_in"), 16)

        def gathers(it, par, left=2):
            for k in range(TOPK):
                if k + AHEAD == TOPK and left == 2:
                    pool.wait_ge(S.sem("topk_done"), it + 3)
                if k + AHEAD < TOPK and left >= 1:
                    gather("u", it + 1, k + AHEAD, 1 - par)
                elif k + AHEAD >= TOPK and left == 2:
                    gather("u", it + 2, k + AHEAD - TOPK, par)
                if k == 0:
                    pool.wait_ge(S.sem("dve_w"), it + 1)
                gather("v", it, k, par)

        for n in range(TOPK + AHEAD):
            if n % TOPK == 0:
                pool.wait_ge(S.sem("topk_done"), n // TOPK + 1)
            gather("u", n // TOPK, n % TOPK, n // TOPK)
        with pool.Fori(0, (NIT - 2) // 2) as i:
            for j in range(2):
                gathers(i * 2 + j, j)
        for j in range(2):
            gathers(NIT - 2 + j, j, left=1 - j)


def feature_columns(a):
    return np.ascontiguousarray(np.asarray(a, np.float32).reshape(-1, P).T)


def kernel(**inputs):
    import concourse.bacc as bacc
    from concourse.bass_utils import run_bass_kernel_spmd

    f = {k: np.asarray(v) for k, v in inputs.items()}
    ins, outs = {}, {}
    ins["x_all"] = np.concatenate([f["x_prompt"].reshape(T, D), f["x_sample"].reshape(TS, D)])
    ins["mem_prompt"] = f["mem_prompt"].reshape(MEM, D)
    ins["const"] = CONST
    params = {"g0": f["norm_g"][0, 0], "g1": f["norm_g"][0, 1], "g2": f["norm_g"][0, 2], "gm": f["ca_mem_g"],
              "gout": f["out_g"], "mu": f["a_mu"], "w0": f["a_w0"], "a0": f["a_a0"], "kks": f["a_kk"],
              "ka": f["a_ka"], "rk": f["a_rk"], "lnw": f["a_lnw"], "lnb": f["a_lnb"]}
    ins["cols"] = np.hstack([feature_columns(params[k]) for k in COLS])
    for k in ("w_in", "ca_wk", "ca_wv", "w_out", "ca_wq", "ca_wo", "peer_wq"):
        ins[k] = f[k][0]
    ins["a_w2"], ins["a_a2"], ins["a_g2"] = f["a_w2"][0], f["a_a2"][0], f["a_g2"][0]
    ins["shift"] = f["state_a_shift"][0].reshape(B, KC, P).transpose(2, 1, 0)
    ins["s0T"] = f["state_a_wkv"][0].reshape(B, 2, 2, HD, HD).transpose(2, 4, 0, 1, 3).reshape(P, B, 2, HD)
    ins["c_lng"], ins["c_lnb"], ins["b_f"] = f["c_lng"], f["c_lnb"], f["b_f"]
    ws = f["c_ws"][0].transpose(2, 0, 1)
    ins["wsT"] = ws
    ins["ws4"] = np.tile(ws[:Q, :, :Q], (B, 1, B))
    ins["bsr"] = np.repeat(f["c_bs"][0].reshape(2, 2, P).transpose(1, 0, 2), HD, axis=0)
    ins["page_table"] = f["page_table"].reshape(1, -1)
    n_phys = f["cache_b_k"].shape[1]
    ins["k_pool"] = f["cache_b_k"][0].reshape(n_phys, P, 2, P).transpose(0, 3, 2, 1).reshape(n_phys * P, 2 * P)
    ins["v_pool"] = f["cache_b_v"][0].reshape(n_phys * P, GW)
    ins["lf_pool"] = f["cache_b_logf"][0].reshape(n_phys * P, 4)
    ins["dkT"] = f["cache_d_k"][0].reshape(B, PAST, 2, P).transpose(3, 0, 2, 1)
    ins["dv"] = f["cache_d_v"][0].reshape(B, 2, P, GW).transpose(2, 0, 1, 3)
    ins["gains"] = np.stack([f["norm_g"][0, 1], f["norm_g"][0, 2], f["final_g"]])
    ins["mk_s"] = f["cache_mem_k"][0].reshape(B, MEM, KC, P).transpose(0, 3, 2, 1).reshape(B, P, KC * MEM)
    ins["mv_s"] = f["cache_mem_v"][0].reshape(B, 2, P, D).transpose(0, 2, 1, 3).reshape(B, P, 2 * D)
    ins["keysT"] = f["peer_keys"][0].transpose(3, 0, 1, 2).reshape(P, 16, NK)
    ins["peer_u"], ins["peer_v"] = f["peer_u"][0], f["peer_v"][0]
    outs["o_y"] = (N, D)
    outs["o_lf"] = (P, 3, 4)
    outs["o_cv"] = (TS, GW)
    outs["o_shift"] = (P, KC, 1 + B)
    outs["o_pwkv"] = (P, 2, HD)
    outs["o_swkv"] = (P, B, 2, HD)
    outs["o_bk"] = (P, 2, N)
    outs["o_dk"] = (P, 2, N)
    outs["o_tok0"] = (P, TW)
    outs["o_tok1"] = (P, TW)
    outs["o_tok2"] = (TS, TW)
    outs["o_memk"] = (D, MEM)
    outs["o_memv"] = (MEM, D)

    def declare(nc):
        io = {}
        for k, a in ins.items():
            io[k] = nc.dram_tensor(k, a.shape, mybir.dt.from_np(a.dtype), kind="ExternalInput").ap()
        for k, s in outs.items():
            io[k] = nc.dram_tensor(k, s, F32, kind="ExternalOutput").ap()
        return io

    steps = None
    for _ in range(2):
        nc = bacc.Bacc("TRN2", target_bir_lowering=False, num_devices=1)
        steps = build(nc, declare(nc), steps)
    arrays = {k: np.ascontiguousarray(a) for k, a in ins.items()}
    r = run_bass_kernel_spmd(nc, [arrays], core_ids=[0]).results[0]
    fm = {k: r[k].transpose(2, 1, 0).reshape(N, 4, HD) for k in ("o_bk", "o_dk")}
    tok = np.concatenate([r[f"o_tok{t}"] for t in range(3)])
    bv, dv = tok[:, TBV:TBV + GW].reshape(N, 4, HD), tok[:, TDV:TDV + GW].reshape(N, 4, HD)
    lf = r["o_lf"].transpose(1, 0, 2).reshape(3 * P, 4)
    shift = r["o_shift"].transpose(2, 1, 0).reshape(1 + B, D)
    pwkv = r["o_pwkv"].reshape(2, HD, 2, HD).transpose(2, 0, 3, 1).reshape(1, 1, 4, HD, HD)
    swkv = r["o_swkv"].reshape(2, HD, B, 2, HD).transpose(2, 3, 0, 4, 1).reshape(1, B, 4, HD, HD)
    p = lambda a: a[:T].reshape(1, 1, T, *a.shape[1:])
    s = lambda a: a[T:N].reshape(1, B, Q, *a.shape[1:])
    out = (r["o_y"][:T].reshape(1, T, D), r["o_y"][T:].reshape(B, Q, D),
           pwkv, shift[:1].reshape(1, 1, D), p(fm["o_bk"]), p(bv), p(lf), p(fm["o_dk"]), p(dv),
           r["o_memk"].T.reshape(1, 1, MEM, 4, 256), r["o_memv"].reshape(1, 1, MEM, 4, 256),
           swkv, shift[1:].reshape(1, B, D), s(fm["o_bk"]), s(bv), s(lf), r["o_cv"].reshape(1, B, Q, GW),
           s(fm["o_dk"]), s(dv))
    return tuple(np.ascontiguousarray(a) for a in out)
```
